# Optimizing a Trainium2 kernel written in Bass

```python
import jax, jax.numpy as jnp
from jax import lax
import numpy as np

D_MODEL = 1024
BATCH = 1
SEQ = 1024
DEPTH = 2

GRID_W = 64
EPS = 1e-6

A_HEADS = 8
A_HEAD_DIM = D_MODEL // 16
A_WIDTH = A_HEADS * A_HEAD_DIM
CONV_WIDTH = 3
B_GROUPS = 4
B_GROUP_DIM = D_MODEL // 8
B_WIDTH = B_GROUPS * B_GROUP_DIM
EVEN_IN = 4 * A_WIDTH + 2 * B_WIDTH
EVEN_MIX = A_WIDTH + B_WIDTH

HEAD_DIM = 128
N_HEADS = D_MODEL // HEAD_DIM
N_KV_HEADS = N_HEADS // 4
Q_WIDTH = N_HEADS * HEAD_DIM
KV_WIDTH = N_KV_HEADS * HEAD_DIM
ODD_IN = 2 * Q_WIDTH + 2 * KV_WIDTH
ROPE_THETA = 10000.0
Q_BLOCK = 128

N_EVEN = (DEPTH + 1) // 2
N_ODD = DEPTH // 2


def rms_norm(x, g):
    xf = x.astype(jnp.float32)
    y = xf * lax.rsqrt(jnp.mean(xf * xf, axis=-1, keepdims=True) + EPS)
    return (y * g.astype(jnp.float32)).astype(x.dtype)

def centred_depthwise_conv(u, w):
    s = u.shape[1]
    pad = CONV_WIDTH // 2
    up = jnp.pad(u, ((0, 0), (pad, CONV_WIDTH - 1 - pad), (0, 0)))
    out = up[:, 0:s] * w[0]
    for tap in range(1, CONV_WIDTH):
        out = out + up[:, tap:tap + s] * w[tap]
    return out

def short_conv_fourier_mixer(h, w_in, conv_w, w_out):
    bsz, s, _ = h.shape
    proj = h @ w_in
    a_x, a_b, a_c, a_z, b_u, b_z = jnp.split(
        proj,
        [A_WIDTH, 2 * A_WIDTH, 3 * A_WIDTH, 4 * A_WIDTH, 4 * A_WIDTH + B_WIDTH],
        axis=-1)
    y_a = a_b * centred_depthwise_conv(a_c * a_x, conv_w) * jax.nn.silu(a_z)
    u = b_u.reshape(bsz, s, B_GROUPS, B_GROUP_DIM).astype(jnp.float32)
    f = jnp.fft.fft2(u, axes=(1, 3), norm="ortho").real
    y_b = f.reshape(bsz, s, B_WIDTH).astype(h.dtype) * jax.nn.silu(b_z)
    return jnp.concatenate([y_a, y_b], axis=-1) @ w_out

def axial_rope_tables(s):
    rows = s // GRID_W
    row = jnp.repeat(jnp.arange(rows), GRID_W).astype(jnp.float32)
    col = jnp.tile(jnp.arange(GRID_W), rows).astype(jnp.float32)
    n_pair = HEAD_DIM // 4
    inv = ROPE_THETA ** (-jnp.arange(n_pair, dtype=jnp.float32) / n_pair)
    ang = jnp.concatenate([row[:, None] * inv, col[:, None] * inv], axis=-1)
    return jnp.cos(ang), jnp.sin(ang)

def apply_rope(x, cos, sin):
    xf = x.astype(jnp.float32).reshape(x.shape[:-1] + (HEAD_DIM // 2, 2))
    x1, x2 = xf[..., 0], xf[..., 1]
    c = cos[None, :, None, :]
    sn = sin[None, :, None, :]
    out = jnp.stack([x1 * c - x2 * sn, x1 * sn + x2 * c], axis=-1)
    return out.reshape(x.shape).astype(x.dtype)

def gqa_axial_mixer(h, w_in, q_gain, k_gain, w_out):
    bsz, s, _ = h.shape
    proj = h @ w_in
    q, k, v, z = jnp.split(
        proj, [Q_WIDTH, Q_WIDTH + KV_WIDTH, Q_WIDTH + 2 * KV_WIDTH], axis=-1)
    q = q.reshape(bsz, s, N_HEADS, HEAD_DIM)
    k = k.reshape(bsz, s, N_KV_HEADS, HEAD_DIM)
    v = v.reshape(bsz, s, N_KV_HEADS, HEAD_DIM)
    cos, sin = axial_rope_tables(s)
    q = apply_rope(rms_norm(q, q_gain), cos, sin)
    k = apply_rope(rms_norm(k, k_gain), cos, sin)
    groups = N_HEADS // N_KV_HEADS
    n_blk = s // Q_BLOCK
    qb = q.reshape(bsz, n_blk, Q_BLOCK, N_KV_HEADS, groups, HEAD_DIM).transpose(1, 0, 3, 4, 2, 5)
    kt = k.transpose(0, 2, 1, 3)
    vt = v.transpose(0, 2, 1, 3)
    scale = HEAD_DIM ** -0.5

    def attend_block(q_blk):
        sc = jnp.einsum('bkgqd,bksd->bkgqs', q_blk, kt,
                        preferred_element_type=jnp.float32) * scale
        p = jax.nn.softmax(sc, axis=-1)
        return jnp.einsum('bkgqs,bksd->bkgqd', p.astype(vt.dtype), vt)

    o = lax.map(attend_block, qb)
    o = o.transpose(1, 0, 4, 2, 3, 5).reshape(bsz, s, Q_WIDTH)
    return (o * jax.nn.silu(z)) @ w_out

def first_inputs(seed: int = 0) -> dict:
    key = jax.random.key(seed)
    ks = jax.random.split(key, 12)
    f32 = jnp.float32
    x = jax.random.normal(ks[0], (BATCH, SEQ, D_MODEL), f32)
    norm_even = 1.0 + 0.02 * jax.random.normal(ks[1], (N_EVEN, D_MODEL), f32)
    w_in_even = jax.random.normal(ks[2], (N_EVEN, D_MODEL, EVEN_IN), f32) * D_MODEL ** -0.5
    conv_w = jax.random.normal(ks[3], (N_EVEN, CONV_WIDTH, A_WIDTH), f32) * CONV_WIDTH ** -0.5
    w_out_even = jax.random.normal(ks[4], (N_EVEN, EVEN_MIX, D_MODEL), f32) * EVEN_MIX ** -0.5
    norm_odd = 1.0 + 0.02 * jax.random.normal(ks[5], (N_ODD, D_MODEL), f32)
    w_in_odd = jax.random.normal(ks[6], (N_ODD, D_MODEL, ODD_IN), f32) * D_MODEL ** -0.5
    q_gain = 1.0 + 0.02 * jax.random.normal(ks[7], (N_ODD, HEAD_DIM), f32)
    k_gain = 1.0 + 0.02 * jax.random.normal(ks[8], (N_ODD, HEAD_DIM), f32)
    w_out_odd = jax.random.normal(ks[9], (N_ODD, Q_WIDTH, D_MODEL), f32) * Q_WIDTH ** -0.5
    final_norm = 1.0 + 0.02 * jax.random.normal(ks[10], (D_MODEL,), f32)
    return {"x": x, "norm_even": norm_even, "w_in_even": w_in_even, "conv_w": conv_w,
            "w_out_even": w_out_even, "norm_odd": norm_odd, "w_in_odd": w_in_odd,
            "q_gain": q_gain, "k_gain": k_gain, "w_out_odd": w_out_odd,
            "final_norm": final_norm}

def first_block(x, norm_even, w_in_even, conv_w, w_out_even, norm_odd, w_in_odd,
              q_gain, k_gain, w_out_odd, final_norm):
    for layer in range(DEPTH):
        i = layer // 2
        if layer % 2 == 0:
            x = x + short_conv_fourier_mixer(rms_norm(x, norm_even[i]), w_in_even[i],
                                             conv_w[i], w_out_even[i])
        else:
            x = x + gqa_axial_mixer(rms_norm(x, norm_odd[i]), w_in_odd[i],
                                    q_gain[i], k_gain[i], w_out_odd[i])
    return rms_norm(x, final_norm)


DEPTH_2 = 1

D_MIX = 2 * D_MODEL
D_POOL = D_MIX // 2
D_MLSTM = D_MIX - D_POOL
POOL_WINDOWS = (2, 4, 8, 16)
N_POOL_GROUPS = len(POOL_WINDOWS)
POOL_GROUP_DIM = D_POOL // N_POOL_GROUPS
N_HEADS_2 = 4
HEAD_DIM_2 = D_MLSTM // N_HEADS_2
QKV_BLOCK = 4
N_QKV_BLOCKS = D_MLSTM // QKV_BLOCK
CONV_WIDTH_2 = 5
CHUNK = 128
N_DIRS = 2
NEG_INF = -1e30


def rms_norm_2(x, g):
    xf = x.astype(jnp.float32)
    y = xf * lax.rsqrt(jnp.mean(xf * xf, axis=-1, keepdims=True) + EPS)
    return (y * g.astype(jnp.float32)).astype(x.dtype)

def window_mean_minus_self(u, w):
    S = u.shape[1]
    left = (w - 1) // 2
    right = w - 1 - left
    uf = u.astype(jnp.float32)
    cs = jnp.concatenate([jnp.zeros_like(uf[:, :1]), jnp.cumsum(uf, axis=1)], axis=1)
    t = np.arange(S)
    lo = np.maximum(t - left, 0)
    hi = np.minimum(t + right, S - 1)
    total = cs[:, hi + 1] - cs[:, lo]
    count = (hi - lo + 1).astype(np.float32)[None, :, None]
    return (total / count - uf).astype(u.dtype)

def pool_mixer(u, pool_w, pool_scale):
    B, S, _ = u.shape
    ug = u.reshape(B, S, N_POOL_GROUPS, POOL_GROUP_DIM)
    pooled = jnp.stack([window_mean_minus_self(ug[:, :, g], w) for g, w in enumerate(POOL_WINDOWS)], axis=2)
    mixed = jnp.einsum('bsgc,gcd->bsgd', pooled, pool_w).reshape(B, S, D_POOL)
    return mixed * pool_scale

def centred_depthwise_conv_2(u, w, b):
    K, C = w.shape
    pad = K // 2
    y = lax.conv_general_dilated(u, w[:, None, :].astype(u.dtype), window_strides=(1,),
                                 padding=[(pad, pad)], dimension_numbers=('NWC', 'WIO', 'NWC'),
                                 feature_group_count=C)
    return y + b

def headwise(u, w):
    B, S, _ = u.shape
    return jnp.einsum('bsni,nio->bsno', u.reshape(B, S, w.shape[0], w.shape[1]), w).reshape(B, S, -1)

def mlstm_chunkwise(q, k, v, log_i, log_f):
    B, H, S, d = q.shape
    nc = S // CHUNK

    def to_chunks(a):
        return jnp.moveaxis(a.reshape(B, H, nc, CHUNK, *a.shape[3:]), 2, 0)

    qc, kc, vc, ic, fc = map(to_chunks, (q, k, v, log_i, log_f))
    lower_tri = jnp.tril(jnp.ones((CHUNK, CHUNK), dtype=bool))

    def step(carry, xs):
        C, n, m = carry
        qj, kj, vj, ij, fj = xs
        b = jnp.cumsum(fj, axis=-1)
        log_inter = b + m[..., None]
        log_D = b[..., :, None] - b[..., None, :] + ij[..., None, :]
        log_D = jnp.where(lower_tri, log_D, NEG_INF)
        m_t = jnp.maximum(log_inter, jnp.max(log_D, axis=-1))
        inter_w = jnp.exp(log_inter - m_t)
        s = jnp.einsum('bhtd,bhsd->bhts', qj, kj) * jnp.exp(log_D - m_t[..., None])
        num = jnp.einsum('bhts,bhse->bhte', s, vj) + inter_w[..., None] * jnp.einsum('bhtd,bhde->bhte', qj, C)
        den = jnp.sum(s, axis=-1) + inter_w * jnp.einsum('bhtd,bhd->bht', qj, n)
        h = num / jnp.maximum(jnp.abs(den), jnp.exp(-m_t))[..., None]
        bL = b[..., -1]
        log_s = bL[..., None] - b + ij
        m_new = jnp.maximum(bL + m, jnp.max(log_s, axis=-1))
        decay = jnp.exp(bL + m - m_new)
        ws = jnp.exp(log_s - m_new[..., None])
        C_new = decay[..., None, None] * C + jnp.einsum('bhs,bhsd,bhse->bhde', ws, kj, vj)
        n_new = decay[..., None] * n + jnp.einsum('bhs,bhsd->bhd', ws, kj)
        return (C_new, n_new, m_new), h

    init = (jnp.zeros((B, H, d, d), jnp.float32), jnp.zeros((B, H, d), jnp.float32),
            jnp.zeros((B, H), jnp.float32))
    _, hs = lax.scan(step, init, (qc, kc, vc, ic, fc))
    return jnp.moveaxis(hs, 0, 2).reshape(B, H, S, d)

def mlstm_branch(u, conv_w, conv_b, w_q, w_k, w_v, w_gates, b_gates, mh_norm_w, skip_w):
    B, S, _ = u.shape
    c = jax.nn.silu(centred_depthwise_conv_2(u, conv_w, conv_b))
    q = headwise(c, w_q)
    k = headwise(c, w_k)
    v = headwise(u, w_v)
    qkv = jnp.concatenate([q, k, v], axis=-1).astype(jnp.float32)
    gates = jnp.einsum('bsc,ncg->nbsg', qkv, w_gates.astype(jnp.float32)) \
        + b_gates.astype(jnp.float32)[:, None, None, :]
    gates = jnp.transpose(gates, (0, 1, 3, 2))
    log_i = gates[:, :, :N_HEADS_2]
    log_f = jax.nn.log_sigmoid(gates[:, :, N_HEADS_2:])

    def heads(a):
        return a.reshape(B, S, N_HEADS_2, HEAD_DIM_2).transpose(0, 2, 1, 3).astype(jnp.float32)

    qh, kh, vh = heads(q), heads(k) * (HEAD_DIM_2 ** -0.5), heads(v)
    h_fwd = mlstm_chunkwise(qh, kh, vh, log_i[0], log_f[0])
    h_bwd = jnp.flip(mlstm_chunkwise(jnp.flip(qh, 2), jnp.flip(kh, 2), jnp.flip(vh, 2),
                                     jnp.flip(log_i[1], -1), jnp.flip(log_f[1], -1)), 2)
    h = h_fwd + h_bwd
    mu = jnp.mean(h, axis=-1, keepdims=True)
    var = jnp.mean(jnp.square(h - mu), axis=-1, keepdims=True)
    h = (h - mu) * lax.rsqrt(var + EPS)
    h = h.transpose(0, 2, 1, 3).reshape(B, S, D_MLSTM)
    out = h * mh_norm_w.astype(jnp.float32) + skip_w.astype(jnp.float32) * c.astype(jnp.float32)
    return out.astype(u.dtype)

def second_inputs(seed: int = 0) -> dict:
    key = jax.random.key(seed)
    ks = jax.random.split(key, 20)
    nrm = jax.random.normal
    f32 = jnp.float32
    x = nrm(ks[0], (BATCH, SEQ, D_MODEL), f32)
    norm_in_g = 1.0 + 0.1 * nrm(ks[1], (DEPTH_2, D_MODEL), f32)
    w_in = nrm(ks[2], (DEPTH_2, D_MODEL, 2 * D_MIX), f32) * D_MODEL ** -0.5
    pool_w = nrm(ks[3], (DEPTH_2, N_POOL_GROUPS, POOL_GROUP_DIM, POOL_GROUP_DIM), f32) * POOL_GROUP_DIM ** -0.5
    pool_scale = 1.0 + 0.1 * nrm(ks[4], (DEPTH_2, D_POOL), f32)
    conv_w = nrm(ks[5], (DEPTH_2, CONV_WIDTH_2, D_MLSTM), f32) * CONV_WIDTH_2 ** -0.5
    conv_b = 0.01 * nrm(ks[6], (DEPTH_2, D_MLSTM), f32)
    w_q = nrm(ks[7], (DEPTH_2, N_QKV_BLOCKS, QKV_BLOCK, QKV_BLOCK), f32) * QKV_BLOCK ** -0.5
    w_k = nrm(ks[8], (DEPTH_2, N_QKV_BLOCKS, QKV_BLOCK, QKV_BLOCK), f32) * QKV_BLOCK ** -0.5
    w_v = nrm(ks[9], (DEPTH_2, N_QKV_BLOCKS, QKV_BLOCK, QKV_BLOCK), f32) * QKV_BLOCK ** -0.5
    w_gates = nrm(ks[10], (DEPTH_2, N_DIRS, 3 * D_MLSTM, 2 * N_HEADS_2), f32) * (3 * D_MLSTM) ** -0.5
    b_i = 0.1 * nrm(ks[11], (DEPTH_2, N_DIRS, N_HEADS_2), f32)
    b_f = jnp.linspace(3.0, 6.0, N_HEADS_2, dtype=f32) + 0.1 * nrm(ks[12], (DEPTH_2, N_DIRS, N_HEADS_2), f32)
    b_gates = jnp.concatenate([b_i, b_f], axis=-1)
    mh_norm_w = 1.0 + 0.1 * nrm(ks[13], (DEPTH_2, D_MLSTM), f32)
    skip_w = 1.0 + 0.1 * nrm(ks[14], (DEPTH_2, D_MLSTM), f32)
    w_out = nrm(ks[15], (DEPTH_2, D_MIX, D_MODEL), f32) * D_MIX ** -0.5
    norm_out_g = 1.0 + 0.1 * nrm(ks[16], (D_MODEL,), f32)
    return {"x": x, "norm_in_g": norm_in_g, "w_in": w_in, "pool_w": pool_w, "pool_scale": pool_scale,
            "conv_w": conv_w, "conv_b": conv_b, "w_q": w_q, "w_k": w_k, "w_v": w_v,
            "w_gates": w_gates, "b_gates": b_gates, "mh_norm_w": mh_norm_w, "skip_w": skip_w,
            "w_out": w_out, "norm_out_g": norm_out_g}

def second_block(x, norm_in_g, w_in, pool_w, pool_scale, conv_w, conv_b, w_q, w_k, w_v,
              w_gates, b_gates, mh_norm_w, skip_w, w_out, norm_out_g):
    h = x
    for l in range(DEPTH_2):
        u = rms_norm_2(h, norm_in_g[l])
        proj = jnp.einsum('bsd,de->bse', u, w_in[l])
        pool_x, pool_z, m_x, m_z = jnp.split(proj, [D_POOL, 2 * D_POOL, 2 * D_POOL + D_MLSTM], axis=-1)
        y_pool = pool_mixer(pool_x, pool_w[l], pool_scale[l]) * jax.nn.silu(pool_z)
        y_m = mlstm_branch(m_x, conv_w[l], conv_b[l], w_q[l], w_k[l], w_v[l], w_gates[l],
                           b_gates[l], mh_norm_w[l], skip_w[l]) * jax.nn.silu(m_z)
        y = jnp.concatenate([y_pool.astype(h.dtype), y_m.astype(h.dtype)], axis=-1)
        h = h + jnp.einsum('bse,ed->bsd', y, w_out[l])
    return rms_norm_2(h, norm_out_g)


def setup_inputs(seed=0):
    out = dict(first_inputs(seed))
    for name, value in second_inputs(seed + 1).items():
        if name != "x":
            out[name + "_2"] = value
    return out


def reference(
    x, norm_even, w_in_even, conv_w, w_out_even, norm_odd, w_in_odd, q_gain, k_gain, w_out_odd,
    final_norm, norm_in_g_2, w_in_2, pool_w_2, pool_scale_2, conv_w_2, conv_b_2, w_q_2, w_k_2,
    w_v_2, w_gates_2, b_gates_2, mh_norm_w_2, skip_w_2, w_out_2, norm_out_g_2,
):
    x = first_block(
        x, norm_even, w_in_even, conv_w, w_out_even, norm_odd, w_in_odd, q_gain, k_gain,
        w_out_odd, final_norm,
    )
    return second_block(
        x, norm_in_g_2, w_in_2, pool_w_2, pool_scale_2, conv_w_2, conv_b_2, w_q_2, w_k_2, w_v_2,
        w_gates_2, b_gates_2, mh_norm_w_2, skip_w_2, w_out_2, norm_out_g_2,
    )


_drawn_inputs = setup_inputs


def setup_inputs(seed=0):
    import zlib

    import numpy as np

    out = dict(_drawn_inputs(seed))
    spreads = {}
    factors = {'norm_odd': 8.0, 'q_gain': 8.0, 'k_gain': 8.0, 'conv_b_2': 4.996}
    for name, (base, spread) in spreads.items():
        noise = np.random.default_rng([zlib.crc32(name.encode()), seed]).standard_normal(out[name].shape)
        drawn = base * np.exp(spread * noise) if base else spread * noise
        out[name] = __import__('jax').numpy.asarray(drawn.astype(out[name].dtype))
    for name, factor in factors.items():
        out[name] = (out[name] * factor).astype(out[name].dtype)
    return out
```

```python
from contextlib import ExitStack

import numpy as np
import concourse.bass as bass
from concourse import mybir

P = 128
S = 1024
D = 1024
KT = D // P
HALF = 512
EPS = 1e-6
F32 = mybir.dt.float32
F32R = mybir.dt.float32r
ALU = mybir.AluOpType
ACT = mybir.ActivationFunctionType
AX = mybir.AxisListType

AB = 4
RADIX = 8
HEADS, KV_HEADS = 8, 2
GROUP = HEADS // KV_HEADS
QT = S // P
SCORE_SCALE = float(P) ** -0.5
WINDOWS = (2, 4, 8, 16)
PAD = 8
MH = 4
MD = 256
VE = MD + 1
CH = S // P
NDIR = 2
TAPS2 = 5
NEG = -1e30

EVEN_IN, EVEN_OUT, ODD_IN, ODD_OUT, SEC_IN, SEC_OUT = 24, 8, 20, 8, 32, 16
BASE = np.cumsum([0, EVEN_IN, EVEN_OUT, ODD_IN, ODD_OUT, SEC_IN, SEC_OUT]).tolist()
UNITS = BASE[-1]

PARAMS = {}
_at = 0
for _name, _n in (("norm_even", 8), ("conv_w", 12), ("norm_odd", 8), ("final_norm", 8), ("norm_in", 8),
                  ("norm_out", 8), ("q_gain", 1), ("k_gain", 1), ("pool_scale", 8), ("conv_w2", 40),
                  ("conv_b2", 8), ("mh_norm", 8), ("skip", 8)):
    PARAMS[_name] = _at
    _at += _n
N_PARAMS = _at



def linker(eng, step):
    count = {}

    def link(instruction, semaphore=None):
        semaphore = step if semaphore is None else semaphore
        instruction.then_inc(semaphore, 1)
        count[id(semaphore)] = count.get(id(semaphore), 0) + 1
        eng.wait_ge(semaphore, count[id(semaphore)])

    def signal(semaphore):
        eng.sem_inc(semaphore, 1)
        count[id(semaphore)] = count.get(id(semaphore), 0) + 1

    return link, signal


def build(nc, x_t, weight_units, channel_params, ident_in, dft_d, dft_s, rope, edge, masks, block_mask,
          qkv_blocks, gate_w, gate_b, pool_w, reset_mask, out):
    ctx = ExitStack()
    with ctx:
        def sem(name):
            return ctx.enter_context(nc.semaphore(name))

        def dram(name, shape):
            return nc.dram_tensor(name, shape, F32).ap()

        x1_dram = dram("x1_dram", [KT, P, S])
        x2_dram = dram("x2_dram", [KT, P, S])
        y1_dram = dram("y1_dram", [KT, P, S])
        y2_dram = dram("y2_dram", [KT, P, S])
        y3_dram = dram("y3_dram", [2 * KT, P, S])
        mz_dram = dram("mz_dram", [KT, P, S])
        gate_dram = dram("gate_dram", [16, S])
        bm_dram = dram("bm_dram", [2 * MH, S])
        decay_dram = dram("decay_dram", [2 * MH, CH])

        at = [-(-nc.sbuf_base // 32) * 32]

        def keep(name, shape, dt=F32):
            tensor = nc.alloc_sbuf_tensor_at(name, shape, dt, offset=at[0])
            size = 4
            for n in shape[1:]:
                size *= n
            at[0] += -(-size // 32) * 32
            assert at[0] <= nc.sbuf_usable_end, name
            return tensor


        par = keep("par", [P, N_PARAMS])
        ident = keep("ident", [P, P])
        ones = keep("ones", [P, P])
        eps_col = keep("eps_col", [P, 1])
        w_raw = keep("w_raw", [P, 3, KT * P])
        w_hi = keep("w_hi", [P, 2, KT * P], F32R)
        w_lo = keep("w_lo", [P, 2, KT * P], F32R)

        def col(name, i=0):
            return par[:, PARAMS[name] + i:PARAMS[name] + i + 1]

        op_start = at[0]
        op_hi = keep("op_hi", [P, KT, S], F32R)
        op_lo = keep("op_lo", [P, KT, S], F32R)
        phase_start = at[0]
        xa = keep("xa", [P, KT, S])
        stage_a = keep("stage_a", [P, 2, S])
        sq_a = keep("sq_a", [P, 2, S])
        rstd_a = keep("rstd_a", [P, S])
        y_a = keep("y_a", [P, 2, S])
        tab_d = keep("tab_d", [P, 3, 2 * P])
        tab_s = keep("tab_s", [P, 2, RADIX, P])
        spec = keep("spec", [P, RADIX, 2 * P])
        parts = keep("parts", [P, RADIX, P])
        fold = keep("fold", [P, RADIX, P])
        bu = keep("bu", [P, RADIX, P])
        ax_sb = keep("ax_sb", [P, S])
        u_pad = keep("u_pad", [P, S + 2])
        cv = keep("cv", [P, S])
        sz_a = keep("sz_a", [P, S])
        sz_b = keep("sz_b", [P, S])
        at[0] = phase_start
        q_hi = keep("q_hi", [P, 2, S], F32R)
        q_lo = keep("q_lo", [P, 2, S], F32R)
        k_hi = keep("k_hi", [P, KV_HEADS, S], F32R)
        k_lo = keep("k_lo", [P, KV_HEADS, S], F32R)
        v_hi = keep("v_hi", [P, KV_HEADS, QT, P], F32R)
        v_lo = keep("v_lo", [P, KV_HEADS, QT, P], F32R)
        pt_hi = keep("pt_hi", [P, QT, 2 * P], F32R)
        pt_lo = keep("pt_lo", [P, QT, 2 * P], F32R)
        prob = keep("prob", [P, 2, S])
        rope_sb = keep("rope_sb", [P, 2, S])
        sz_q = keep("sz_q", [P, 2, S])
        sq_b = keep("sq_b", [P, S])
        rstd_b = keep("rstd_b", [P, S])
        qn = keep("qn", [P, S])
        y_b = keep("y_b", [P, 2, S])
        stat_b = keep("stat_b", [P, 2, 4])
        at[0] = phase_start
        xc = keep("xc", [P, KT, S])
        stage_c = keep("stage_c", [P, 2, S])
        sq_c = keep("sq_c", [P, 2, S])
        rstd_c = keep("rstd_c", [P, S])
        at[0] = phase_start
        u_rows = keep("u_rows", [P, KT, S + 4])
        c_rows = keep("c_rows", [P, KT, S])
        conv_acc = keep("conv_acc", [P, 2, S + 2 * PAD])
        pool_pad = keep("pool_pad", [P, S + 2 * PAD])
        pooled = keep("pooled", [P, 2, S])
        sz_p = keep("sz_p", [P, S])
        y_d = keep("y_d", [P, 2, S])
        pw_sb = keep("pw_sb", [P, 2, 2, MD])
        gw_sb = keep("gw_sb", [P, 3 * KT, 16])
        gw_eff = keep("gw_eff", [P, 2 * KT, 16])
        blocks_d = keep("blocks_d", [P, 3, KT, 4])
        bmask_d = keep("bmask_d", [P, 32])
        bdt = keep("bdt", [P, 2, P])
        edge_sb = keep("edge_sb", [P, 4, 2, PAD])
        gate_rows = keep("gate_rows", [16, S])
        gb_sb = keep("gb_sb", [16, 1])
        at[0] = op_start
        q_t = keep("q_t", [P, 2, S])
        k_t = keep("k_t", [P, 2, S])
        k_tok = keep("k_tok", [P, CH, MD])
        v_tok = keep("v_tok", [P, CH, VE])
        h_tok = keep("h_tok", [P, CH, MD])
        bm_b = keep("bm_b", [P, NDIR, S])
        state = keep("state", [P, NDIR, 2, VE])
        e_w = keep("e_w", [P, NDIR, P])
        w_t = keep("w_t", [P, NDIR, P])
        num_a = keep("num_a", [P, NDIR, VE])
        num_b = keep("num_b", [P, NDIR, VE])
        k_w = keep("k_w", [P, NDIR, MD])
        assert at[0] <= phase_start
        at[0] = phase_start + 4 * KT * (2 * S + 4)
        bd = keep("bd", [P, 3, KT, P])
        blocks_e = keep("blocks_e", [P, 3, KT, 4])
        bmask_e = keep("bmask_e", [P, 32])
        mask_sb = keep("mask_sb", [P, NDIR, P])
        g_tok = keep("g_tok", [P, CH, 32])
        decay_b = keep("decay_b", [P, 2 * MH, CH])
        small = keep("small", [P, NDIR, 4])
        bn6 = keep("bn6", [P, CH, 6])
        bn2 = keep("bn2", [P, CH, 2])
        rstd_h = keep("rstd_h", [P, CH])
        rows_start = at[0]
        i_row = keep("i_row", [36, S])
        f_row = keep("f_row", [36, S])
        t_row = keep("t_row", [36, S])
        b_row = keep("b_row", [36, S])
        reset_row = keep("reset_row", [36, S])
        a_row = keep("a_row", [36, S])
        g_rows = keep("g_rows", [32, S])
        mp_row = keep("mp_row", [36, CH])
        end_row = keep("end_row", [36, CH])
        dec_tmp = keep("dec_tmp", [36, CH])
        dec_row = keep("dec_row", [36, CH])
        at[0] = rows_start
        out_e = keep("out_e", [P, 2, S])
        mz_sb = keep("mz_sb", [P, 2, S])
        at[0] = op_start
        o_hi = keep("o_hi", [P, 2 * KT, S], F32R)
        o_lo = keep("o_lo", [P, 2 * KT, S], F32R)
        xf = keep("xf", [P, KT, S])
        stage_f = keep("stage_f", [P, 2, S])
        sq_f = keep("sq_f", [P, 1, S])
        rstd_f = keep("rstd_f", [P, S])

        pair = [ctx.enter_context(nc.psum_tensor(f"pair{i}", [P, S], F32)) for i in range(2)]
        aux = ctx.enter_context(nc.psum_tensor("aux", [P, 4 * HALF], F32))

        consts = sem("consts")
        ready0 = sem("ready0")
        w_loaded = [sem(f"w_loaded{i}") for i in range(3)]
        w_hi_done = sem("w_hi_done")
        w_split = sem("w_split")
        unit_done = sem("unit_done")
        pair_free = [sem(f"pair_free{i}") for i in range(2)]
        x_loaded = [sem(f"x_loaded{i}") for i in range(KT)]
        x_done = sem("x_done")
        sq_ready, stat_done, rstd_ready = sem("sq_ready"), sem("stat_done"), sem("rstd_ready")
        hn_ready, hi_ready, op_ready = sem("hn_ready"), sem("hi_ready"), sem("op_ready")
        x_stored = sem("x_stored")
        y_in = [sem(f"y_in{i}") for i in range(2)]
        y_made = sem("y_made")
        y_stored = [sem(f"y_stored{i}") for i in range(2)]
        dve_step, act_step = sem("dve_step"), sem("act_step")
        bu_ready, parts_ready, fft1_done = sem("bu_ready"), sem("parts_ready"), sem("fft1_done")
        spec_ready, fft2_done = sem("spec_ready"), sem("fft2_done")
        ax_ready, prod_done, szb_ready, sza_ready = sem("ax_ready"), sem("prod_done"), sem("szb_ready"), sem("sza_ready")
        qsq, qstat, qrstd, qn_ready, rot_ready = sem("qsq"), sem("qstat"), sem("qrstd"), sem("qn_ready"), sem("rot_ready")
        qr_ready, qhi_ready, q_ready = sem("qr_ready"), sem("qhi_ready"), sem("q_ready")
        vt_ready, vtr_done, vhi_ready, v_ready = sem("vt_ready"), sem("vtr_done"), sem("vhi_ready"), sem("v_ready")
        szq_ready, s_done, neg_ready, exp_done = sem("szq_ready"), sem("s_done"), sem("neg_ready"), sem("exp_done")
        p_ready, t_done, pt_hi_ready, pt_ready = sem("p_ready"), sem("t_done"), sem("pt_hi_ready"), sem("pt_ready")
        pv_done, yq_done = sem("pv_done"), sem("yq_done")
        consts_d, pads_ready = sem("consts_d"), sem("pads_ready")
        bdt_ready, weff_done, weff_ready = sem("bdt_ready"), sem("weff_done"), sem("weff_ready")
        u_ready, conv_done, c_ready, gate_done, gate_ready, gate_stored = (
            sem("u_ready"), sem("conv_done"), sem("c_ready"), sem("gate_done"), sem("gate_ready"), sem("gate_stored"))
        px_ready, pooled_ready, mix_done, szp_ready = sem("px_ready"), sem("pooled_ready"), sem("mix_done"), sem("szp_ready")
        pw_loaded = [sem(f"pw_loaded{i}") for i in range(2)]
        mz_ready = sem("mz_ready")
        mz_stored = [sem(f"mz_stored{i}") for i in range(2)]
        consts_e, rows_in = sem("consts_e"), sem("rows_in")
        rows_clear, bm_made, row_act, row_dve = sem("rows_clear"), sem("bm_made"), sem("row_act"), sem("row_dve")
        g_made, g_moved, decay_in = sem("g_made"), sem("g_moved"), sem("decay_in")
        gt_done, gt_ready, bd_ready = sem("gt_done"), sem("gt_ready"), sem("bd_ready")
        bm_loaded, bm_ready = sem("bm_loaded"), sem("bm_ready")
        prep_done, prep_act, prep_dve = sem("prep_done"), sem("prep_act"), sem("prep_dve")
        st_done, e_ready, wt_ready, ab_done = sem("st_done"), sem("e_ready"), sem("wt_ready"), sem("ab_done")
        kw_ready, upd_done, state_ready, acp_ready, h_done = (
            sem("kw_ready"), sem("upd_done"), sem("state_ready"), sem("acp_ready"), sem("h_done"))
        bn_ready, rh_ready, ln_done, ht_done = sem("bn_ready"), sem("rh_ready"), sem("ln_done"), sem("ht_done")
        mz_in = [sem(f"mz_in{i}") for i in range(2)]
        out_made, out_stored = sem("out_made"), [sem(f"out_stored{i}") for i in range(2)]

        JOBS = BASE[5] + KT

        def job_of(unit):
            return unit if unit < BASE[5] else BASE[5] + (unit - BASE[5]) // 2

        def last_unit(job):
            return job if job < BASE[5] else BASE[5] + 2 * (job - BASE[5]) + 1

        def wait_job(eng, job):
            eng.wait_ge(unit_done, last_unit(job) + 1)

        OP0 = {"even": 0, "y1": KT, "odd": 2 * KT, "y2": 3 * KT, "in": 4 * KT, "y3": 5 * KT}
        UNIT0 = {"even": BASE[0], "y1": BASE[1], "odd": BASE[2], "y2": BASE[3], "in": BASE[4], "y3": BASE[5]}
        Y0 = {"y1": 0, "y2": KT, "y3": 2 * KT}

        Y_ORDER = {"y1": [b for j in range(AB) for b in (AB + j, j)],
                   "y2": list(range(HEADS)),
                   "y3": list(range(2 * KT))}
        Y_DRAM = {"y1": y1_dram, "y2": y2_dram, "y3": y3_dram}

        block = ctx.enter_context(nc.Block())

        @block.sync
        def _(sp):
            loaded = [0]

            def weights_to(n):
                for u in range(loaded[0], min(n, UNITS)):
                    if u >= 3:
                        sp.wait_ge(w_split, u - 2)
                    sp.dma_start(w_raw[:, u % 3, :], weight_units[u]).then_inc(w_loaded[u % 3], 16)
                loaded[0] = max(loaded[0], n)

            def store_y(layer, n, buf):
                sp.wait_ge(y_made, Y0[layer] + n + 1)
                sp.dma_start(Y_DRAM[layer][Y_ORDER[layer][n]], buf[:, n % 2, :]).then_inc(
                    y_stored[n % 2], 16)

            def load_y(layer, k, buf):
                n = Y_ORDER[layer].index(k)
                sp.wait_ge(y_stored[n % 2], 16 * (Y0[layer] // 2 + n // 2 + 1))
                if k >= 2:
                    sp.wait_ge(op_ready, OP0[layer] + k - 1)
                sp.dma_start(buf[:, k % 2, :], Y_DRAM[layer][k]).then_inc(y_in[k % 2], 16)

            sp.dma_start(ident[:, :], ident_in).then_inc(consts, 16)
            sp.dma_start(par[:, :], channel_params).then_inc(consts, 16)
            for k in range(KT):
                sp.dma_start(xa[:, k, :], x_t[k]).then_inc(x_loaded[k], 16)
            weights_to(2)
            sp.dma_start(tab_d[:, :, :], dft_d).then_inc(consts, 16)
            sp.dma_start(tab_s[:, :, :, :], dft_s).then_inc(consts, 16)
            for j in range(AB):
                weights_to(6 * j + 9)
                store_y("y1", 2 * j, y_a)
                store_y("y1", 2 * j + 1, y_a)
            for k in range(KT):
                load_y("y1", k, stage_a)
            weights_to(BASE[2] + 3)
            for k in range(KT):
                sp.wait_ge(x_done, k + 1)
                sp.dma_start(x1_dram[k], xa[:, k, :]).then_inc(x_stored, 16)
            sp.wait_ge(op_ready, OP0["odd"] + KT)
            sp.wait_ge(x_stored, 16 * KT)
            sp.dma_start(rope_sb[:, :, :], rope).then_inc(consts, 16)
            for h in range(HEADS):
                weights_to(min(BASE[2] + 11 + 2 * h, BASE[3] + 3))
                store_y("y2", h, y_b)
            sp.wait_ge(y_stored[0], 16 * (Y0["y2"] // 2 + HEADS // 2))
            sp.wait_ge(y_stored[1], 16 * (Y0["y2"] // 2 + HEADS // 2))
            sp.wait_ge(unit_done, BASE[3])
            for k in range(KT):
                load_y("y2", k, stage_c)
                sp.dma_start(xc[:, k, :], x1_dram[k]).then_inc(x_loaded[k], 16)
            weights_to(BASE[4] + 3)
            for k in range(KT):
                sp.wait_ge(x_done, 2 * KT + k + 1)
                sp.dma_start(x2_dram[k], xc[:, k, :]).then_inc(x_stored, 16)
            sp.wait_ge(op_ready, OP0["in"] + KT)
            sp.wait_ge(x_stored, 32 * KT)
            sp.dma_start(blocks_d[:, :, :, :], qkv_blocks[1]).then_inc(consts_d, 16)
            sp.dma_start(bmask_d[:, :], block_mask).then_inc(consts_d, 16)
            sp.dma_start(gw_sb[:, :, :], gate_w).then_inc(consts_d, 16)
            sp.dma_start(gb_sb[:, :], gate_b).then_inc(consts_d, 16)
            sp.dma_start(edge_sb[:, :, :, :], edge).then_inc(consts_d, 16)
            for g in range(2):
                sp.dma_start(pw_sb[:, g, :, :], pool_w[g]).then_inc(pw_loaded[g], 16)
            for g in range(4):
                weights_to(BASE[4] + 15 + 4 * g)
                store_y("y3", 2 * g, y_d)
                store_y("y3", 2 * g + 1, y_d)
                if g + 2 < 4:
                    sp.dma_start(pw_sb[:, g % 2, :, :], pool_w[g + 2]).then_inc(pw_loaded[g % 2], 16)
                if g == 1:
                    sp.wait_ge(gate_ready, 1)
                    sp.dma_start(gate_dram[:, :], gate_rows[:, :]).then_inc(gate_stored, 16)
            for t in range(KT):
                weights_to(min(BASE[4] + 28 + t, BASE[5] + 3))
                sp.wait_ge(mz_ready, t + 1)
                sp.dma_start(mz_dram[t], y_d[:, t % 2, :]).then_inc(mz_stored[t % 2], 16)
            sp.wait_ge(mz_stored[0], 16 * KT // 2)
            sp.wait_ge(mz_stored[1], 16 * KT // 2)
            sp.wait_ge(gate_stored, 16)
            sp.dma_start(blocks_e[:, :, :, :], qkv_blocks[0]).then_inc(consts_e, 16)
            sp.dma_start(bmask_e[:, :], block_mask).then_inc(consts_e, 16)
            sp.dma_start(mask_sb[:, :, :], masks).then_inc(consts_e, 16)
            sp.wait_ge(rows_clear, 2)
            for d in range(NDIR):
                sp.dma_start(i_row[32 * d:32 * d + MH, :],
                             gate_dram[MH * d:MH * d + MH, :]).then_inc(rows_in, 16)
                sp.dma_start(f_row[32 * d:32 * d + MH, :],
                             gate_dram[8 + MH * d:8 + MH * d + MH, :]).then_inc(rows_in, 16)
            sp.dma_start(reset_row[:, :], reset_mask).then_inc(rows_in, 16)
            sp.wait_ge(bm_made, 1)
            for d in range(NDIR):
                sp.dma_start(bm_dram[MH * d:MH * d + MH, :],
                             reset_row[32 * d:32 * d + MH, :]).then_inc(g_moved, 16)
            sp.wait_ge(g_made, 1)
            for d in range(NDIR):
                for n, row in enumerate((a_row, t_row, f_row, b_row)):
                    sp.dma_start(g_rows[8 * n + MH * d:8 * n + MH * d + MH, :],
                                 row[32 * d:32 * d + MH, :]).then_inc(g_moved, 16)
                sp.dma_start(decay_dram[MH * d:MH * d + MH, :],
                             dec_row[32 * d:32 * d + MH, :]).then_inc(g_moved, 16)
            sp.wait_ge(g_moved, 16 * 12)
            sp.dma_start(decay_b[:, :, :].rearrange("p r c -> p (r c)"),
                         decay_dram.rearrange("r c -> (r c)").rearrange("(a n) -> a n", a=1)
                         .broadcast_to([P, 2 * MH * CH])).then_inc(decay_in, 16)
            for h in range(MH):
                if h >= 1:
                    sp.wait_ge(e_ready, NDIR * CH * h)
                for d in range(NDIR):
                    sp.dma_start(bm_b[:, d, :], bm_dram[MH * d + h:MH * d + h + 1, :]
                                 .broadcast_to([P, S])).then_inc(bm_loaded, 16)
                for t in range(2):
                    if h >= 1:
                        sp.wait_ge(y_made, Y0["y3"] + KT + 2 * h + t - 1)
                    else:
                        sp.wait_ge(gt_ready, 1)
                    sp.dma_start(mz_sb[:, t, :], mz_dram[2 * h + t]).then_inc(mz_in[t], 16)
                for t in range(2):
                    store_y("y3", KT + 2 * h + t, out_e)
            sp.wait_ge(y_stored[0], 16 * (Y0["y3"] // 2 + KT))
            sp.wait_ge(y_stored[1], 16 * (Y0["y3"] // 2 + KT))
            for k in range(KT):
                sp.dma_start(xf[:, k, :], x2_dram[k]).then_inc(x_loaded[k], 16)
            for k in range(2 * KT):
                load_y("y3", k, stage_f)
            weights_to(UNITS)
            for k in range(KT):
                sp.wait_ge(out_made, k + 1)
                sp.dma_start(out[k], stage_f[:, k % 2, :]).then_inc(out_stored[k % 2], 16)
            sp.wait_ge(out_stored[0], 16 * KT // 2)
            sp.wait_ge(out_stored[1], 16 * KT // 2)

        @block.gpsimd
        def _(pool):
            for u in range(UNITS):
                pool.wait_ge(w_loaded[u % 3], 16 * (u // 3 + 1))
                if u >= 2:
                    pool.wait_ge(unit_done, u - 1)
                    pool.wait_ge(w_split, u - 1)
                pool.tensor_copy(w_hi[:, u % 2, :], w_raw[:, u % 3, :]).then_inc(w_hi_done, 1)
                pool.wait_ge(w_hi_done, u + 1)
                pool.tensor_tensor(w_lo[:, u % 2, :], w_raw[:, u % 3, :], w_hi[:, u % 2, :],
                                   ALU.subtract).then_inc(w_split, 1)

        @block.tensor
        def _(pe):
            def unit(u, job, hi, lo, layer, kt0=0, wait_operand=False, first=True, last=True):
                pe.wait_ge(w_split, u + 1)
                if first and job >= 2:
                    pe.wait_ge(pair_free[job % 2], job // 2)
                acc = pair[job % 2]
                for k in range(KT):
                    if wait_operand:
                        pe.wait_ge(op_ready, OP0[layer] + kt0 + k + 1)
                    wh = w_hi[:, u % 2, k * P:(k + 1) * P]
                    wl = w_lo[:, u % 2, k * P:(k + 1) * P]
                    for n, (w, x) in enumerate(((wh, hi), (wh, lo), (wl, hi))):
                        for half in range(2):
                            cols = slice(half * HALF, (half + 1) * HALF)
                            mm = pe.matmul(acc[:, cols], w, x[:, kt0 + k, cols],
                                           start=(first and k == 0 and n == 0),
                                           stop=(last and k == KT - 1 and n == 2))
                mm.then_inc(unit_done, 1)

            def norm_stats(n, sq, bufs):
                for k in range(KT):
                    pe.wait_ge(sq_ready, KT * n + k + 1)
                    for half in range(2):
                        cols = slice(half * HALF, (half + 1) * HALF)
                        mm = pe.matmul(aux[:, cols], ones[:, :], sq[:, k % bufs, cols],
                                       start=(k == 0), stop=(k == KT - 1))
                    mm.then_inc(stat_done, 1)

            pe.wait_ge(consts, 64)
            pe.wait_ge(ready0, 2)
            norm_stats(0, sq_a, 2)

            def fft_channels(j):
                pe.wait_ge(parts_ready, j + 1)
                if j == 0:
                    pe.wait_ge(rstd_ready, 1)
                else:
                    pe.wait_ge(y_made, 2 * j - 1)
                for k1 in range(RADIX):
                    o = aux[:, k1 * 2 * P:(k1 + 1) * 2 * P]
                    if k1 % 4 == 0:
                        mm = pe.matmul(o, parts[:, k1 // 4, :], tab_d[:, 0, :], start=True, stop=True)
                    else:
                        r = min(k1, RADIX - k1)
                        pe.matmul(o, parts[:, 2 * r, :], tab_d[:, 0, :], start=True, stop=False)
                        mm = pe.matmul(o, parts[:, 2 * r + 1, :], tab_d[:, 1 if k1 < 4 else 2, :],
                                       start=False, stop=True)
                mm.then_inc(fft1_done, 1)

            def fft_time(j):
                pe.wait_ge(spec_ready, j + 1)
                for k1 in range(RADIX):
                    o = aux[:, k1 * P:(k1 + 1) * P]
                    pe.matmul(o, spec[:, k1, 0:P], tab_s[:, 0, k1, :], start=True, stop=False)
                    mm = pe.matmul(o, spec[:, k1, P:2 * P], tab_s[:, 1, k1, :], start=False, stop=True)
                mm.then_inc(fft2_done, 1)

            for j in range(AB):
                for i in range(6):
                    u = 6 * j + i
                    unit(u, u, op_hi, op_lo, "even", wait_operand=(u == 0))
                    if i == 1:
                        fft_channels(j)
                    if i == 2:
                        fft_time(j)
            for e in range(KT):
                unit(BASE[1] + e, BASE[1] + e, op_hi, op_lo, "y1", wait_operand=(e == 0))
            norm_stats(1, sq_a, 2)

            def q_stats(i):
                pe.wait_ge(qsq, i + 1)
                if i == 0:
                    pe.wait_ge(rstd_ready, 2)
                for half in range(2):
                    cols = slice(half * HALF, (half + 1) * HALF)
                    mm = pe.matmul(aux[:, cols], ones[:, :], sq_b[:, cols], start=True, stop=True)
                mm.then_inc(qstat, 1)

            def v_transpose(g):
                pe.wait_ge(vt_ready, g + 1)
                if g >= 1:
                    pe.wait_ge(v_ready, g)
                for t in range(QT):
                    mm = pe.transpose(aux[:, 2 * HALF + t * P:2 * HALF + (t + 1) * P],
                                      qn[:, t * P:(t + 1) * P], ident[:, :])
                mm.then_inc(vtr_done, 1)

            for g in range(KV_HEADS):
                unit(BASE[2] + 2 * g, BASE[2] + 2 * g, op_hi, op_lo, "odd", wait_operand=(g == 0))
                q_stats(g)
                unit(BASE[2] + 2 * g + 1, BASE[2] + 2 * g + 1, op_hi, op_lo, "odd")
                v_transpose(g)

            def head_units(h):
                for i in range(2):
                    u = BASE[2] + 4 + 2 * h + i
                    if h >= 2 and i == 0:
                        pe.wait_ge(pt_ready, QT * (h - 1))
                    if h >= 2 and i == 1:
                        pe.wait_ge(yq_done, 4 * (h - 1))
                    unit(u, u, op_hi, op_lo, "odd")
                if h >= 1:
                    pe.wait_ge(exp_done, QT * (h - 1))
                q_stats(KV_HEADS + h)

            def scores(h, i):
                t = h * QT + i
                if i == 0:
                    pe.wait_ge(q_ready, KV_HEADS + h + 1)
                    if h == 0:
                        pe.wait_ge(v_ready, KV_HEADS)
                if i < 2:
                    pe.wait_ge(qrstd, KV_HEADS + min(h + 1, HEADS - 1) + 1)
                if t >= 2:
                    pe.wait_ge(exp_done, t - 1)
                b = (t % 2) * S
                g = h // GROUP
                rows = slice(i * P, (i + 1) * P)
                for n, (a, k) in enumerate(((q_hi, k_hi), (q_hi, k_lo), (q_lo, k_hi))):
                    for half in range(2):
                        cols = slice(half * HALF, (half + 1) * HALF)
                        mm = pe.matmul(aux[:, b + half * HALF:b + (half + 1) * HALF],
                                       a[:, h % 2, rows], k[:, g, cols],
                                       start=(n == 0), stop=(n == 2))
                mm.then_inc(s_done, 1)

            def turn(h, i):
                t = h * QT + i
                pe.wait_ge(p_ready, t + 1)
                if t >= 1:
                    pe.wait_ge(pt_ready, t)
                if i == 0:
                    z_job = BASE[2] + 4 + 2 * min(h + 1, HEADS - 1)
                    pe.wait_ge(pair_free[z_job % 2], z_job // 2 + 1)
                for k in range(QT):
                    mm = pe.transpose(pair[0][:, k * P:(k + 1) * P],
                                      prob[:, t % 2, k * P:(k + 1) * P], ident[:, :])
                mm.then_inc(t_done, 1)

            def weigh_values(h, m):
                t = h * 4 + m
                pe.wait_ge(pt_ready, h * QT + 2 * m + 2)
                if m == 0:
                    q_job = BASE[2] + 5 + 2 * min(h + 1, HEADS - 1)
                    pe.wait_ge(pair_free[q_job % 2], q_job // 2 + 1)
                if t >= 2:
                    pe.wait_ge(yq_done, t - 1)
                g = h // GROUP
                o = pair[1][:, (t % 2) * HALF:(t % 2) * HALF + 2 * P]
                for k in range(QT):
                    for n, (v, p) in enumerate(((v_hi, pt_hi), (v_hi, pt_lo), (v_lo, pt_hi))):
                        mm = pe.matmul(o, v[:, g, k, :], p[:, k, :],
                                       start=(k == 0 and n == 0), stop=(k == QT - 1 and n == 2))
                mm.then_inc(pv_done, 1)

            head_units(0)
            for h in range(HEADS):
                if h + 1 < HEADS:
                    head_units(h + 1)
                scores(h, 0)
                scores(h, 1)
                for i in range(QT):
                    turn(h, i)
                    if i + 2 < QT:
                        scores(h, i + 2)
                    if i % 2:
                        weigh_values(h, i // 2)
            pe.wait_ge(pt_ready, QT * HEADS)
            pe.wait_ge(yq_done, 4 * HEADS)
            for e in range(KT):
                unit(BASE[3] + e, BASE[3] + e, op_hi, op_lo, "y2", wait_operand=(e == 0))
            norm_stats(2, sq_c, 2)
            pe.wait_ge(rstd_ready, 3)
            norm_stats(3, sq_c, 2)

            for i in range(3 * KT):
                t, which = i // 3, i % 3
                pe.wait_ge(bdt_ready, i + 1)
                if i == 0:
                    pe.wait_ge(rstd_ready, 4)
                pos = (t if which < 2 else KT + t) * 16
                mm = pe.matmul(aux[:, pos:pos + 16], bdt[:, i % 2, :], gw_sb[:, which * KT + t, :],
                               start=(which != 1), stop=(which != 0))
                mm.then_inc(weff_done, 1)

            def gates(t):
                for half in range(2):
                    cols = slice(half * HALF, (half + 1) * HALF)
                    o = aux[0:16, 2 * HALF + half * HALF:2 * HALF + (half + 1) * HALF]
                    pe.wait_ge(weff_ready, 1)
                    pe.wait_ge(u_ready, t + 1)
                    pe.matmul(o, gw_eff[:, KT + t, :], u_rows[:, t, 2 + half * HALF:2 + (half + 1) * HALF],
                              start=(t == 0), stop=False)
                    pe.wait_ge(c_ready, t + 1)
                    mm = pe.matmul(o, gw_eff[:, t, :], c_rows[:, t, cols], start=False, stop=(t == KT - 1))
                if t == KT - 1:
                    mm.then_inc(gate_done, 1)

            for t in range(KT):
                unit(BASE[4] + t, BASE[4] + t, op_hi, op_lo, "in", wait_operand=(t == 0))
                if t >= 1:
                    gates(t - 1)
            for g in range(4):
                for i in range(4):
                    unit(BASE[4] + 8 + 4 * g + i, BASE[4] + 8 + 4 * g + i, op_hi, op_lo, "in")
                    if g == 0 and i == 0:
                        gates(KT - 1)
                    if i >= 2:
                        m = i - 2
                        pe.wait_ge(pooled_ready, 2 * g + 2)
                        pe.wait_ge(pw_loaded[g % 2], 16 * (g // 2 + 1))
                        if 2 * g + m >= 1:
                            pe.wait_ge(y_made, Y0["y3"] + 2 * g + m)
                        for half in range(2):
                            cols = slice(half * HALF, (half + 1) * HALF)
                            for k in range(2):
                                mm = pe.matmul(aux[:, cols], pw_sb[:, g % 2, k, m * P:(m + 1) * P],
                                               pooled[:, k, cols], start=(k == 0), stop=(k == 1))
                        mm.then_inc(mix_done, 1)
            for t in range(KT):
                unit(BASE[4] + 24 + t, BASE[4] + 24 + t, op_hi, op_lo, "in")

            pe.wait_ge(g_moved, 16 * 12)
            for c in range(CH):
                mm = pe.transpose(aux[:, c * 32:(c + 1) * 32], g_rows[:, c * P:(c + 1) * P], ident[0:32, 0:32])
            mm.then_inc(gt_done, 1)
            pe.wait_ge(bd_ready, 1)
            pe.wait_ge(pair_free[(BASE[5] - 1) % 2], (BASE[5] - 1) // 2 + 1)
            pe.wait_ge(pair_free[(BASE[5] - 2) % 2], (BASE[5] - 2) // 2 + 1)

            def prepare(h):
                def step(n):
                    if n % 2 == 0 and 4 * h + n // 2 >= 1:
                        pe.wait_ge(prep_act, 4 * h + n // 2)
                    if n % 2 and 4 * h + n // 2 >= 1:
                        pe.wait_ge(prep_dve, 4 * h + n // 2)
                if h >= 1:
                    pe.wait_ge(y_made, Y0["y3"] + KT + 2 * h)
                for n in range(4):
                    step(n)
                    i = n % 2
                    for half in range(2):
                        cols = slice(half * HALF, (half + 1) * HALF)
                        mm = pe.matmul(pair[n % 2][:, cols], bd[:, n // 2, 2 * h + i, :],
                                       c_rows[:, 2 * h + i, cols], start=True, stop=True)
                    mm.then_inc(prep_done, 1)
                for n in range(4, 8):
                    step(n)
                    for c in range(4):
                        chunk = 4 * (n % 2) + c
                        for i in range(2):
                            if n < 6:
                                x = c_rows[:, 2 * h + i, chunk * P:(chunk + 1) * P]
                            else:
                                x = u_rows[:, 2 * h + i, 2 + chunk * P:2 + (chunk + 1) * P]
                            mm = pe.matmul(pair[n % 2][:, c * MD + i * P:c * MD + (i + 1) * P], x,
                                           bd[:, 1 if n < 6 else 2, 2 * h + i, :], start=True, stop=True)
                    mm.then_inc(prep_done, 1)

            for h in range(MH):
                prepare(h)
                pe.wait_ge(prep_act, 4 * h + 2)
                pe.wait_ge(prep_dve, 4 * h + 2)
                pe.wait_ge(gt_ready, 1)
                if h >= 1:
                    pe.wait_ge(wt_ready, NDIR * CH * h)
                for c in range(CH):
                    for i in range(2):
                        mm = pe.matmul(aux[:, c * P:(c + 1) * P], k_t[:, i, c * P:(c + 1) * P],
                                       q_t[:, i, c * P:(c + 1) * P], start=(i == 0), stop=(i == 1))
                mm.then_inc(st_done, 1)
                pe.wait_ge(prep_act, 4 * h + 4)
                pe.wait_ge(prep_dve, 4 * h + 4)
                for n in range(CH):
                    for d in range(NDIR):
                        c = n if d == 0 else CH - 1 - n
                        g = NDIR * (CH * h + n) + d
                        ks = NDIR * ((CH - 1) * h + n) + d
                        if n >= 1:
                            pe.wait_ge(h_done, g - 1)
                        pe.wait_ge(wt_ready, g + 1)
                        mm = pe.matmul(pair[0][:, d * HALF:d * HALF + VE], w_t[:, d, :], v_tok[:, c, :],
                                       start=True, stop=True)
                        if n >= 1:
                            pe.wait_ge(state_ready, NDIR * ((CH - 1) * h + n - 1) + d + 1)
                            for i in range(2):
                                mm = pe.matmul(pair[1][:, d * HALF:d * HALF + VE],
                                               q_t[:, i, c * P:(c + 1) * P], state[:, d, i, :],
                                               start=(i == 0), stop=(i == 1))
                        mm.then_inc(ab_done, 1)
                        if n < CH - 1:
                            pe.wait_ge(kw_ready, ks + 1)
                            if ks >= 1:
                                pe.wait_ge(state_ready, ks)
                            for i in range(2):
                                o = aux[:, 2 * HALF + i * HALF:2 * HALF + i * HALF + VE]
                                mm = pe.matmul(o, k_w[:, d, i * P:(i + 1) * P], v_tok[:, c, :],
                                               start=True, stop=True)
                            mm.then_inc(upd_done, 1)
                pe.wait_ge(ln_done, h + 1)
                for i in range(2):
                    for c in range(CH):
                        mm = pe.transpose(pair[i][:, c * P:(c + 1) * P], h_tok[:, c, i * P:(i + 1) * P],
                                          ident[:, :])
                    mm.then_inc(ht_done, 1)

            pe.wait_ge(y_made, Y0["y3"] + 2 * KT)
            for e in range(KT):
                for i in range(2):
                    unit(BASE[5] + 2 * e + i, BASE[5] + e, o_hi, o_lo, "y3", kt0=KT * i,
                         wait_operand=(e == 0), first=(i == 0), last=(i == 1))
            norm_stats(4, sq_f, 1)

        @block.scalar
        def _(act):
            link, signal = linker(act, act_step)

            def norm_squares(n, x, sq, bufs, x0, by_dma):
                for k in range(KT):
                    if by_dma:
                        act.wait_ge(x_loaded[k], 16)
                    else:
                        act.wait_ge(x_done, x0 + k + 1)
                    if k >= bufs:
                        act.wait_ge(stat_done, KT * n + k - bufs + 1)
                    link(act.activation(sq[:, k % bufs, :], x[:, k, :], ACT.Square), sq_ready)


            def norm_rstd(n, rstd):
                act.wait_ge(stat_done, KT * (n + 1))
                link(act.activation(rstd[:, :], aux[:, 0:S], ACT.Ln, bias=eps_col[:, :], scale=1.0 / D))
                link(act.activation(rstd[:, :], rstd[:, :], ACT.Exp, scale=-0.5), rstd_ready)

            his = [0]

            def split_norm(hn0, stage, hi):
                for k in range(KT):
                    act.wait_ge(hn_ready, hn0 + k + 1)
                    link(act.activation(hi[:, k, :], stage[:, k % 2, :], ACT.Copy), hi_ready)
                his[0] += KT

            def split_y(layer, stage, hi, blocks, in0):
                act.wait_ge(unit_done, UNIT0[layer])
                for k in range(blocks):
                    act.wait_ge(y_in[k % 2], 16 * (in0 + k // 2 + 1))
                    link(act.activation(hi[:, k, :], stage[:, k % 2, :], ACT.Copy), hi_ready)

            act.wait_ge(ready0, 2)
            norm_squares(0, xa, sq_a, 2, 0, True)
            norm_rstd(0, rstd_a)
            split_norm(0, stage_a, op_hi)
            for j in range(AB):
                u = 6 * j
                wait_job(act, u)
                if j >= 1:
                    act.wait_ge(parts_ready, j)
                link(act.activation(bu[:, :, :].rearrange("p a b -> p (a b)"), pair[u % 2][:, :],
                                     ACT.Copy), bu_ready)
                signal(pair_free[u % 2])
                wait_job(act, u + 1)
                if j >= 1:
                    act.wait_ge(prod_done, j)
                link(act.activation(ax_sb[:, :], pair[(u + 1) % 2][:, :], ACT.Copy), ax_ready)
                signal(pair_free[(u + 1) % 2])
                act.wait_ge(fft1_done, j + 1)
                if j >= 1:
                    act.wait_ge(fft2_done, j)
                link(act.activation(spec[:, :, :].rearrange("p a b -> p (a b)"), aux[:, :],
                                     ACT.Copy), spec_ready)
                wait_job(act, u + 3)
                if j >= 1:
                    act.wait_ge(y_made, 2 * j - 1)
                link(act.activation(sz_b[:, :], pair[(u + 3) % 2][:, :], ACT.Silu), szb_ready)
                signal(pair_free[(u + 3) % 2])
                wait_job(act, u + 5)
                if j >= 1:
                    act.wait_ge(y_made, 2 * j)
                link(act.activation(sz_a[:, :], pair[(u + 5) % 2][:, :], ACT.Silu), sza_ready)
                signal(pair_free[(u + 5) % 2])
            split_y("y1", stage_a, op_hi, KT, 0)
            norm_squares(1, xa, sq_a, 2, 0, False)
            norm_rstd(1, rstd_a)
            act.wait_ge(unit_done, BASE[2])
            split_norm(KT, stage_a, op_hi)

            act.wait_ge(op_ready, OP0["odd"] + KT)
            act.wait_ge(x_stored, 16 * KT)

            def q_prepare(i, unit_no, dst_hi, slot):
                wait_job(act, unit_no)
                if i >= 1:
                    act.wait_ge(qr_ready, i)
                link(act.activation(sq_b[:, :], pair[unit_no % 2][:, :], ACT.Square), qsq)
                act.wait_ge(qstat, i + 1)
                link(act.activation(rstd_b[:, :], aux[:, 0:S], ACT.Ln, bias=eps_col[:, :], scale=1.0 / P))
                link(act.activation(rstd_b[:, :], rstd_b[:, :], ACT.Exp, scale=-0.5), qrstd)
                act.wait_ge(qn_ready, i + 1)
                half = P // 2
                link(act.activation(rstd_b[0:half, :], qn[half:P, :], ACT.Copy), rot_ready)
                link(act.activation(rstd_b[half:P, :], qn[0:half, :], ACT.Copy), rot_ready)
                act.wait_ge(qr_ready, i + 1)
                if i >= KV_HEADS + 2:
                    act.wait_ge(s_done, QT * (i - KV_HEADS - 1))
                link(act.activation(dst_hi[:, slot, :], qn[:, :], ACT.Copy), qhi_ready)

            for g in range(KV_HEADS):
                q_prepare(g, BASE[2] + 2 * g, k_hi, g)
                u = BASE[2] + 2 * g + 1
                wait_job(act, u)
                act.wait_ge(q_ready, g + 1)
                link(act.activation(qn[:, :], pair[u % 2][:, :], ACT.Copy), vt_ready)
                signal(pair_free[u % 2])
                act.wait_ge(vtr_done, g + 1)
                link(act.activation(v_hi[:, g, :, :].rearrange("p a b -> p (a b)"),
                                     aux[:, 2 * HALF:4 * HALF], ACT.Copy), vhi_ready)

            def head_gate(h):
                u = BASE[2] + 4 + 2 * h
                wait_job(act, u)
                if h >= 2:
                    act.wait_ge(yq_done, 4 * (h - 1))
                link(act.activation(sz_q[:, h % 2, :], pair[u % 2][:, :], ACT.Silu), szq_ready)
                signal(pair_free[u % 2])

            head_gate(0)
            q_prepare(KV_HEADS, BASE[2] + 5, q_hi, 0)
            for h in range(HEADS):
                if h + 1 < HEADS:
                    head_gate(h + 1)
                    q_prepare(KV_HEADS + h + 1, BASE[2] + 7 + 2 * h, q_hi, (h + 1) % 2)

                def exponentials(t):
                    act.wait_ge(neg_ready, t + 1)
                    if t >= 2:
                        act.wait_ge(t_done, t - 1)
                    link(act.activation(prob[:, t % 2, :], aux[:, (t % 2) * S:(t % 2 + 1) * S], ACT.Exp,
                                         bias=stat_b[:, t % 2, 0:1], scale=SCORE_SCALE,
                                         accum_out=stat_b[:, t % 2, 1:2]), exp_done)

                def turned(t):
                    act.wait_ge(t_done, t + 1)
                    if t >= 2 and t % 2 == 0:
                        act.wait_ge(pv_done, t // 2)
                    link(act.activation(pt_hi[:, :, (t % 2) * P:(t % 2 + 1) * P],
                                         pair[0][:, :].rearrange("p (k q) -> p k q", k=QT),
                                         ACT.Copy), pt_hi_ready)

                for i in range(QT):
                    exponentials(h * QT + i)
                    if i >= 1:
                        turned(h * QT + i - 1)
                turned(h * QT + QT - 1)
            split_y("y2", stage_c, op_hi, KT, KT // 2)
            norm_squares(2, xc, sq_c, 2, KT, False)
            norm_rstd(2, rstd_c)
            norm_squares(3, xc, sq_c, 2, 2 * KT, False)
            act.wait_ge(x_done, 3 * KT)
            norm_rstd(3, rstd_c)
            act.wait_ge(unit_done, BASE[4])
            split_norm(2 * KT, stage_c, op_hi)

            act.wait_ge(op_ready, OP0["in"] + KT)
            act.wait_ge(x_stored, 32 * KT)
            act.wait_ge(pads_ready, 1)

            def conv_silu(t):
                act.wait_ge(conv_done, t + 1)
                link(act.activation(c_rows[:, t, :], conv_acc[:, t % 2, 0:S], ACT.Silu), c_ready)

            for t in range(KT):
                u = BASE[4] + t
                wait_job(act, u)
                link(act.activation(u_rows[:, t, 2:2 + S], pair[u % 2][:, :], ACT.Copy), u_ready)
                signal(pair_free[u % 2])
                if t >= 1:
                    conv_silu(t - 1)
            conv_silu(KT - 1)
            for g in range(4):
                for i in range(2):
                    n = 2 * g + i
                    u = BASE[4] + 8 + 4 * g + i
                    wait_job(act, u)
                    if n >= 1:
                        act.wait_ge(pooled_ready, n)
                    link(act.activation(pool_pad[:, PAD:PAD + S], pair[u % 2][:, :], ACT.Copy), px_ready)
                    signal(pair_free[u % 2])
                    if n == 1:
                        act.wait_ge(gate_done, 1)
                        act.wait_ge(consts_d, 80)
                        link(act.activation(gate_rows[:, :], aux[0:16, 2 * HALF:4 * HALF], ACT.Identity,
                                             bias=gb_sb[:, :]), gate_ready)
                for i in range(2):
                    n = 2 * g + i
                    u = BASE[4] + 10 + 4 * g + i
                    wait_job(act, u)
                    if n >= 1:
                        act.wait_ge(y_made, Y0["y3"] + n)
                    link(act.activation(sz_p[:, :], pair[u % 2][:, :], ACT.Silu), szp_ready)
                    signal(pair_free[u % 2])
            for t in range(KT):
                u = BASE[4] + 24 + t
                wait_job(act, u)
                if t < 2:
                    act.wait_ge(y_stored[t], 16 * (Y0["y3"] // 2 + KT // 2))
                else:
                    act.wait_ge(mz_stored[t % 2], 16 * (t // 2))
                link(act.activation(y_d[:, t % 2, :], pair[u % 2][:, :], ACT.Silu), mz_ready)
                signal(pair_free[u % 2])

            act.wait_ge(rows_in, 16 * 5)
            act.wait_ge(rows_clear, 4)
            link(act.activation(t_row[:, :], f_row[:, :], ACT.Abs))
            link(act.activation(t_row[:, :], t_row[:, :], ACT.Exp, scale=-1.0))
            link(act.activation(t_row[:, :], t_row[:, :], ACT.Ln, bias=ones[0:36, 0:1]), row_act)

            def back(row):
                return row[:, ::-1]

            d0, d1 = slice(0, MH), slice(32, 32 + MH)
            act.wait_ge(row_dve, 1)
            link(act.activation(b_row[d0, :], t_row[d0, :], ACT.Exp, scale=-1.0))
            link(act.activation(b_row[d1, :], back(t_row[d1, :]), ACT.Exp, scale=-1.0))
            link(act.activation(dec_row[d0, :], dec_tmp[d0, :], ACT.Exp))
            link(act.activation(dec_row[d1, :], back(dec_tmp[d1, :]), ACT.Exp))
            act.wait_ge(row_dve, 2)
            link(act.activation(t_row[d0, :], f_row[d0, :], ACT.Exp))
            link(act.activation(t_row[d1, :], back(f_row[d1, :]), ACT.Exp))
            act.wait_ge(row_dve, 3)
            link(act.activation(f_row[d0, :], i_row[d0, :], ACT.Exp))
            link(act.activation(f_row[d1, :], back(i_row[d1, :]), ACT.Exp), g_made)

            for h in range(MH):
                for m, dst in enumerate((q_t[:, 0, :], k_t[:, 0, :],
                                         k_tok[:, 0:4, :].rearrange("p c d -> p (c d)"), v_tok[:, 0:4, 0:MD])):
                    act.wait_ge(prep_done, 8 * h + 2 * m + 1)
                    src = pair[0][:, :] if m < 3 else pair[0][:, :].rearrange("p (c d) -> p c d", c=4)
                    link(act.activation(dst, src, ACT.Copy), prep_act)

                def decayed(n, d):
                    g = NDIR * (CH * h + n) + d
                    c = n if d == 0 else CH - 1 - n
                    if n == 0:
                        act.wait_ge(bm_ready, h + 1)
                        act.wait_ge(gt_ready, 1)
                    if g >= 2:
                        act.wait_ge(wt_ready, g - 1)
                    r = MH * d + h
                    link(act.activation(e_w[:, d, :], bm_b[:, d, c * P:(c + 1) * P], ACT.Exp,
                                         bias=g_tok[:, c, r:r + 1]), e_ready)

                for d in range(NDIR):
                    decayed(0, d)
                for n in range(CH):
                    for d in range(NDIR):
                        g = NDIR * (CH * h + n) + d
                        act.wait_ge(ab_done, g + 1)
                        if g >= 2:
                            act.wait_ge(h_done, g - 1)
                        link(act.activation(num_a[:, d, :], pair[0][:, d * HALF:d * HALF + VE],
                                             ACT.Copy), acp_ready)
                        if n + 1 < CH:
                            decayed(n + 1, d)
                act.wait_ge(bn_ready, h + 1)
                if h >= 1:
                    act.wait_ge(ln_done, h)
                link(act.activation(rstd_h[:, :], bn2[:, :, 1], ACT.Ln, bias=eps_col[:, :]))
                link(act.activation(rstd_h[:, :], rstd_h[:, :], ACT.Exp, scale=-0.5), rh_ready)

            act.wait_ge(y_made, Y0["y3"] + 2 * KT)
            split_y("y3", stage_f, o_hi, 2 * KT, KT)
            norm_squares(4, xf, sq_f, 1, 3 * KT, False)
            norm_rstd(4, rstd_f)

        @block.vector
        def _(dve):
            link, signal = linker(dve, dve_step)

            def low_part(lo, full, hi, done):
                link(dve.tensor_tensor(lo, full, hi, ALU.subtract), done)

            def norm_apply(n, x, stage, rstd, gain, hn0, op0):
                dve.wait_ge(rstd_ready, n + 1)
                for k in range(KT + 1):
                    if k < KT:
                        link(dve.scalar_tensor_tensor(out=stage[:, k % 2, :], in0=x[:, k, :], scalar=col(gain, k),
                                               in1=rstd[:, :], op0=ALU.mult, op1=ALU.mult), hn_ready)
                    if k >= 1:
                        low(k - 1, stage, op0)

            def low(k, stage, op0, hi=None, lo=None):
                dve.wait_ge(hi_ready, op0 + k + 1)
                low_part((op_lo if lo is None else lo)[:, k, :], stage[:, k % 2, :],
                         (op_hi if hi is None else hi)[:, k, :], op_ready)

            def free(unit_no):
                signal(pair_free[job_of(unit_no) % 2])

            link(dve.memset(ones[:, :], 1.0), ready0)
            link(dve.memset(eps_col[:, :], EPS), ready0)
            link(dve.memset(u_pad[:, 0:1], 0.0))
            link(dve.memset(u_pad[:, S + 1:S + 2], 0.0))
            dve.wait_ge(consts, 64)

            norm_apply(0, xa, stage_a, rstd_a, "norm_even", 0, 0)
            R2 = float(np.sqrt(0.5))
            for j in range(AB):
                dve.wait_ge(bu_ready, j + 1)
                link(dve.tensor_tensor(fold[:, 0:4, :], bu[:, 0:4, :], bu[:, 4:8, :], ALU.add))
                link(dve.tensor_tensor(fold[:, 4:8, :], bu[:, 0:4, :], bu[:, 4:8, :], ALU.subtract))
                if j >= 1:
                    dve.wait_ge(fft1_done, j)
                link(dve.tensor_tensor(bu[:, 0:2, :], fold[:, 0:2, :], fold[:, 2:4, :], ALU.add))
                link(dve.tensor_tensor(parts[:, 4:6, :], fold[:, 0:2, :], fold[:, 2:4, :], ALU.subtract))
                link(dve.tensor_tensor(bu[:, 2, :], fold[:, 5, :], fold[:, 7, :], ALU.subtract))
                link(dve.tensor_tensor(bu[:, 3, :], fold[:, 5, :], fold[:, 7, :], ALU.add))
                link(dve.tensor_tensor(parts[:, 0, :], bu[:, 0, :], bu[:, 1, :], ALU.add))
                link(dve.tensor_tensor(parts[:, 1, :], bu[:, 0, :], bu[:, 1, :], ALU.subtract))

                def combine(dst, a, scale, b, op, done=None):
                    link(dve.scalar_tensor_tensor(out=dst, in0=a, scalar=scale, in1=b, op0=ALU.mult, op1=op), done)

                combine(parts[:, 2, :], bu[:, 2, :], R2, fold[:, 4, :], ALU.add)
                combine(parts[:, 3, :], bu[:, 3, :], R2, fold[:, 6, :], ALU.add)
                combine(parts[:, 6, :], bu[:, 2, :], -R2, fold[:, 4, :], ALU.add)
                combine(parts[:, 7, :], bu[:, 3, :], R2, fold[:, 6, :], ALU.subtract, parts_ready)
                u = 6 * j + 2
                wait_job(dve, u)
                dve.wait_ge(ax_ready, j + 1)
                link(dve.tensor_tensor(u_pad[:, 1:S + 1], pair[u % 2][:, :], ax_sb[:, :], ALU.mult), prod_done)
                dve.wait_ge(prod_done, j + 1)
                free(u)
                link(dve.tensor_scalar(cv[:, :], u_pad[:, 0:S], col("conv_w", 3 * j), None, ALU.mult))
                for tap in (1, 2):
                    link(dve.scalar_tensor_tensor(out=cv[:, :], in0=u_pad[:, tap:tap + S],
                                                scalar=col("conv_w", 3 * j + tap), in1=cv[:, :],
                                                op0=ALU.mult, op1=ALU.add))
                dve.wait_ge(fft2_done, j + 1)
                dve.wait_ge(szb_ready, j + 1)
                if j >= 1:
                    dve.wait_ge(y_stored[0], 16 * j)
                link(dve.tensor_tensor(y_a[:, 0, :].rearrange("p (k2 k1) -> p k1 k2", k1=RADIX),
                                aux[:, 0:S].rearrange("p (k1 k2) -> p k1 k2", k1=RADIX),
                                sz_b[:, :].rearrange("p (k2 k1) -> p k1 k2", k1=RADIX),
                                ALU.mult), y_made)
                u = 6 * j + 4
                wait_job(dve, u)
                link(dve.tensor_tensor(cv[:, :], pair[u % 2][:, :], cv[:, :], ALU.mult))
                free(u)
                dve.wait_ge(sza_ready, j + 1)
                if j >= 1:
                    dve.wait_ge(y_stored[1], 16 * j)
                link(dve.tensor_tensor(y_a[:, 1, :], cv[:, :], sz_a[:, :], ALU.mult), y_made)
            for k in range(KT):
                low(k, stage_a, OP0["y1"])

            def add_residual(unit0, x, count0, jobs=None):
                for k in range(KT):
                    job = unit0 + k
                    wait_job(dve, job)
                    link(dve.tensor_tensor(x[:, k, :], pair[job % 2][:, :], x[:, k, :], ALU.add), x_done)
                    signal(pair_free[job % 2])

            add_residual(BASE[1], xa, 0)
            norm_apply(1, xa, stage_a, rstd_a, "norm_odd", KT, OP0["odd"])

            dve.wait_ge(x_stored, 16 * KT)
            dve.wait_ge(op_ready, OP0["odd"] + KT)
            dve.wait_ge(consts, 80)

            def q_prepare(i, unit_no, gain, dst_hi, dst_lo, slot):
                dve.wait_ge(qrstd, i + 1)
                link(dve.scalar_tensor_tensor(out=qn[:, :], in0=pair[unit_no % 2][:, :], scalar=col(gain),
                                       in1=rstd_b[:, :], op0=ALU.mult, op1=ALU.mult), qn_ready)
                signal(pair_free[unit_no % 2])
                link(dve.tensor_tensor(sq_b[:, :], qn[:, :], rope_sb[:, 0, :], ALU.mult))
                dve.wait_ge(rot_ready, 2 * i + 2)
                link(dve.tensor_tensor(rstd_b[:, :], rstd_b[:, :], rope_sb[:, 1, :], ALU.mult))
                link(dve.tensor_tensor(qn[:, :], sq_b[:, :], rstd_b[:, :], ALU.add), qr_ready)
                dve.wait_ge(qhi_ready, i + 1)
                low_part(dst_lo[:, slot, :], qn[:, :], dst_hi[:, slot, :], q_ready)

            for g in range(KV_HEADS):
                q_prepare(g, BASE[2] + 2 * g, "k_gain", k_hi, k_lo, g)
                dve.wait_ge(vhi_ready, g + 1)
                low_part(v_lo[:, g, :, :].rearrange("p a b -> p (a b)"), aux[:, 2 * HALF:4 * HALF],
                         v_hi[:, g, :, :].rearrange("p a b -> p (a b)"), v_ready)
            q_prepare(KV_HEADS, BASE[2] + 5, "q_gain", q_hi, q_lo, 0)
            for h in range(HEADS):
                if h + 1 < HEADS:
                    q_prepare(KV_HEADS + h + 1, BASE[2] + 7 + 2 * h, "q_gain", q_hi, q_lo, (h + 1) % 2)

                def maxima(t):
                    dve.wait_ge(s_done, t + 1)
                    if t >= 2:
                        dve.wait_ge(exp_done, t - 1)
                    link(dve.reduce_max(stat_b[:, t % 2, 2:3], aux[:, (t % 2) * S:(t % 2 + 1) * S], AX.X))
                    link(dve.tensor_scalar(stat_b[:, t % 2, 0:1], stat_b[:, t % 2, 2:3], -SCORE_SCALE, None,
                                    ALU.mult), neg_ready)

                def normalise(t):
                    dve.wait_ge(exp_done, t + 1)
                    link(dve.reciprocal(stat_b[:, t % 2, 3:4], stat_b[:, t % 2, 1:2]))
                    link(dve.tensor_scalar(prob[:, t % 2, :], prob[:, t % 2, :], stat_b[:, t % 2, 3:4], None,
                                    ALU.mult), p_ready)

                def turned_low(t):
                    dve.wait_ge(pt_hi_ready, t + 1)
                    cols = slice((t % 2) * P, (t % 2 + 1) * P)
                    low_part(pt_lo[:, :, cols], pair[0][:, :].rearrange("p (k q) -> p k q", k=QT),
                             pt_hi[:, :, cols], pt_ready)

                def gate_values(m):
                    n = h * 4 + m
                    dve.wait_ge(pv_done, n + 1)
                    if m == 0:
                        dve.wait_ge(szq_ready, h + 1)
                        if h >= 2:
                            dve.wait_ge(y_stored[h % 2], 16 * (Y0["y2"] // 2 + h // 2))
                    cols = slice(m * 2 * P, (m + 1) * 2 * P)
                    link(dve.tensor_tensor(y_b[:, h % 2, cols], pair[1][:, (n % 2) * HALF:(n % 2) * HALF + 2 * P],
                                    sz_q[:, h % 2, cols], ALU.mult), yq_done)
                    if m == 3:
                        signal(y_made)

                t0 = h * QT
                maxima(t0)
                for i in range(QT):
                    normalise(t0 + i)
                    if i + 1 < QT:
                        maxima(t0 + i + 1)
                    if i >= 1:
                        turned_low(t0 + i - 1)
                    if i >= 3 and i % 2:
                        gate_values(i // 2 - 1)
                turned_low(t0 + QT - 1)
                gate_values(3)
            for k in range(KT):
                low(k, stage_c, OP0["y2"])
            for k in range(KT):
                dve.wait_ge(x_loaded[k], 32)
            add_residual(BASE[3], xc, KT)
            dve.wait_ge(rstd_ready, 3)
            for k in range(KT):
                link(dve.scalar_tensor_tensor(out=xc[:, k, :], in0=xc[:, k, :], scalar=col("final_norm", k),
                                       in1=rstd_c[:, :], op0=ALU.mult, op1=ALU.mult), x_done)
            norm_apply(3, xc, stage_c, rstd_c, "norm_in", 2 * KT, OP0["in"])

            dve.wait_ge(op_ready, OP0["in"] + KT)
            dve.wait_ge(x_stored, 32 * KT)
            for t in range(KT):
                link(dve.memset(u_rows[:, t, 0:2], 0.0))
                link(dve.memset(u_rows[:, t, 2 + S:4 + S], 0.0))
            link(dve.memset(pool_pad[:, 0:PAD], 0.0))
            link(dve.memset(pool_pad[:, PAD + S:2 * PAD + S], 0.0), pads_ready)
            dve.wait_ge(consts_d, 80)

            def block_diagonal(dst, blocks, mask, done=None):
                link(dve.tensor_tensor(dst.rearrange("p (m o) -> p m o", o=4),
                                       blocks.unsqueeze(1).broadcast_to([P, 32, 4]),
                                       mask[:, :].unsqueeze(2).broadcast_to([P, 32, 4]), ALU.mult), done)

            for i in range(3 * KT):
                if i >= 2:
                    dve.wait_ge(weff_done, i - 1)
                block_diagonal(bdt[:, i % 2, :], blocks_d[:, i % 3, i // 3, :], bmask_d, bdt_ready)
            dve.wait_ge(weff_done, 3 * KT)
            link(dve.tensor_copy(gw_eff[:, :, :].rearrange("p a b -> p (a b)"), aux[:, 0:2 * KT * 16]), weff_ready)
            for t in range(KT):
                dve.wait_ge(u_ready, t + 1)
                if t >= 2:
                    dve.wait_ge(c_ready, t - 1)
                acc = conv_acc[:, t % 2, 0:S]
                link(dve.tensor_scalar(acc, u_rows[:, t, 0:S], col("conv_w2", TAPS2 * t), col("conv_b2", t),
                                     ALU.mult, ALU.add))
                for tap in range(1, TAPS2):
                    link(dve.scalar_tensor_tensor(out=acc, in0=u_rows[:, t, tap:tap + S],
                                                 scalar=col("conv_w2", TAPS2 * t + tap), in1=acc,
                                                 op0=ALU.mult, op1=ALU.add))
                signal(conv_done)
            dve.wait_ge(c_ready, KT)
            for g, w in enumerate(WINDOWS):
                left = (w - 1) // 2
                right = w - 1 - left
                for i in range(2):
                    n = 2 * g + i
                    dve.wait_ge(px_ready, n + 1)
                    src, length, span, b = pool_pad[:, :], S + 2 * PAD, 1, 0
                    while span < w:
                        length -= span
                        dst = conv_acc[:, b, 0:length]
                        link(dve.tensor_tensor(dst, src[:, 0:length], src[:, span:span + length], ALU.add))
                        src, b, span = conv_acc[:, b, :], 1 - b, 2 * span
                    total = src[:, PAD - left:PAD - left + S]
                    if left:
                        link(dve.tensor_tensor(total[:, 0:left], total[:, 0:left], edge_sb[:, g, 0, 0:left], ALU.mult))
                    link(dve.tensor_tensor(total[:, S - right:S], total[:, S - right:S],
                                         edge_sb[:, g, 1, PAD - right:PAD], ALU.mult))
                    if g >= 1:
                        dve.wait_ge(mix_done, 2 * g)
                    link(dve.scalar_tensor_tensor(out=pooled[:, i, :], in0=total, scalar=1.0 / w,
                                           in1=pool_pad[:, PAD:PAD + S], op0=ALU.mult,
                                           op1=ALU.subtract), pooled_ready)
                for i in range(2):
                    n = 2 * g + i
                    dve.wait_ge(mix_done, n + 1)
                    dve.wait_ge(szp_ready, n + 1)
                    if n >= 2:
                        dve.wait_ge(y_stored[n % 2], 16 * (Y0["y3"] // 2 + n // 2))
                    link(dve.scalar_tensor_tensor(out=y_d[:, n % 2, :], in0=aux[:, 0:S], scalar=col("pool_scale", n),
                                           in1=sz_p[:, :], op0=ALU.mult, op1=ALU.mult), y_made)

            dve.wait_ge(y_stored[0], 16 * (Y0["y3"] // 2 + KT // 2))
            dve.wait_ge(y_stored[1], 16 * (Y0["y3"] // 2 + KT // 2))
            dve.wait_ge(gate_stored, 16)
            dve.wait_ge(mz_stored[0], 16 * KT // 2)
            dve.wait_ge(mz_stored[1], 16 * KT // 2)
            dve.wait_ge(unit_done, BASE[5])
            link(dve.memset(i_row[:, :], 0.0), rows_clear)
            link(dve.memset(f_row[:, :], 0.0), rows_clear)
            link(dve.memset(mp_row[:, :], 0.0), rows_clear)
            link(dve.memset(v_tok[:, :, MD:VE], 1.0), rows_clear)
            dve.wait_ge(consts_e, 48)
            for i in range(3 * KT):
                block_diagonal(bd[:, i // KT, i % KT, :], blocks_e[:, i // KT, i % KT, :], bmask_e)
            ks = bd[:, 1, :, :].rearrange("p a b -> p (a b)")
            link(dve.tensor_scalar(ks, ks, float(MD) ** -0.5, None, ALU.mult), bd_ready)
            d0, d1 = slice(0, MH), slice(32, 32 + MH)
            dve.wait_ge(row_act, 1)
            dve.wait_ge(rows_in, 16 * 5)
            link(dve.scalar_tensor_tensor(out=f_row[:, :], in0=f_row[:, :], scalar=0.0, in1=t_row[:, :],
                                        op0=ALU.min, op1=ALU.subtract))
            link(dve.tensor_copy(b_row[d1, :], i_row[d1, ::-1]))
            link(dve.tensor_copy(a_row[d1, :], f_row[d1, ::-1]))
            link(dve.tensor_copy(i_row[d1, :], b_row[d1, :]))
            link(dve.tensor_copy(f_row[d1, :], a_row[d1, :]))
            link(dve.tensor_tensor_scan(b_row[:, :], reset_row[:, :], f_row[:, :], 0.0, ALU.mult, ALU.add))
            link(dve.tensor_tensor_scan(t_row[:, :], f_row[:, :], i_row[:, :], 0.0, ALU.add, ALU.max))
            link(dve.tensor_tensor(f_row[:, :], b_row[:, :], t_row[:, :], ALU.subtract))
            link(dve.tensor_tensor(i_row[:, :], i_row[:, :], b_row[:, :], ALU.subtract))
            link(dve.tensor_copy(mp_row[:, 1:CH], t_row[:, P - 1:S - P:P]))
            link(dve.tensor_copy(end_row[:, :], f_row[:, P - 1:S:P]))
            link(dve.tensor_tensor(dec_tmp[:, :], end_row[:, :], mp_row[:, :], ALU.add))
            link(dve.tensor_copy(reset_row[d0, :], f_row[d0, :]))
            link(dve.tensor_copy(reset_row[d1, :], f_row[d1, ::-1]))
            link(dve.tensor_copy(a_row[d0, :], i_row[d0, :]))
            link(dve.tensor_copy(a_row[d1, :], i_row[d1, ::-1]))
            signal(bm_made)
            signal(row_dve)

            def by_chunk(row):
                return row[:, :].rearrange("p (c s) -> p c s", c=CH)

            link(dve.tensor_tensor(by_chunk(f_row), by_chunk(f_row),
                                 mp_row[:, :].unsqueeze(2).broadcast_to([36, CH, P]), ALU.add))
            signal(row_dve)
            link(dve.tensor_tensor(by_chunk(i_row), by_chunk(i_row),
                                 end_row[:, :].unsqueeze(2).broadcast_to([36, CH, P]), ALU.add))
            signal(row_dve)
            dve.wait_ge(gt_done, 1)
            link(dve.tensor_copy(g_tok[:, :, :].rearrange("p a b -> p (a b)"), aux[:, 0:CH * 32]), gt_ready)
            dve.wait_ge(decay_in, 16)

            for h in range(MH):
                for m, dst in enumerate((q_t[:, 1, :], k_t[:, 1, :],
                                         k_tok[:, 4:8, :].rearrange("p c d -> p (c d)"), v_tok[:, 4:8, 0:MD])):
                    dve.wait_ge(prep_done, 8 * h + 2 * m + 2)
                    src = pair[1][:, :] if m < 3 else pair[1][:, :].rearrange("p (c d) -> p c d", c=4)
                    link(dve.tensor_copy(dst, src), prep_dve)
                dve.wait_ge(bm_loaded, 32 * (h + 1))
                for d in range(NDIR):
                    link(dve.tensor_tensor(by_chunk(bm_b[:, d, :]), by_chunk(bm_b[:, d, :]),
                                          mask_sb[:, d, :].unsqueeze(1).broadcast_to([P, CH, P]), ALU.add))
                signal(bm_ready)
                dve.wait_ge(prep_act, 4 * h + 4)
                dve.wait_ge(st_done, h + 1)

                def weights(n, d):
                    g = NDIR * (CH * h + n) + d
                    ks = NDIR * ((CH - 1) * h + n) + d
                    c = n if d == 0 else CH - 1 - n
                    dve.wait_ge(e_ready, g + 1)
                    if g >= 2:
                        dve.wait_ge(ab_done, g - 1)
                    link(dve.tensor_tensor(w_t[:, d, :], aux[:, c * P:(c + 1) * P], e_w[:, d, :],
                                    ALU.mult), wt_ready)
                    if n < CH - 1:
                        if ks >= 2:
                            dve.wait_ge(upd_done, ks - 1)
                        r = 16 + MH * d + h
                        link(dve.tensor_scalar(k_w[:, d, :], k_tok[:, c, :], g_tok[:, c, r:r + 1], None,
                                        ALU.mult), kw_ready)

                def finish(n, d):
                    g = NDIR * (CH * h + n) + d
                    ks = NDIR * ((CH - 1) * h + n) + d
                    c = n if d == 0 else CH - 1 - n
                    r = MH * d + h
                    if n < CH - 1:
                        dve.wait_ge(upd_done, ks + 1)
                        upd = aux[:, 2 * HALF:4 * HALF].rearrange("p (i e) -> p i e", i=2)[:, :, 0:VE]
                        if n == 0:
                            link(dve.tensor_copy(state[:, d, :, :], upd), state_ready)
                        else:
                            link(dve.scalar_tensor_tensor(out=state[:, d, :, :], in0=state[:, d, :, :],
                                                   scalar=decay_b[:, r, c:c + 1], in1=upd,
                                                   op0=ALU.mult, op1=ALU.add), state_ready)
                    dve.wait_ge(acp_ready, g + 1)
                    num = num_a[:, d, :]
                    if n >= 1:
                        dve.wait_ge(ab_done, g + 1)
                        link(dve.scalar_tensor_tensor(out=num_b[:, d, :], in0=pair[1][:, d * HALF:d * HALF + VE],
                                                    scalar=g_tok[:, c, 8 + r:9 + r], in1=num_a[:, d, :],
                                                    op0=ALU.mult, op1=ALU.add))
                        num = num_b[:, d, :]
                    link(dve.tensor_scalar(small[:, d, 2:3], num[:, MD:VE], -1.0, g_tok[:, c, 24 + r:25 + r],
                                         ALU.mult, ALU.max))
                    link(dve.tensor_tensor(small[:, d, 0:1], small[:, d, 2:3], num[:, MD:VE], ALU.max))
                    link(dve.reciprocal(small[:, d, 1:2], small[:, d, 0:1]))
                    if n < CH // 2:
                        link(dve.tensor_scalar(h_tok[:, c, :], num[:, 0:MD], small[:, d, 1:2], None,
                                        ALU.mult), h_done)
                    else:
                        link(dve.scalar_tensor_tensor(out=h_tok[:, c, :], in0=num[:, 0:MD], scalar=small[:, d, 1:2],
                                               in1=h_tok[:, c, :], op0=ALU.mult, op1=ALU.add), h_done)

                order = [(n, d) for n in range(CH) for d in range(NDIR)]
                weights(*order[0])
                for m in range(len(order)):
                    if m + 1 < len(order):
                        weights(*order[m + 1])
                    finish(*order[m])
                dve.wait_ge(h_done, NDIR * CH * (h + 1))
                for c in range(CH):
                    link(dve.bn_stats(bn6[:, c, :], h_tok[:, c, :]))
                for c in range(CH):
                    link(dve.bn_aggr(bn2[:, c, :], bn6[:, c, :]))
                signal(bn_ready)
                dve.wait_ge(rh_ready, h + 1)
                for c in range(CH):
                    link(dve.tensor_scalar(h_tok[:, c, :], h_tok[:, c, :], bn2[:, c, 0:1], rstd_h[:, c:c + 1],
                                          ALU.subtract, ALU.mult))
                signal(ln_done)
                for i in range(2):
                    n = 2 * h + i
                    if h >= 1:
                        dve.wait_ge(y_stored[i], 16 * ((Y0["y3"] + KT) // 2 + h))
                    link(dve.tensor_scalar(out_e[:, i, :], c_rows[:, n, :], col("skip", n), None, ALU.mult))
                    dve.wait_ge(ht_done, n + 1)
                    link(dve.scalar_tensor_tensor(out=out_e[:, i, :], in0=pair[i][:, :], scalar=col("mh_norm", n),
                                                in1=out_e[:, i, :], op0=ALU.mult, op1=ALU.add))
                    dve.wait_ge(mz_in[i], 16 * (h + 1))
                    link(dve.tensor_tensor(out_e[:, i, :], out_e[:, i, :], mz_sb[:, i, :], ALU.mult), y_made)

            for k in range(2 * KT):
                low(k, stage_f, OP0["y3"], o_hi, o_lo)
            for k in range(KT):
                dve.wait_ge(x_loaded[k], 48)
            add_residual(BASE[5], xf, 3 * KT)
            dve.wait_ge(rstd_ready, 5)
            for k in range(KT):
                if k >= 2:
                    dve.wait_ge(out_stored[k % 2], 16 * (k // 2))
                link(dve.scalar_tensor_tensor(out=stage_f[:, k % 2, :], in0=xf[:, k, :], scalar=col("norm_out", k),
                                       in1=rstd_f[:, :], op0=ALU.mult, op1=ALU.mult), out_made)


def _tables():
    f = np.float32
    n = np.arange(P)
    ang = 2 * np.pi * np.outer(n, n) / P
    scale = 1.0 / np.sqrt(S * P)
    c, s = np.cos(ang) * scale, np.sin(ang) * scale
    dft_d = np.stack([np.concatenate([c, s], 1), np.concatenate([-s, c], 1), np.concatenate([s, -c], 1)], 1)
    k = np.arange(S).reshape(P, RADIX).T
    phase = 2 * np.pi * (n[:, None, None] * k[None]) / S
    dft_s = np.stack([np.cos(phase), -np.sin(phase)], 1)
    pairs = P // 4
    inv = (f(10000.0) ** (-np.arange(pairs, dtype=f) / f(pairs))).astype(f)
    t = np.arange(S)
    row, colm = (t // 64).astype(f), (t % 64).astype(f)
    a = np.concatenate([row[None] * inv[:, None], colm[None] * inv[:, None]], 0).astype(f).astype(np.float64)
    cs, sn = np.cos(a), np.sin(a)
    rope = np.stack([np.concatenate([cs, cs]), np.concatenate([-sn, sn])], 1)
    edge = np.ones((4, 2, PAD))
    for g, w in enumerate(WINDOWS):
        left = (w - 1) // 2
        right = w - 1 - left
        for t_ in range(left):
            edge[g, 0, t_] = w / (t_ + right + 1)
        for j in range(right):
            edge[g, 1, PAD - right + j] = w / (left + 1 + right - 1 - j)
    i = np.arange(P)
    masks = np.stack([np.where(i[:, None] <= i[None], 0.0, NEG), np.where(i[:, None] >= i[None], 0.0, NEG)], 1)
    block_mask = (i[:, None] // 4 == np.arange(32)[None]).astype(f)
    reset = np.ones((36, S))
    reset[:, ::P] = 0.0
    return {"ident_in": np.eye(P), "dft_d": dft_d, "dft_s": dft_s, "rope": rope,
            "edge": np.broadcast_to(edge, (P, 4, 2, PAD)), "masks": masks, "block_mask": block_mask,
            "reset_mask": reset}


def _units(w, blocks):
    out = []
    for b in blocks:
        cols, k0 = b if isinstance(b, tuple) else (b, 0)
        part = w[k0 * P:(k0 + KT) * P][:, cols]
        out.append(part.reshape(KT, P, P).transpose(1, 0, 2).reshape(P, KT * P))
    return out


def kernel(**inputs):
    import concourse.bacc as _bacc
    from concourse.bass_utils import run_bass_kernel_spmd as _run

    a = {k: np.asarray(v) for k, v in inputs.items()}

    def cols(b):
        return np.arange(b * P, (b + 1) * P)

    pair_order = np.concatenate([np.arange(0, P, 2), np.arange(1, P, 2)])
    units = []
    for j in range(AB):
        units += _units(a["w_in_even"][0], [cols(b) for b in (16 + j, j, 8 + j, 20 + j, 4 + j, 12 + j)])
    units += _units(a["w_out_even"][0], [cols(e) for e in range(KT)])
    w = a["w_in_odd"][0]
    for g in range(KV_HEADS):
        units += _units(w, [cols(HEADS + g)[pair_order], cols(HEADS + KV_HEADS + g)])
    for h in range(HEADS):
        units += _units(w, [cols(HEADS + 2 * KV_HEADS + h), cols(h)[pair_order]])
    units += _units(a["w_out_odd"][0], [cols(e) for e in range(KT)])
    w = a["w_in_2"][0]
    units += _units(w, [cols(16 + t) for t in range(KT)])
    for g in range(4):
        units += _units(w, [cols(b) for b in (2 * g, 2 * g + 1, 8 + 2 * g, 9 + 2 * g)])
    units += _units(w, [cols(24 + t) for t in range(KT)])
    units += _units(a["w_out_2"][0], [(cols(e), KT * i) for e in range(KT) for i in range(2)])

    def by_block(v):
        return v.reshape(-1, P).T

    def taps(v):
        return v.reshape(v.shape[0], -1, P).transpose(2, 1, 0).reshape(P, -1)

    params = {"norm_even": by_block(a["norm_even"][0]), "conv_w": taps(a["conv_w"][0]),
              "norm_odd": by_block(a["norm_odd"][0]), "final_norm": by_block(a["final_norm"]),
              "norm_in": by_block(a["norm_in_g_2"][0]), "norm_out": by_block(a["norm_out_g_2"]),
              "q_gain": a["q_gain"][0][pair_order][:, None], "k_gain": a["k_gain"][0][pair_order][:, None],
              "pool_scale": by_block(a["pool_scale_2"][0]), "conv_w2": taps(a["conv_w_2"][0]),
              "conv_b2": by_block(a["conv_b_2"][0]), "mh_norm": by_block(a["mh_norm_w_2"][0]),
              "skip": by_block(a["skip_w_2"][0])}
    qkv = np.stack([a[k][0] for k in ("w_q_2", "w_k_2", "w_v_2")]).reshape(3, KT, 32, 4, 4)
    straight = qkv.reshape(3, KT, P, 4).transpose(2, 0, 1, 3)
    turned = qkv.transpose(0, 1, 2, 4, 3).reshape(3, KT, P, 4).transpose(2, 0, 1, 3)
    gw = a["w_gates_2"][0].reshape(NDIR, 3 * KT, P, 2, MH).transpose(2, 1, 3, 0, 4).reshape(P, 3 * KT, 16)
    gb = a["b_gates_2"][0].reshape(NDIR, 2, MH).transpose(1, 0, 2).reshape(16, 1)
    arrays = {"x_t": a["x"][0].T.reshape(KT, P, S), "weight_units": np.stack(units),
              "channel_params": np.concatenate([params[k] for k in PARAMS], 1),
              "qkv_blocks": np.stack([straight, turned]), "gate_w": gw, "gate_b": gb,
              "pool_w": a["pool_w_2"][0].reshape(4, 2, P, MD).transpose(0, 2, 1, 3)}
    arrays.update({k: v.astype(np.float32) for k, v in _tables().items()})
    arrays = {k: np.ascontiguousarray(v) for k, v in arrays.items()}

    nc = _bacc.Bacc("TRN2", target_bir_lowering=False, num_devices=1)
    args = {k: nc.dram_tensor(k, v.shape, mybir.dt.from_np(v.dtype), kind="ExternalInput").ap()
            for k, v in arrays.items()}
    out = nc.dram_tensor("out", [KT, P, S], F32, kind="ExternalOutput").ap()
    build(nc, out=out, **args)
    r = _run(nc, [arrays], core_ids=[0])
    return r.results[0]["out"].reshape(D, S).T.reshape(1, S, D)
```

```python
from contextlib import ExitStack

import numpy as np
import concourse.bass as bass
from concourse import mybir

P = 128
S = 1024
D = 1024
KT = D // P
HALF = 512
EPS = 1e-6
F32 = mybir.dt.float32
F32R = mybir.dt.float32r
ALU = mybir.AluOpType
ACT = mybir.ActivationFunctionType
AX = mybir.AxisListType

AB = 4
RADIX = 8
HEADS, KV_HEADS = 8, 2
GROUP = HEADS // KV_HEADS
QT = S // P
SCORE_SCALE = float(P) ** -0.5
WINDOWS = (2, 4, 8, 16)
PAD = 8
MH = 4
MD = 256
VE = MD + 1
CH = S // P
NDIR = 2
TAPS2 = 5
NEG = -1e30

EVEN_IN, EVEN_OUT, ODD_IN, ODD_OUT, SEC_IN, SEC_OUT = 24, 8, 20, 8, 32, 16
BASE = np.cumsum([0, EVEN_IN, EVEN_OUT, ODD_IN, ODD_OUT, SEC_IN, SEC_OUT]).tolist()
UNITS = BASE[-1]

PARAMS = {}
_at = 0
for _name, _n in (("norm_even", 8), ("conv_w", 12), ("norm_odd", 8), ("final_norm", 8), ("norm_in", 8),
                  ("norm_out", 8), ("q_gain", 2), ("k_gain", 2), ("pool_scale", 8), ("conv_w2", 40),
                  ("conv_b2", 8), ("mh_norm", 8), ("skip", 8)):
    PARAMS[_name] = _at
    _at += _n
N_PARAMS = _at



def linker(eng, step):
    count = {}

    def link(instruction, semaphore=None):
        semaphore = step if semaphore is None else semaphore
        instruction.then_inc(semaphore, 1)
        count[id(semaphore)] = count.get(id(semaphore), 0) + 1
        eng.wait_ge(semaphore, count[id(semaphore)])

    def signal(semaphore):
        eng.sem_inc(semaphore, 1)
        count[id(semaphore)] = count.get(id(semaphore), 0) + 1

    return link, signal


def build(nc, x_t, weight_units, channel_params, ident_in, dft_d, dft_s, rope, edge, masks, block_mask,
          qkv_blocks, gate_w, gate_b, pool_w, reset_mask, out):
    ctx = ExitStack()
    with ctx:
        def sem(name):
            return ctx.enter_context(nc.semaphore(name))

        def dram(name, shape):
            return nc.dram_tensor(name, shape, F32).ap()

        x1_dram = dram("x1_dram", [KT, P, S])
        x2_dram = dram("x2_dram", [KT, P, S])
        y1_dram = dram("y1_dram", [KT, P, S])
        y2_dram = dram("y2_dram", [KT, P, S])
        y3_dram = dram("y3_dram", [2 * KT, P, S])
        mz_dram = dram("mz_dram", [KT, P, S])
        gate_dram = dram("gate_dram", [16, S])
        bm_dram = dram("bm_dram", [2 * MH, S])
        decay_dram = dram("decay_dram", [2 * MH, CH])

        at = [-(-nc.sbuf_base // 32) * 32]

        def keep(name, shape, dt=F32):
            tensor = nc.alloc_sbuf_tensor_at(name, shape, dt, offset=at[0])
            size = 4
            for n in shape[1:]:
                size *= n
            at[0] += -(-size // 32) * 32
            assert at[0] <= nc.sbuf_usable_end, name
            return tensor


        par = keep("par", [P, N_PARAMS])
        ident = keep("ident", [P, P])
        ones = keep("ones", [P, P])
        eps_col = keep("eps_col", [P, 1])
        w_raw = keep("w_raw", [P, 3, KT * P])
        w_hi = keep("w_hi", [P, 2, KT * P], F32R)
        w_lo = keep("w_lo", [P, 2, KT * P], F32R)

        def col(name, i=0):
            return par[:, PARAMS[name] + i:PARAMS[name] + i + 1]

        op_start = at[0]
        op_hi = keep("op_hi", [P, KT, S], F32R)
        op_lo = keep("op_lo", [P, KT, S], F32R)
        phase_start = at[0]
        xa = keep("xa", [P, KT, S])
        stage_a = keep("stage_a", [P, 2, S])
        sq_a = keep("sq_a", [P, 2, S])
        rstd_a = keep("rstd_a", [P, S])
        y_a = keep("y_a", [P, 2, S])
        tab_d = keep("tab_d", [P, 3, 2 * P])
        tab_s = keep("tab_s", [P, 2, RADIX, P])
        spec = keep("spec", [P, RADIX, 2 * P])
        parts = keep("parts", [P, RADIX, P])
        fold = keep("fold", [P, RADIX, P])
        bu = keep("bu", [P, RADIX, P])
        ax_sb = keep("ax_sb", [P, S])
        u_pad = keep("u_pad", [P, S + 2])
        cv = keep("cv", [P, S])
        sz_a = keep("sz_a", [P, S])
        sz_b = keep("sz_b", [P, S])
        at[0] = phase_start
        q_hi = keep("q_hi", [P, 2, S], F32R)
        q_lo = keep("q_lo", [P, 2, S], F32R)
        k_hi = keep("k_hi", [P, KV_HEADS, S], F32R)
        k_lo = keep("k_lo", [P, KV_HEADS, S], F32R)
        v_hi = keep("v_hi", [P, KV_HEADS, QT, P], F32R)
        v_lo = keep("v_lo", [P, KV_HEADS, QT, P], F32R)
        pt_hi = keep("pt_hi", [P, QT, 2 * P], F32R)
        pt_lo = keep("pt_lo", [P, QT, 2 * P], F32R)
        prob = keep("prob", [P, 2, S])
        rope_sb = keep("rope_sb", [P, 2, S])
        sz_q = keep("sz_q", [P, 2, S])
        q_raw = keep("q_raw", [P, 2, S])
        sq_b = keep("sq_b", [P, S])
        rstd_b = keep("rstd_b", [P, S])
        y_b = keep("y_b", [P, 2, S])
        stat_b = keep("stat_b", [P, 2, 4])
        at[0] = phase_start
        xc = keep("xc", [P, KT, S])
        stage_c = keep("stage_c", [P, 2, S])
        sq_c = keep("sq_c", [P, 2, S])
        rstd_c = keep("rstd_c", [P, S])
        at[0] = phase_start
        u_rows = keep("u_rows", [P, KT, S + 4])
        c_rows = keep("c_rows", [P, KT, S])
        conv_acc = keep("conv_acc", [P, 2, S + 2 * PAD])
        pool_pad = keep("pool_pad", [P, S + 2 * PAD])
        pooled = keep("pooled", [P, 2, S])
        sz_p = keep("sz_p", [P, S])
        y_d = keep("y_d", [P, 2, S])
        pw_sb = keep("pw_sb", [P, 2, 2, MD])
        gw_sb = keep("gw_sb", [P, 3 * KT, 16])
        gw_eff = keep("gw_eff", [P, 2 * KT, 16])
        blocks_d = keep("blocks_d", [P, 3, KT, 4])
        bmask_d = keep("bmask_d", [P, 32])
        bdt = keep("bdt", [P, 2, P])
        edge_sb = keep("edge_sb", [P, 4, 2, PAD])
        gate_rows = keep("gate_rows", [16, S])
        gb_sb = keep("gb_sb", [16, 1])
        at[0] = op_start
        q_t = keep("q_t", [P, 2, S])
        k_t = keep("k_t", [P, 2, S])
        k_tok = keep("k_tok", [P, CH, MD])
        v_tok = keep("v_tok", [P, CH, VE])
        h_tok = keep("h_tok", [P, CH, MD])
        bm_b = keep("bm_b", [P, NDIR, S])
        state = keep("state", [P, NDIR, 2, VE])
        e_w = keep("e_w", [P, NDIR, P])
        w_t = keep("w_t", [P, NDIR, P])
        num_a = keep("num_a", [P, NDIR, VE])
        num_b = keep("num_b", [P, NDIR, VE])
        k_w = keep("k_w", [P, NDIR, MD])
        assert at[0] <= phase_start
        at[0] = phase_start + 4 * KT * (2 * S + 4)
        bd = keep("bd", [P, 3, KT, P])
        blocks_e = keep("blocks_e", [P, 3, KT, 4])
        bmask_e = keep("bmask_e", [P, 32])
        mask_sb = keep("mask_sb", [P, NDIR, P])
        g_tok = keep("g_tok", [P, CH, 32])
        decay_b = keep("decay_b", [P, 2 * MH, CH])
        small = keep("small", [P, NDIR, 4])
        bn6 = keep("bn6", [P, CH, 6])
        bn2 = keep("bn2", [P, CH, 2])
        rstd_h = keep("rstd_h", [P, CH])
        rows_start = at[0]
        i_row = keep("i_row", [36, S])
        f_row = keep("f_row", [36, S])
        t_row = keep("t_row", [36, S])
        b_row = keep("b_row", [36, S])
        reset_row = keep("reset_row", [36, S])
        a_row = keep("a_row", [36, S])
        g_rows = keep("g_rows", [32, S])
        mp_row = keep("mp_row", [36, CH])
        end_row = keep("end_row", [36, CH])
        dec_tmp = keep("dec_tmp", [36, CH])
        dec_row = keep("dec_row", [36, CH])
        at[0] = rows_start
        out_e = keep("out_e", [P, 2, S])
        mz_sb = keep("mz_sb", [P, 2, S])
        at[0] = op_start
        o_hi = keep("o_hi", [P, 2 * KT, S], F32R)
        o_lo = keep("o_lo", [P, 2 * KT, S], F32R)
        xf = keep("xf", [P, KT, S])
        stage_f = keep("stage_f", [P, 2, S])
        sq_f = keep("sq_f", [P, 1, S])
        rstd_f = keep("rstd_f", [P, S])

        pair = [ctx.enter_context(nc.psum_tensor(f"pair{i}", [P, S], F32)) for i in range(2)]
        aux = ctx.enter_context(nc.psum_tensor("aux", [P, 4 * HALF], F32))

        consts = sem("consts")
        ready0 = sem("ready0")
        w_loaded = [sem(f"w_loaded{i}") for i in range(3)]
        w_hi_done = sem("w_hi_done")
        w_split = sem("w_split")
        unit_done = sem("unit_done")
        pair_free = [sem(f"pair_free{i}") for i in range(2)]
        x_loaded = [sem(f"x_loaded{i}") for i in range(KT)]
        x_done = sem("x_done")
        sq_ready, stat_done, rstd_ready = sem("sq_ready"), sem("stat_done"), sem("rstd_ready")
        hn_ready, hi_ready, op_ready = sem("hn_ready"), sem("hi_ready"), sem("op_ready")
        x_stored = sem("x_stored")
        y_in = [sem(f"y_in{i}") for i in range(2)]
        y_made = sem("y_made")
        y_stored = [sem(f"y_stored{i}") for i in range(2)]
        dve_step, act_step = sem("dve_step"), sem("act_step")
        bu_ready, parts_ready, fft1_done = sem("bu_ready"), sem("parts_ready"), sem("fft1_done")
        spec_ready, fft2_done = sem("spec_ready"), sem("fft2_done")
        ax_ready, prod_done, szb_ready, sza_ready = sem("ax_ready"), sem("prod_done"), sem("szb_ready"), sem("sza_ready")
        qsq, qstat, qrstd, qr_ready = sem("qsq"), sem("qstat"), sem("qrstd"), sem("qr_ready")
        raw_ready = sem("raw_ready")
        qhi_ready, q_ready = sem("qhi_ready"), sem("q_ready")
        bg_done, bg_free = sem("bg_done"), sem("bg_free")
        vt_ready, vtr_done, vhi_ready, v_ready = sem("vt_ready"), sem("vtr_done"), sem("vhi_ready"), sem("v_ready")
        szq_ready, s_done, neg_ready, exp_done = sem("szq_ready"), sem("s_done"), sem("neg_ready"), sem("exp_done")
        p_ready, t_done, pt_hi_ready, pt_ready = sem("p_ready"), sem("t_done"), sem("pt_hi_ready"), sem("pt_ready")
        pv_done, yq_done = sem("pv_done"), sem("yq_done")
        consts_d, pads_ready = sem("consts_d"), sem("pads_ready")
        bdt_ready, weff_done, weff_ready = sem("bdt_ready"), sem("weff_done"), sem("weff_ready")
        u_ready, conv_done, c_ready, gate_done, gate_ready, gate_stored = (
            sem("u_ready"), sem("conv_done"), sem("c_ready"), sem("gate_done"), sem("gate_ready"), sem("gate_stored"))
        px_ready, pooled_ready, mix_done, szp_ready = sem("px_ready"), sem("pooled_ready"), sem("mix_done"), sem("szp_ready")
        pw_loaded = [sem(f"pw_loaded{i}") for i in range(2)]
        mz_ready = sem("mz_ready")
        mz_stored = [sem(f"mz_stored{i}") for i in range(2)]
        consts_e, rows_in = sem("consts_e"), sem("rows_in")
        rows_clear, bm_made, row_act, row_dve = sem("rows_clear"), sem("bm_made"), sem("row_act"), sem("row_dve")
        g_made, g_moved, decay_in = sem("g_made"), sem("g_moved"), sem("decay_in")
        gt_done, gt_ready, bd_ready = sem("gt_done"), sem("gt_ready"), sem("bd_ready")
        bm_loaded, bm_ready = sem("bm_loaded"), sem("bm_ready")
        prep_done, prep_act, prep_dve = sem("prep_done"), sem("prep_act"), sem("prep_dve")
        st_done, e_ready, wt_ready, ab_done = sem("st_done"), sem("e_ready"), sem("wt_ready"), sem("ab_done")
        kw_ready, upd_done, state_ready, acp_ready, h_done = (
            sem("kw_ready"), sem("upd_done"), sem("state_ready"), sem("acp_ready"), sem("h_done"))
        bn_ready, rh_ready, ln_done, ht_done = sem("bn_ready"), sem("rh_ready"), sem("ln_done"), sem("ht_done")
        mz_in = [sem(f"mz_in{i}") for i in range(2)]
        out_made, out_stored = sem("out_made"), [sem(f"out_stored{i}") for i in range(2)]

        JOBS = BASE[5] + KT

        def job_of(unit):
            return unit if unit < BASE[5] else BASE[5] + (unit - BASE[5]) // 2

        def last_unit(job):
            return job if job < BASE[5] else BASE[5] + 2 * (job - BASE[5]) + 1

        def wait_job(eng, job):
            eng.wait_ge(unit_done, last_unit(job) + 1)

        OP0 = {"even": 0, "y1": KT, "odd": 2 * KT, "y2": 3 * KT, "in": 4 * KT, "y3": 5 * KT}
        UNIT0 = {"even": BASE[0], "y1": BASE[1], "odd": BASE[2], "y2": BASE[3], "in": BASE[4], "y3": BASE[5]}
        Y0 = {"y1": 0, "y2": KT, "y3": 2 * KT}

        Y_ORDER = {"y1": [b for j in range(AB) for b in (AB + j, j)],
                   "y2": list(range(HEADS)),
                   "y3": list(range(2 * KT))}
        Y_DRAM = {"y1": y1_dram, "y2": y2_dram, "y3": y3_dram}

        block = ctx.enter_context(nc.Block())

        @block.sync
        def _(sp):
            loaded = [0]

            def weights_to(n):
                for u in range(loaded[0], min(n, UNITS)):
                    if u >= 3:
                        sp.wait_ge(w_split, u - 2)
                    sp.dma_start(w_raw[:, u % 3, :], weight_units[u]).then_inc(w_loaded[u % 3], 16)
                loaded[0] = max(loaded[0], n)

            def store_y(layer, n, buf):
                sp.wait_ge(y_made, Y0[layer] + n + 1)
                sp.dma_start(Y_DRAM[layer][Y_ORDER[layer][n]], buf[:, n % 2, :]).then_inc(
                    y_stored[n % 2], 16)

            def load_y(layer, k, buf):
                n = Y_ORDER[layer].index(k)
                sp.wait_ge(y_stored[n % 2], 16 * (Y0[layer] // 2 + n // 2 + 1))
                if k >= 2:
                    sp.wait_ge(op_ready, OP0[layer] + k - 1)
                sp.dma_start(buf[:, k % 2, :], Y_DRAM[layer][k]).then_inc(y_in[k % 2], 16)

            sp.dma_start(ident[:, :], ident_in).then_inc(consts, 16)
            sp.dma_start(par[:, :], channel_params).then_inc(consts, 16)
            for k in range(KT):
                sp.dma_start(xa[:, k, :], x_t[k]).then_inc(x_loaded[k], 16)
            weights_to(2)
            sp.dma_start(tab_d[:, :, :], dft_d).then_inc(consts, 16)
            sp.dma_start(tab_s[:, :, :, :], dft_s).then_inc(consts, 16)
            for j in range(AB):
                weights_to(6 * j + 9)
                store_y("y1", 2 * j, y_a)
                store_y("y1", 2 * j + 1, y_a)
            for k in range(KT):
                load_y("y1", k, stage_a)
            weights_to(BASE[2] + 3)
            for k in range(KT):
                sp.wait_ge(x_done, k + 1)
                sp.dma_start(x1_dram[k], xa[:, k, :]).then_inc(x_stored, 16)
            sp.wait_ge(op_ready, OP0["odd"] + KT)
            sp.wait_ge(x_stored, 16 * KT)
            sp.dma_start(rope_sb[:, :, :], rope).then_inc(consts, 16)
            for h in range(HEADS):
                weights_to(min(BASE[2] + 11 + 2 * h, BASE[3] + 3))
                store_y("y2", h, y_b)
                if h == HEADS - 2:
                    sp.wait_ge(q_ready, KV_HEADS + 2 * HEADS)
                    for k in range(KT - 1):
                        load_y("y2", k, q_raw)
                    sp.wait_ge(s_done, QT * HEADS)
                    for k in range(KT):
                        sp.dma_start(xc[:, k, :], x1_dram[k]).then_inc(x_loaded[k], 16)
            weights_to(BASE[4] + 3)
            for k in range(KT):
                sp.wait_ge(x_done, 2 * KT + k + 1)
                sp.dma_start(x2_dram[k], xc[:, k, :]).then_inc(x_stored, 16)
            sp.wait_ge(op_ready, OP0["in"] + KT)
            sp.wait_ge(x_stored, 32 * KT)
            sp.dma_start(blocks_d[:, :, :, :], qkv_blocks[1]).then_inc(consts_d, 16)
            sp.dma_start(bmask_d[:, :], block_mask).then_inc(consts_d, 16)
            sp.dma_start(gw_sb[:, :, :], gate_w).then_inc(consts_d, 16)
            sp.dma_start(gb_sb[:, :], gate_b).then_inc(consts_d, 16)
            sp.dma_start(edge_sb[:, :, :, :], edge).then_inc(consts_d, 16)
            for g in range(2):
                sp.dma_start(pw_sb[:, g, :, :], pool_w[g]).then_inc(pw_loaded[g], 16)
            for g in range(4):
                weights_to(BASE[4] + 15 + 4 * g)
                store_y("y3", 2 * g, y_d)
                store_y("y3", 2 * g + 1, y_d)
                if g + 2 < 4:
                    sp.dma_start(pw_sb[:, g % 2, :, :], pool_w[g + 2]).then_inc(pw_loaded[g % 2], 16)
                if g == 1:
                    sp.wait_ge(gate_ready, 1)
                    sp.dma_start(gate_dram[:, :], gate_rows[:, :]).then_inc(gate_stored, 16)
            for t in range(KT):
                weights_to(min(BASE[4] + 28 + t, BASE[5] + 3))
                sp.wait_ge(mz_ready, t + 1)
                sp.dma_start(mz_dram[t], y_d[:, t % 2, :]).then_inc(mz_stored[t % 2], 16)
            sp.wait_ge(mz_stored[0], 16 * KT // 2)
            sp.wait_ge(mz_stored[1], 16 * KT // 2)
            sp.wait_ge(gate_stored, 16)
            sp.dma_start(blocks_e[:, :, :, :], qkv_blocks[0]).then_inc(consts_e, 16)
            sp.dma_start(bmask_e[:, :], block_mask).then_inc(consts_e, 16)
            sp.dma_start(mask_sb[:, :, :], masks).then_inc(consts_e, 16)
            sp.wait_ge(rows_clear, 2)
            for d in range(NDIR):
                sp.dma_start(i_row[32 * d:32 * d + MH, :],
                             gate_dram[MH * d:MH * d + MH, :]).then_inc(rows_in, 16)
                sp.dma_start(f_row[32 * d:32 * d + MH, :],
                             gate_dram[8 + MH * d:8 + MH * d + MH, :]).then_inc(rows_in, 16)
            sp.dma_start(reset_row[:, :], reset_mask).then_inc(rows_in, 16)
            sp.wait_ge(bm_made, 1)
            for d in range(NDIR):
                sp.dma_start(bm_dram[MH * d:MH * d + MH, :],
                             reset_row[32 * d:32 * d + MH, :]).then_inc(g_moved, 16)
            sp.wait_ge(g_made, 1)
            for d in range(NDIR):
                for n, row in enumerate((a_row, t_row, f_row, b_row)):
                    sp.dma_start(g_rows[8 * n + MH * d:8 * n + MH * d + MH, :],
                                 row[32 * d:32 * d + MH, :]).then_inc(g_moved, 16)
                sp.dma_start(decay_dram[MH * d:MH * d + MH, :],
                             dec_row[32 * d:32 * d + MH, :]).then_inc(g_moved, 16)
            sp.wait_ge(g_moved, 16 * 12)
            sp.dma_start(decay_b[:, :, :].rearrange("p r c -> p (r c)"),
                         decay_dram.rearrange("r c -> (r c)").rearrange("(a n) -> a n", a=1)
                         .broadcast_to([P, 2 * MH * CH])).then_inc(decay_in, 16)
            for h in range(MH):
                if h >= 1:
                    sp.wait_ge(e_ready, NDIR * CH * h)
                for d in range(NDIR):
                    sp.dma_start(bm_b[:, d, :], bm_dram[MH * d + h:MH * d + h + 1, :]
                                 .broadcast_to([P, S])).then_inc(bm_loaded, 16)
                for t in range(2):
                    if h >= 1:
                        sp.wait_ge(y_made, Y0["y3"] + KT + 2 * h + t - 1)
                    else:
                        sp.wait_ge(gt_ready, 1)
                    sp.dma_start(mz_sb[:, t, :], mz_dram[2 * h + t]).then_inc(mz_in[t], 16)
                for t in range(2):
                    store_y("y3", KT + 2 * h + t, out_e)
            sp.wait_ge(y_stored[0], 16 * (Y0["y3"] // 2 + KT))
            sp.wait_ge(y_stored[1], 16 * (Y0["y3"] // 2 + KT))
            for k in range(KT):
                sp.dma_start(xf[:, k, :], x2_dram[k]).then_inc(x_loaded[k], 16)
            for k in range(2 * KT):
                load_y("y3", k, stage_f)
            weights_to(UNITS)
            for k in range(KT):
                sp.wait_ge(out_made, k + 1)
                sp.dma_start(out[k], stage_f[:, k % 2, :]).then_inc(out_stored[k % 2], 16)
            sp.wait_ge(out_stored[0], 16 * KT // 2)
            sp.wait_ge(out_stored[1], 16 * KT // 2)

        @block.gpsimd
        def _(pool):
            for u in range(UNITS):
                pool.wait_ge(w_loaded[u % 3], 16 * (u // 3 + 1))
                if u >= 2:
                    pool.wait_ge(unit_done, u - 1)
                    pool.wait_ge(w_split, u - 1)
                pool.tensor_copy(w_hi[:, u % 2, :], w_raw[:, u % 3, :]).then_inc(w_hi_done, 1)
                pool.wait_ge(w_hi_done, u + 1)
                pool.tensor_tensor(w_lo[:, u % 2, :], w_raw[:, u % 3, :], w_hi[:, u % 2, :],
                                   ALU.subtract).then_inc(w_split, 1)

        @block.tensor
        def _(pe):
            def unit(u, job, hi, lo, layer, kt0=0, wait_operand=False, first=True, last=True):
                pe.wait_ge(w_split, u + 1)
                if first and job >= 2:
                    pe.wait_ge(pair_free[job % 2], job // 2)
                acc = pair[job % 2]
                for k in range(KT):
                    if wait_operand:
                        pe.wait_ge(op_ready, OP0[layer] + kt0 + k + 1)
                    wh = w_hi[:, u % 2, k * P:(k + 1) * P]
                    wl = w_lo[:, u % 2, k * P:(k + 1) * P]
                    for n, (w, x) in enumerate(((wh, hi), (wh, lo), (wl, hi))):
                        for half in range(2):
                            cols = slice(half * HALF, (half + 1) * HALF)
                            mm = pe.matmul(acc[:, cols], w, x[:, kt0 + k, cols],
                                           start=(first and k == 0 and n == 0),
                                           stop=(last and k == KT - 1 and n == 2))
                mm.then_inc(unit_done, 1)

            def norm_stats(n, sq, bufs):
                for k in range(KT):
                    pe.wait_ge(sq_ready, KT * n + k + 1)
                    for half in range(2):
                        cols = slice(half * HALF, (half + 1) * HALF)
                        mm = pe.matmul(aux[:, cols], ones[:, :], sq[:, k % bufs, cols],
                                       start=(k == 0), stop=(k == KT - 1))
                    mm.then_inc(stat_done, 1)

            pe.wait_ge(consts, 64)
            pe.wait_ge(ready0, 2)
            norm_stats(0, sq_a, 2)

            def fft_channels(j):
                pe.wait_ge(parts_ready, j + 1)
                if j == 0:
                    pe.wait_ge(rstd_ready, 1)
                else:
                    pe.wait_ge(y_made, 2 * j - 1)
                for k1 in range(RADIX):
                    o = aux[:, k1 * 2 * P:(k1 + 1) * 2 * P]
                    if k1 % 4 == 0:
                        mm = pe.matmul(o, parts[:, k1 // 4, :], tab_d[:, 0, :], start=True, stop=True)
                    else:
                        r = min(k1, RADIX - k1)
                        pe.matmul(o, parts[:, 2 * r, :], tab_d[:, 0, :], start=True, stop=False)
                        mm = pe.matmul(o, parts[:, 2 * r + 1, :], tab_d[:, 1 if k1 < 4 else 2, :],
                                       start=False, stop=True)
                mm.then_inc(fft1_done, 1)

            def fft_time(j):
                pe.wait_ge(spec_ready, j + 1)
                for k1 in range(RADIX):
                    o = aux[:, k1 * P:(k1 + 1) * P]
                    pe.matmul(o, spec[:, k1, 0:P], tab_s[:, 0, k1, :], start=True, stop=False)
                    mm = pe.matmul(o, spec[:, k1, P:2 * P], tab_s[:, 1, k1, :], start=False, stop=True)
                mm.then_inc(fft2_done, 1)

            for j in range(AB):
                for i in range(6):
                    u = 6 * j + i
                    unit(u, u, op_hi, op_lo, "even", wait_operand=(u == 0))
                    if i == 1:
                        fft_channels(j)
                    if i == 2:
                        fft_time(j)
            for e in range(KT):
                unit(BASE[1] + e, BASE[1] + e, op_hi, op_lo, "y1", wait_operand=(e == 0))
            norm_stats(1, sq_a, 2)

            def v_transpose(g):
                pe.wait_ge(vt_ready, g + 1)
                if g >= 1:
                    pe.wait_ge(v_ready, g)
                for t in range(QT):
                    mm = pe.transpose(aux[:, 2 * HALF + t * P:2 * HALF + (t + 1) * P],
                                      prob[:, g, t * P:(t + 1) * P], ident[:, :])
                mm.then_inc(vtr_done, 1)

            for g in range(KV_HEADS):
                unit(BASE[2] + 2 * g, BASE[2] + 2 * g, op_hi, op_lo, "odd", wait_operand=(g == 0))
                unit(BASE[2] + 2 * g + 1, BASE[2] + 2 * g + 1, op_hi, op_lo, "odd")
                pe.wait_ge(qsq, g + 1)
                if g == 0:
                    pe.wait_ge(rstd_ready, 2)
                else:
                    pe.wait_ge(qrstd, g)
                for half in range(2):
                    cols = slice(half * HALF, (half + 1) * HALF)
                    mm = pe.matmul(aux[:, cols], ones[:, :], sq_b[:, cols], start=True, stop=True)
                mm.then_inc(qstat, 1)
                v_transpose(g)

            bank = pair[1][:, 0:HALF]

            def piece(h, which, c, part):
                u = BASE[2] + 4 + 2 * h + which
                cols = slice(c * HALF, (c + 1) * HALF)
                if part == 0:
                    pe.wait_ge(w_split, u + 1)
                    n = 6 * h + (2 * c if which == 0 else 4 + c)
                    if n >= 1:
                        pe.wait_ge(bg_free, n)
                for k in range(4 * part, 4 * part + 4):
                    wh = w_hi[:, u % 2, k * P:(k + 1) * P]
                    wl = w_lo[:, u % 2, k * P:(k + 1) * P]
                    for n, (w, x) in enumerate(((wh, op_hi), (wh, op_lo), (wl, op_hi))):
                        mm = pe.matmul(bank, w, x[:, k, cols], start=(k == 0 and n == 0),
                                       stop=(k == KT - 1 and n == 2))
                if part == 1:
                    mm.then_inc(bg_done if c == 0 else unit_done, 1)

            def q_stats(h, c):
                pe.wait_ge(qsq, KV_HEADS + 2 * h + c + 1)
                pe.wait_ge(bg_free, 6 * h + 2 * c + 1)
                pe.matmul(bank, ones[:, :], sq_b[:, c * HALF:(c + 1) * HALF],
                          start=True, stop=True).then_inc(qstat, 1)

            def scores(t):
                h, i = t // QT, t % QT
                if i == 0:
                    pe.wait_ge(q_ready, KV_HEADS + 2 * h + 2)
                    pe.wait_ge(v_ready, KV_HEADS)
                if t >= 2:
                    pe.wait_ge(exp_done, t - 1)
                b = (t % 2) * S
                g = h // GROUP
                rows = slice(i * P, (i + 1) * P)
                for n, (a, k) in enumerate(((q_hi, k_hi), (q_hi, k_lo), (q_lo, k_hi))):
                    for half in range(2):
                        cols = slice(half * HALF, (half + 1) * HALF)
                        mm = pe.matmul(aux[:, b + half * HALF:b + (half + 1) * HALF],
                                       a[:, h % 2, rows], k[:, g, cols],
                                       start=(n == 0), stop=(n == 2))
                mm.then_inc(s_done, 1)

            def turn(t):
                pe.wait_ge(p_ready, t + 1)
                if t >= 1:
                    pe.wait_ge(pt_ready, t)
                else:
                    pe.wait_ge(pair_free[0], (BASE[2] + 4) // 2)
                for k in range(QT):
                    mm = pe.transpose(pair[0][:, k * P:(k + 1) * P],
                                      prob[:, t % 2, k * P:(k + 1) * P], ident[:, :])
                mm.then_inc(t_done, 1)

            def weigh_values(m):
                pe.wait_ge(pt_ready, 2 * m + 2)
                if m >= 1:
                    pe.wait_ge(yq_done, m)
                g = m // 4 // GROUP
                for k in range(QT):
                    for n, (v, p) in enumerate(((v_hi, pt_hi), (v_hi, pt_lo), (v_lo, pt_hi))):
                        mm = pe.matmul(pair[1][:, HALF:HALF + 2 * P], v[:, g, k, :], p[:, k, :],
                                       start=(k == 0 and n == 0), stop=(k == QT - 1 and n == 2))
                mm.then_inc(pv_done, 1)

            pe.wait_ge(pair_free[1], (BASE[2] + 4) // 2)
            for c in range(2):
                piece(0, 0, c, 0)
                piece(0, 0, c, 1)
                q_stats(0, c)
            piece(0, 1, 0, 0)
            piece(0, 1, 0, 1)
            scores(0)
            scores(1)
            piece(0, 1, 1, 0)
            piece(0, 1, 1, 1)
            for t in range(QT * HEADS):
                h, i = t // QT, t % QT
                turn(t)
                if h + 1 < HEADS and i in (2, 4):
                    q_stats(h + 1, i // 2 - 1)
                if t + 2 < QT * HEADS:
                    scores(t + 2)
                if h + 1 < HEADS:
                    piece(h + 1, i // 4, i // 2 % 2, i % 2)
                if i % 2:
                    weigh_values(t // 2)
            pe.wait_ge(pt_ready, QT * HEADS)
            pe.wait_ge(yq_done, 4 * HEADS)
            for e in range(KT):
                unit(BASE[3] + e, BASE[3] + e, op_hi, op_lo, "y2", wait_operand=(e == 0))
            norm_stats(2, sq_c, 2)
            pe.wait_ge(rstd_ready, 3)
            norm_stats(3, sq_c, 2)

            for i in range(3 * KT):
                t, which = i // 3, i % 3
                pe.wait_ge(bdt_ready, i + 1)
                if i == 0:
                    pe.wait_ge(rstd_ready, 4)
                pos = (t if which < 2 else KT + t) * 16
                mm = pe.matmul(aux[:, pos:pos + 16], bdt[:, i % 2, :], gw_sb[:, which * KT + t, :],
                               start=(which != 1), stop=(which != 0))
                mm.then_inc(weff_done, 1)

            def gates(t):
                for half in range(2):
                    cols = slice(half * HALF, (half + 1) * HALF)
                    o = aux[0:16, 2 * HALF + half * HALF:2 * HALF + (half + 1) * HALF]
                    pe.wait_ge(weff_ready, 1)
                    pe.wait_ge(u_ready, t + 1)
                    pe.matmul(o, gw_eff[:, KT + t, :], u_rows[:, t, 2 + half * HALF:2 + (half + 1) * HALF],
                              start=(t == 0), stop=False)
                    pe.wait_ge(c_ready, t + 1)
                    mm = pe.matmul(o, gw_eff[:, t, :], c_rows[:, t, cols], start=False, stop=(t == KT - 1))
                if t == KT - 1:
                    mm.then_inc(gate_done, 1)

            for t in range(KT):
                unit(BASE[4] + t, BASE[4] + t, op_hi, op_lo, "in", wait_operand=(t == 0))
                if t >= 1:
                    gates(t - 1)
            for g in range(4):
                for i in range(4):
                    unit(BASE[4] + 8 + 4 * g + i, BASE[4] + 8 + 4 * g + i, op_hi, op_lo, "in")
                    if g == 0 and i == 0:
                        gates(KT - 1)
                    if i >= 2:
                        m = i - 2
                        pe.wait_ge(pooled_ready, 2 * g + 2)
                        pe.wait_ge(pw_loaded[g % 2], 16 * (g // 2 + 1))
                        if 2 * g + m >= 1:
                            pe.wait_ge(y_made, Y0["y3"] + 2 * g + m)
                        for half in range(2):
                            cols = slice(half * HALF, (half + 1) * HALF)
                            for k in range(2):
                                mm = pe.matmul(aux[:, cols], pw_sb[:, g % 2, k, m * P:(m + 1) * P],
                                               pooled[:, k, cols], start=(k == 0), stop=(k == 1))
                        mm.then_inc(mix_done, 1)
            for t in range(KT):
                unit(BASE[4] + 24 + t, BASE[4] + 24 + t, op_hi, op_lo, "in")

            pe.wait_ge(g_moved, 16 * 12)
            for c in range(CH):
                mm = pe.transpose(aux[:, c * 32:(c + 1) * 32], g_rows[:, c * P:(c + 1) * P], ident[0:32, 0:32])
            mm.then_inc(gt_done, 1)
            pe.wait_ge(bd_ready, 1)
            pe.wait_ge(pair_free[(BASE[5] - 1) % 2], (BASE[5] - 1) // 2 + 1)
            pe.wait_ge(pair_free[(BASE[5] - 2) % 2], (BASE[5] - 2) // 2 + 1)

            def prepare(h):
                def step(n):
                    if n % 2 == 0 and 4 * h + n // 2 >= 1:
                        pe.wait_ge(prep_act, 4 * h + n // 2)
                    if n % 2 and 4 * h + n // 2 >= 1:
                        pe.wait_ge(prep_dve, 4 * h + n // 2)
                if h >= 1:
                    pe.wait_ge(y_made, Y0["y3"] + KT + 2 * h)
                for n in range(4):
                    step(n)
                    i = n % 2
                    for half in range(2):
                        cols = slice(half * HALF, (half + 1) * HALF)
                        mm = pe.matmul(pair[n % 2][:, cols], bd[:, n // 2, 2 * h + i, :],
                                       c_rows[:, 2 * h + i, cols], start=True, stop=True)
                    mm.then_inc(prep_done, 1)
                for n in range(4, 8):
                    step(n)
                    for c in range(4):
                        chunk = 4 * (n % 2) + c
                        for i in range(2):
                            if n < 6:
                                x = c_rows[:, 2 * h + i, chunk * P:(chunk + 1) * P]
                            else:
                                x = u_rows[:, 2 * h + i, 2 + chunk * P:2 + (chunk + 1) * P]
                            mm = pe.matmul(pair[n % 2][:, c * MD + i * P:c * MD + (i + 1) * P], x,
                                           bd[:, 1 if n < 6 else 2, 2 * h + i, :], start=True, stop=True)
                    mm.then_inc(prep_done, 1)

            for h in range(MH):
                prepare(h)
                pe.wait_ge(prep_act, 4 * h + 2)
                pe.wait_ge(prep_dve, 4 * h + 2)
                pe.wait_ge(gt_ready, 1)
                if h >= 1:
                    pe.wait_ge(wt_ready, NDIR * CH * h)
                for c in range(CH):
                    for i in range(2):
                        mm = pe.matmul(aux[:, c * P:(c + 1) * P], k_t[:, i, c * P:(c + 1) * P],
                                       q_t[:, i, c * P:(c + 1) * P], start=(i == 0), stop=(i == 1))
                mm.then_inc(st_done, 1)
                pe.wait_ge(prep_act, 4 * h + 4)
                pe.wait_ge(prep_dve, 4 * h + 4)
                for n in range(CH):
                    for d in range(NDIR):
                        c = n if d == 0 else CH - 1 - n
                        g = NDIR * (CH * h + n) + d
                        ks = NDIR * ((CH - 1) * h + n) + d
                        if n >= 1:
                            pe.wait_ge(h_done, g - 1)
                        pe.wait_ge(wt_ready, g + 1)
                        mm = pe.matmul(pair[0][:, d * HALF:d * HALF + VE], w_t[:, d, :], v_tok[:, c, :],
                                       start=True, stop=True)
                        if n >= 1:
                            pe.wait_ge(state_ready, NDIR * ((CH - 1) * h + n - 1) + d + 1)
                            for i in range(2):
                                mm = pe.matmul(pair[1][:, d * HALF:d * HALF + VE],
                                               q_t[:, i, c * P:(c + 1) * P], state[:, d, i, :],
                                               start=(i == 0), stop=(i == 1))
                        mm.then_inc(ab_done, 1)
                        if n < CH - 1:
                            pe.wait_ge(kw_ready, ks + 1)
                            if ks >= 1:
                                pe.wait_ge(state_ready, ks)
                            for i in range(2):
                                o = aux[:, 2 * HALF + i * HALF:2 * HALF + i * HALF + VE]
                                mm = pe.matmul(o, k_w[:, d, i * P:(i + 1) * P], v_tok[:, c, :],
                                               start=True, stop=True)
                            mm.then_inc(upd_done, 1)
                pe.wait_ge(ln_done, h + 1)
                for i in range(2):
                    for c in range(CH):
                        mm = pe.transpose(pair[i][:, c * P:(c + 1) * P], h_tok[:, c, i * P:(i + 1) * P],
                                          ident[:, :])
                    mm.then_inc(ht_done, 1)

            pe.wait_ge(y_made, Y0["y3"] + 2 * KT)
            for e in range(KT):
                for i in range(2):
                    unit(BASE[5] + 2 * e + i, BASE[5] + e, o_hi, o_lo, "y3", kt0=KT * i,
                         wait_operand=(e == 0), first=(i == 0), last=(i == 1))
            norm_stats(4, sq_f, 1)

        @block.scalar
        def _(act):
            link, signal = linker(act, act_step)

            def norm_squares(n, x, sq, bufs, x0, by_dma):
                for k in range(KT):
                    if by_dma:
                        act.wait_ge(x_loaded[k], 16)
                    else:
                        act.wait_ge(x_done, x0 + k + 1)
                    if k >= bufs:
                        act.wait_ge(stat_done, KT * n + k - bufs + 1)
                    link(act.activation(sq[:, k % bufs, :], x[:, k, :], ACT.Square), sq_ready)


            def norm_rstd(n, rstd):
                act.wait_ge(stat_done, KT * (n + 1))
                link(act.activation(rstd[:, :], aux[:, 0:S], ACT.Ln, bias=eps_col[:, :], scale=1.0 / D))
                link(act.activation(rstd[:, :], rstd[:, :], ACT.Exp, scale=-0.5), rstd_ready)

            his = [0]

            def split_norm(hn0, stage, hi):
                for k in range(KT):
                    act.wait_ge(hn_ready, hn0 + k + 1)
                    link(act.activation(hi[:, k, :], stage[:, k % 2, :], ACT.Copy), hi_ready)
                his[0] += KT

            def split_y(layer, stage, hi, blocks, in0):
                act.wait_ge(unit_done, UNIT0[layer])
                for k in range(blocks):
                    act.wait_ge(y_in[k % 2], 16 * (in0[k % 2] + k // 2 + 1))
                    link(act.activation(hi[:, k, :], stage[:, k % 2, :], ACT.Copy), hi_ready)

            def y_hi(k, stage):
                act.wait_ge(unit_done, BASE[3])
                act.wait_ge(y_in[k % 2], 16 * (KT // 2 + k // 2 + 1))
                link(act.activation(op_hi[:, k, :], stage[:, k % 2, :], ACT.Copy), hi_ready)

            act.wait_ge(ready0, 2)
            norm_squares(0, xa, sq_a, 2, 0, True)
            norm_rstd(0, rstd_a)
            split_norm(0, stage_a, op_hi)
            for j in range(AB):
                u = 6 * j
                wait_job(act, u)
                if j >= 1:
                    act.wait_ge(parts_ready, j)
                link(act.activation(bu[:, :, :].rearrange("p a b -> p (a b)"), pair[u % 2][:, :],
                                     ACT.Copy), bu_ready)
                signal(pair_free[u % 2])
                wait_job(act, u + 1)
                if j >= 1:
                    act.wait_ge(prod_done, j)
                link(act.activation(ax_sb[:, :], pair[(u + 1) % 2][:, :], ACT.Copy), ax_ready)
                signal(pair_free[(u + 1) % 2])
                act.wait_ge(fft1_done, j + 1)
                if j >= 1:
                    act.wait_ge(fft2_done, j)
                link(act.activation(spec[:, :, :].rearrange("p a b -> p (a b)"), aux[:, :],
                                     ACT.Copy), spec_ready)
                wait_job(act, u + 3)
                if j >= 1:
                    act.wait_ge(y_made, 2 * j - 1)
                link(act.activation(sz_b[:, :], pair[(u + 3) % 2][:, :], ACT.Silu), szb_ready)
                signal(pair_free[(u + 3) % 2])
                wait_job(act, u + 5)
                if j >= 1:
                    act.wait_ge(y_made, 2 * j)
                link(act.activation(sz_a[:, :], pair[(u + 5) % 2][:, :], ACT.Silu), sza_ready)
                signal(pair_free[(u + 5) % 2])
            split_y("y1", stage_a, op_hi, KT, (0, 0))
            norm_squares(1, xa, sq_a, 2, 0, False)
            norm_rstd(1, rstd_a)
            act.wait_ge(unit_done, BASE[2])
            split_norm(KT, stage_a, op_hi)

            act.wait_ge(op_ready, OP0["odd"] + KT)
            act.wait_ge(x_stored, 16 * KT)

            def raw(r, src, cols):
                if r >= 1:
                    act.wait_ge(q_ready, min(r, max(KV_HEADS, r - 1)))
                half = P // 2
                link(act.activation(sq_b[:, cols], src, ACT.Square), qsq)
                link(act.activation(q_raw[:, 0, cols], src, ACT.Copy))
                link(act.activation(q_raw[0:half, 1, cols], src[half:P], ACT.Copy))
                link(act.activation(q_raw[half:P, 1, cols], src[0:half], ACT.Copy))
                signal(raw_ready)

            def head_rstd(r, src, cols, freed=None):
                act.wait_ge(qstat, r + 1)
                link(act.activation(rstd_b[:, cols], src, ACT.Ln, bias=eps_col[:, :], scale=1.0 / P))
                if freed is not None:
                    signal(freed)
                link(act.activation(rstd_b[:, cols], rstd_b[:, cols], ACT.Exp, scale=-0.5), qrstd)

            def split_hi(r, dst, cols):
                act.wait_ge(qr_ready, r + 1)
                link(act.activation(dst, q_raw[:, 0, cols], ACT.Copy), qhi_ready)

            whole = slice(0, S)
            for g in range(KV_HEADS):
                u = BASE[2] + 2 * g
                wait_job(act, u)
                raw(g, pair[u % 2][:, :], whole)
                signal(pair_free[u % 2])
                u = BASE[2] + 2 * g + 1
                wait_job(act, u)
                link(act.activation(prob[:, g, :], pair[u % 2][:, :], ACT.Copy), vt_ready)
                signal(pair_free[u % 2])
                head_rstd(g, aux[:, 0:S], whole)
                split_hi(g, k_hi[:, g, :], whole)
                act.wait_ge(vtr_done, g + 1)
                link(act.activation(v_hi[:, g, :, :].rearrange("p a b -> p (a b)"),
                                     aux[:, 2 * HALF:4 * HALF], ACT.Copy), vhi_ready)

            bank = pair[1][:, 0:HALF]

            def columns(c):
                return slice(c * HALF, (c + 1) * HALF)

            def q_raw_half(h, c):
                u = BASE[2] + 4 + 2 * h
                if c == 0:
                    act.wait_ge(bg_done, 2 * h + 1)
                else:
                    act.wait_ge(unit_done, u + 1)
                raw(KV_HEADS + 2 * h + c, bank, columns(c))
                signal(bg_free)
                if c == 1:
                    signal(pair_free[u % 2])

            def q_rstd_half(h, c):
                head_rstd(KV_HEADS + 2 * h + c, bank, columns(c), bg_free)

            def q_hi_half(h, c):
                if h >= 2:
                    act.wait_ge(s_done, QT * (h - 1))
                split_hi(KV_HEADS + 2 * h + c, q_hi[:, h % 2, columns(c)], columns(c))

            def z_half(h, c):
                u = BASE[2] + 5 + 2 * h
                if c == 0:
                    act.wait_ge(bg_done, 2 * h + 2)
                    if h >= 2:
                        act.wait_ge(yq_done, 4 * (h - 1))
                else:
                    act.wait_ge(unit_done, u + 1)
                link(act.activation(sz_q[:, h % 2, columns(c)], bank, ACT.Copy))
                signal(bg_free)
                if c == 1:
                    signal(pair_free[u % 2])

            def gate_silu(h):
                link(act.activation(sz_q[:, h % 2, :], sz_q[:, h % 2, :], ACT.Silu), szq_ready)

            def exponentials(t):
                act.wait_ge(neg_ready, t + 1)
                if t >= 2:
                    act.wait_ge(t_done, t - 1)
                link(act.activation(prob[:, t % 2, :], aux[:, (t % 2) * S:(t % 2 + 1) * S], ACT.Exp,
                                     bias=stat_b[:, t % 2, 0:1], scale=SCORE_SCALE,
                                     accum_out=stat_b[:, t % 2, 1:2]), exp_done)

            def turned(t):
                act.wait_ge(t_done, t + 1)
                if t >= 2:
                    act.wait_ge(pv_done, t // 2)
                link(act.activation(pt_hi[:, :, (t % 2) * P:(t % 2 + 1) * P],
                                     pair[0][:, :].rearrange("p (k q) -> p k q", k=QT),
                                     ACT.Copy), pt_hi_ready)

            for c in range(2):
                q_raw_half(0, c)
                q_rstd_half(0, c)
                q_hi_half(0, c)
            z_half(0, 0)
            exponentials(0)
            exponentials(1)
            z_half(0, 1)
            for t in range(QT * HEADS):
                h, i = t // QT, t % QT
                beside = h + 1 < HEADS
                turned(t)
                if beside and i in (2, 4):
                    q_rstd_half(h + 1, i // 2 - 1)
                if t + 2 < QT * HEADS:
                    exponentials(t + 2)
                if beside and i in (3, 5):
                    q_hi_half(h + 1, i // 2 - 1)
                if beside and i in (1, 3):
                    q_raw_half(h + 1, i // 2)
                if beside and i in (5, 7):
                    z_half(h + 1, i // 2 - 2)
                if i == 0:
                    gate_silu(h)
                if not beside and i >= 1:
                    y_hi(i - 1, q_raw)
            act.wait_ge(y_made, Y0["y2"] + KT)
            link(act.activation(op_hi[:, KT - 1, :], y_b[:, (KT - 1) % 2, :], ACT.Copy), hi_ready)
            norm_squares(2, xc, sq_c, 2, KT, False)
            norm_rstd(2, rstd_c)
            norm_squares(3, xc, sq_c, 2, 2 * KT, False)
            act.wait_ge(x_done, 3 * KT)
            norm_rstd(3, rstd_c)
            act.wait_ge(unit_done, BASE[4])
            split_norm(2 * KT, stage_c, op_hi)

            act.wait_ge(op_ready, OP0["in"] + KT)
            act.wait_ge(x_stored, 32 * KT)
            act.wait_ge(pads_ready, 1)

            def conv_silu(t):
                act.wait_ge(conv_done, t + 1)
                link(act.activation(c_rows[:, t, :], conv_acc[:, t % 2, 0:S], ACT.Silu), c_ready)

            for t in range(KT):
                u = BASE[4] + t
                wait_job(act, u)
                link(act.activation(u_rows[:, t, 2:2 + S], pair[u % 2][:, :], ACT.Copy), u_ready)
                signal(pair_free[u % 2])
                if t >= 1:
                    conv_silu(t - 1)
            conv_silu(KT - 1)
            for g in range(4):
                for i in range(2):
                    n = 2 * g + i
                    u = BASE[4] + 8 + 4 * g + i
                    wait_job(act, u)
                    if n >= 1:
                        act.wait_ge(pooled_ready, n)
                    link(act.activation(pool_pad[:, PAD:PAD + S], pair[u % 2][:, :], ACT.Copy), px_ready)
                    signal(pair_free[u % 2])
                    if n == 1:
                        act.wait_ge(gate_done, 1)
                        act.wait_ge(consts_d, 80)
                        link(act.activation(gate_rows[:, :], aux[0:16, 2 * HALF:4 * HALF], ACT.Identity,
                                             bias=gb_sb[:, :]), gate_ready)
                for i in range(2):
                    n = 2 * g + i
                    u = BASE[4] + 10 + 4 * g + i
                    wait_job(act, u)
                    if n >= 1:
                        act.wait_ge(y_made, Y0["y3"] + n)
                    link(act.activation(sz_p[:, :], pair[u % 2][:, :], ACT.Silu), szp_ready)
                    signal(pair_free[u % 2])
            for t in range(KT):
                u = BASE[4] + 24 + t
                wait_job(act, u)
                if t < 2:
                    act.wait_ge(y_stored[t], 16 * (Y0["y3"] // 2 + KT // 2))
                else:
                    act.wait_ge(mz_stored[t % 2], 16 * (t // 2))
                link(act.activation(y_d[:, t % 2, :], pair[u % 2][:, :], ACT.Silu), mz_ready)
                signal(pair_free[u % 2])

            act.wait_ge(rows_in, 16 * 5)
            act.wait_ge(rows_clear, 4)
            link(act.activation(t_row[:, :], f_row[:, :], ACT.Abs))
            link(act.activation(t_row[:, :], t_row[:, :], ACT.Exp, scale=-1.0))
            link(act.activation(t_row[:, :], t_row[:, :], ACT.Ln, bias=ones[0:36, 0:1]), row_act)

            def back(row):
                return row[:, ::-1]

            d0, d1 = slice(0, MH), slice(32, 32 + MH)
            act.wait_ge(row_dve, 1)
            link(act.activation(b_row[d0, :], t_row[d0, :], ACT.Exp, scale=-1.0))
            link(act.activation(b_row[d1, :], back(t_row[d1, :]), ACT.Exp, scale=-1.0))
            link(act.activation(dec_row[d0, :], dec_tmp[d0, :], ACT.Exp))
            link(act.activation(dec_row[d1, :], back(dec_tmp[d1, :]), ACT.Exp))
            act.wait_ge(row_dve, 2)
            link(act.activation(t_row[d0, :], f_row[d0, :], ACT.Exp))
            link(act.activation(t_row[d1, :], back(f_row[d1, :]), ACT.Exp))
            act.wait_ge(row_dve, 3)
            link(act.activation(f_row[d0, :], i_row[d0, :], ACT.Exp))
            link(act.activation(f_row[d1, :], back(i_row[d1, :]), ACT.Exp), g_made)

            for h in range(MH):
                for m, dst in enumerate((q_t[:, 0, :], k_t[:, 0, :],
                                         k_tok[:, 0:4, :].rearrange("p c d -> p (c d)"), v_tok[:, 0:4, 0:MD])):
                    act.wait_ge(prep_done, 8 * h + 2 * m + 1)
                    src = pair[0][:, :] if m < 3 else pair[0][:, :].rearrange("p (c d) -> p c d", c=4)
                    link(act.activation(dst, src, ACT.Copy), prep_act)

                def decayed(n, d):
                    g = NDIR * (CH * h + n) + d
                    c = n if d == 0 else CH - 1 - n
                    if n == 0:
                        act.wait_ge(bm_ready, h + 1)
                        act.wait_ge(gt_ready, 1)
                    if g >= 2:
                        act.wait_ge(wt_ready, g - 1)
                    r = MH * d + h
                    link(act.activation(e_w[:, d, :], bm_b[:, d, c * P:(c + 1) * P], ACT.Exp,
                                         bias=g_tok[:, c, r:r + 1]), e_ready)

                for d in range(NDIR):
                    decayed(0, d)
                for n in range(CH):
                    for d in range(NDIR):
                        g = NDIR * (CH * h + n) + d
                        act.wait_ge(ab_done, g + 1)
                        if g >= 2:
                            act.wait_ge(h_done, g - 1)
                        link(act.activation(num_a[:, d, :], pair[0][:, d * HALF:d * HALF + VE],
                                             ACT.Copy), acp_ready)
                        if n + 1 < CH:
                            decayed(n + 1, d)
                act.wait_ge(bn_ready, h + 1)
                if h >= 1:
                    act.wait_ge(ln_done, h)
                link(act.activation(rstd_h[:, :], bn2[:, :, 1], ACT.Ln, bias=eps_col[:, :]))
                link(act.activation(rstd_h[:, :], rstd_h[:, :], ACT.Exp, scale=-0.5), rh_ready)

            act.wait_ge(y_made, Y0["y3"] + 2 * KT)
            split_y("y3", stage_f, o_hi, 2 * KT, (KT, KT - 1))
            norm_squares(4, xf, sq_f, 1, 3 * KT, False)
            norm_rstd(4, rstd_f)

        @block.vector
        def _(dve):
            link, signal = linker(dve, dve_step)

            def low_part(lo, full, hi, done):
                link(dve.tensor_tensor(lo, full, hi, ALU.subtract), done)

            def norm_apply(n, x, stage, rstd, gain, hn0, op0):
                dve.wait_ge(rstd_ready, n + 1)
                for k in range(KT + 1):
                    if k < KT:
                        link(dve.scalar_tensor_tensor(out=stage[:, k % 2, :], in0=x[:, k, :], scalar=col(gain, k),
                                               in1=rstd[:, :], op0=ALU.mult, op1=ALU.mult), hn_ready)
                    if k >= 1:
                        low(k - 1, stage, op0)

            def low(k, stage, op0, hi=None, lo=None):
                dve.wait_ge(hi_ready, op0 + k + 1)
                low_part((op_lo if lo is None else lo)[:, k, :], stage[:, k % 2, :],
                         (op_hi if hi is None else hi)[:, k, :], op_ready)

            def free(unit_no):
                signal(pair_free[job_of(unit_no) % 2])

            link(dve.memset(ones[:, :], 1.0), ready0)
            link(dve.memset(eps_col[:, :], EPS), ready0)
            link(dve.memset(u_pad[:, 0:1], 0.0))
            link(dve.memset(u_pad[:, S + 1:S + 2], 0.0))
            dve.wait_ge(consts, 64)

            norm_apply(0, xa, stage_a, rstd_a, "norm_even", 0, 0)
            R2 = float(np.sqrt(0.5))
            for j in range(AB):
                dve.wait_ge(bu_ready, j + 1)
                link(dve.tensor_tensor(fold[:, 0:4, :], bu[:, 0:4, :], bu[:, 4:8, :], ALU.add))
                link(dve.tensor_tensor(fold[:, 4:8, :], bu[:, 0:4, :], bu[:, 4:8, :], ALU.subtract))
                if j >= 1:
                    dve.wait_ge(fft1_done, j)
                link(dve.tensor_tensor(bu[:, 0:2, :], fold[:, 0:2, :], fold[:, 2:4, :], ALU.add))
                link(dve.tensor_tensor(parts[:, 4:6, :], fold[:, 0:2, :], fold[:, 2:4, :], ALU.subtract))
                link(dve.tensor_tensor(bu[:, 2, :], fold[:, 5, :], fold[:, 7, :], ALU.subtract))
                link(dve.tensor_tensor(bu[:, 3, :], fold[:, 5, :], fold[:, 7, :], ALU.add))
                link(dve.tensor_tensor(parts[:, 0, :], bu[:, 0, :], bu[:, 1, :], ALU.add))
                link(dve.tensor_tensor(parts[:, 1, :], bu[:, 0, :], bu[:, 1, :], ALU.subtract))

                def combine(dst, a, scale, b, op, done=None):
                    link(dve.scalar_tensor_tensor(out=dst, in0=a, scalar=scale, in1=b, op0=ALU.mult, op1=op), done)

                combine(parts[:, 2, :], bu[:, 2, :], R2, fold[:, 4, :], ALU.add)
                combine(parts[:, 3, :], bu[:, 3, :], R2, fold[:, 6, :], ALU.add)
                combine(parts[:, 6, :], bu[:, 2, :], -R2, fold[:, 4, :], ALU.add)
                combine(parts[:, 7, :], bu[:, 3, :], R2, fold[:, 6, :], ALU.subtract, parts_ready)
                u = 6 * j + 2
                wait_job(dve, u)
                dve.wait_ge(ax_ready, j + 1)
                link(dve.tensor_tensor(u_pad[:, 1:S + 1], pair[u % 2][:, :], ax_sb[:, :], ALU.mult), prod_done)
                dve.wait_ge(prod_done, j + 1)
                free(u)
                link(dve.tensor_scalar(cv[:, :], u_pad[:, 0:S], col("conv_w", 3 * j), None, ALU.mult))
                for tap in (1, 2):
                    link(dve.scalar_tensor_tensor(out=cv[:, :], in0=u_pad[:, tap:tap + S],
                                                scalar=col("conv_w", 3 * j + tap), in1=cv[:, :],
                                                op0=ALU.mult, op1=ALU.add))
                dve.wait_ge(fft2_done, j + 1)
                dve.wait_ge(szb_ready, j + 1)
                if j >= 1:
                    dve.wait_ge(y_stored[0], 16 * j)
                link(dve.tensor_tensor(y_a[:, 0, :].rearrange("p (k2 k1) -> p k1 k2", k1=RADIX),
                                aux[:, 0:S].rearrange("p (k1 k2) -> p k1 k2", k1=RADIX),
                                sz_b[:, :].rearrange("p (k2 k1) -> p k1 k2", k1=RADIX),
                                ALU.mult), y_made)
                u = 6 * j + 4
                wait_job(dve, u)
                link(dve.tensor_tensor(cv[:, :], pair[u % 2][:, :], cv[:, :], ALU.mult))
                free(u)
                dve.wait_ge(sza_ready, j + 1)
                if j >= 1:
                    dve.wait_ge(y_stored[1], 16 * j)
                link(dve.tensor_tensor(y_a[:, 1, :], cv[:, :], sz_a[:, :], ALU.mult), y_made)
            for k in range(KT):
                low(k, stage_a, OP0["y1"])

            def add_residual(unit0, x, count0, jobs=None):
                for k in range(KT):
                    job = unit0 + k
                    wait_job(dve, job)
                    link(dve.tensor_tensor(x[:, k, :], pair[job % 2][:, :], x[:, k, :], ALU.add), x_done)
                    signal(pair_free[job % 2])

            add_residual(BASE[1], xa, 0)
            norm_apply(1, xa, stage_a, rstd_a, "norm_odd", KT, OP0["odd"])

            dve.wait_ge(x_stored, 16 * KT)
            dve.wait_ge(op_ready, OP0["odd"] + KT)
            dve.wait_ge(consts, 80)

            def rotate(r, gain, cols):
                dve.wait_ge(raw_ready, r + 1)
                for n in range(2):
                    link(dve.scalar_tensor_tensor(out=q_raw[:, n, cols], in0=q_raw[:, n, cols],
                                                  scalar=col(gain, n), in1=rope_sb[:, n, cols],
                                                  op0=ALU.mult, op1=ALU.mult))
                link(dve.tensor_tensor(q_raw[:, 0, cols], q_raw[:, 0, cols], q_raw[:, 1, cols], ALU.add))
                dve.wait_ge(qrstd, r + 1)
                link(dve.tensor_tensor(q_raw[:, 0, cols], q_raw[:, 0, cols], rstd_b[:, cols], ALU.mult),
                     qr_ready)

            def split_lo(r, lo, hi, cols):
                dve.wait_ge(qhi_ready, r + 1)
                low_part(lo, q_raw[:, 0, cols], hi, q_ready)

            whole = slice(0, S)
            for g in range(KV_HEADS):
                rotate(g, "k_gain", whole)
                split_lo(g, k_lo[:, g, :], k_hi[:, g, :], whole)
                dve.wait_ge(vhi_ready, g + 1)
                low_part(v_lo[:, g, :, :].rearrange("p a b -> p (a b)"), aux[:, 2 * HALF:4 * HALF],
                         v_hi[:, g, :, :].rearrange("p a b -> p (a b)"), v_ready)

            def q_rotate_half(h, c):
                rotate(KV_HEADS + 2 * h + c, "q_gain", slice(c * HALF, (c + 1) * HALF))

            def q_lo_half(h, c):
                cols = slice(c * HALF, (c + 1) * HALF)
                split_lo(KV_HEADS + 2 * h + c, q_lo[:, h % 2, cols], q_hi[:, h % 2, cols], cols)

            def maxima(t):
                dve.wait_ge(s_done, t + 1)
                if t >= 2:
                    dve.wait_ge(exp_done, t - 1)
                link(dve.reduce_max(stat_b[:, t % 2, 2:3], aux[:, (t % 2) * S:(t % 2 + 1) * S], AX.X))
                link(dve.tensor_scalar(stat_b[:, t % 2, 0:1], stat_b[:, t % 2, 2:3], -SCORE_SCALE, None,
                                ALU.mult), neg_ready)

            def normalise(t):
                dve.wait_ge(exp_done, t + 1)
                link(dve.reciprocal(stat_b[:, t % 2, 3:4], stat_b[:, t % 2, 1:2]))
                link(dve.tensor_scalar(prob[:, t % 2, :], prob[:, t % 2, :], stat_b[:, t % 2, 3:4], None,
                                ALU.mult), p_ready)

            def turned_low(t):
                dve.wait_ge(pt_hi_ready, t + 1)
                cols = slice((t % 2) * P, (t % 2 + 1) * P)
                low_part(pt_lo[:, :, cols], pair[0][:, :].rearrange("p (k q) -> p k q", k=QT),
                         pt_hi[:, :, cols], pt_ready)

            def gate_values(n):
                h, m = n // 4, n % 4
                dve.wait_ge(pv_done, n + 1)
                if m == 0:
                    dve.wait_ge(szq_ready, h + 1)
                    if h >= 2:
                        dve.wait_ge(y_stored[h % 2], 16 * (Y0["y2"] // 2 + h // 2))
                cols = slice(m * 2 * P, (m + 1) * 2 * P)
                link(dve.tensor_tensor(y_b[:, h % 2, cols], pair[1][:, HALF:HALF + 2 * P],
                                sz_q[:, h % 2, cols], ALU.mult), yq_done)
                if m == 3:
                    signal(y_made)

            for c in range(2):
                q_rotate_half(0, c)
                q_lo_half(0, c)
            maxima(0)
            maxima(1)
            normalise(0)
            for t in range(QT * HEADS):
                h, i = t // QT, t % QT
                beside = h + 1 < HEADS
                if t + 1 < QT * HEADS:
                    normalise(t + 1)
                turned_low(t)
                if t + 2 < QT * HEADS:
                    maxima(t + 2)
                if t >= 2 and t % 2 == 0:
                    gate_values(t // 2 - 1)
                if beside and i in (2, 4):
                    q_rotate_half(h + 1, i // 2 - 1)
                if beside and i in (3, 5):
                    q_lo_half(h + 1, i // 2 - 1)
                if not beside and i >= 1:
                    low(i - 1, q_raw, OP0["y2"])
            gate_values(4 * HEADS - 1)
            low(KT - 1, y_b, OP0["y2"])
            for k in range(KT):
                dve.wait_ge(x_loaded[k], 32)
            add_residual(BASE[3], xc, KT)
            dve.wait_ge(rstd_ready, 3)
            for k in range(KT):
                link(dve.scalar_tensor_tensor(out=xc[:, k, :], in0=xc[:, k, :], scalar=col("final_norm", k),
                                       in1=rstd_c[:, :], op0=ALU.mult, op1=ALU.mult), x_done)
            norm_apply(3, xc, stage_c, rstd_c, "norm_in", 2 * KT, OP0["in"])

            dve.wait_ge(op_ready, OP0["in"] + KT)
            dve.wait_ge(x_stored, 32 * KT)
            for t in range(KT):
                link(dve.memset(u_rows[:, t, 0:2], 0.0))
                link(dve.memset(u_rows[:, t, 2 + S:4 + S], 0.0))
            link(dve.memset(pool_pad[:, 0:PAD], 0.0))
            link(dve.memset(pool_pad[:, PAD + S:2 * PAD + S], 0.0), pads_ready)
            dve.wait_ge(consts_d, 80)

            def block_diagonal(dst, blocks, mask, done=None):
                link(dve.tensor_tensor(dst.rearrange("p (m o) -> p m o", o=4),
                                       blocks.unsqueeze(1).broadcast_to([P, 32, 4]),
                                       mask[:, :].unsqueeze(2).broadcast_to([P, 32, 4]), ALU.mult), done)

            for i in range(3 * KT):
                if i >= 2:
                    dve.wait_ge(weff_done, i - 1)
                block_diagonal(bdt[:, i % 2, :], blocks_d[:, i % 3, i // 3, :], bmask_d, bdt_ready)
            dve.wait_ge(weff_done, 3 * KT)
            link(dve.tensor_copy(gw_eff[:, :, :].rearrange("p a b -> p (a b)"), aux[:, 0:2 * KT * 16]), weff_ready)
            for t in range(KT):
                dve.wait_ge(u_ready, t + 1)
                if t >= 2:
                    dve.wait_ge(c_ready, t - 1)
                acc = conv_acc[:, t % 2, 0:S]
                link(dve.tensor_scalar(acc, u_rows[:, t, 0:S], col("conv_w2", TAPS2 * t), col("conv_b2", t),
                                     ALU.mult, ALU.add))
                for tap in range(1, TAPS2):
                    link(dve.scalar_tensor_tensor(out=acc, in0=u_rows[:, t, tap:tap + S],
                                                 scalar=col("conv_w2", TAPS2 * t + tap), in1=acc,
                                                 op0=ALU.mult, op1=ALU.add))
                signal(conv_done)
            dve.wait_ge(c_ready, KT)
            for g, w in enumerate(WINDOWS):
                left = (w - 1) // 2
                right = w - 1 - left
                for i in range(2):
                    n = 2 * g + i
                    dve.wait_ge(px_ready, n + 1)
                    src, length, span, b = pool_pad[:, :], S + 2 * PAD, 1, 0
                    while span < w:
                        length -= span
                        dst = conv_acc[:, b, 0:length]
                        link(dve.tensor_tensor(dst, src[:, 0:length], src[:, span:span + length], ALU.add))
                        src, b, span = conv_acc[:, b, :], 1 - b, 2 * span
                    total = src[:, PAD - left:PAD - left + S]
                    if left:
                        link(dve.tensor_tensor(total[:, 0:left], total[:, 0:left], edge_sb[:, g, 0, 0:left], ALU.mult))
                    link(dve.tensor_tensor(total[:, S - right:S], total[:, S - right:S],
                                         edge_sb[:, g, 1, PAD - right:PAD], ALU.mult))
                    if g >= 1:
                        dve.wait_ge(mix_done, 2 * g)
                    link(dve.scalar_tensor_tensor(out=pooled[:, i, :], in0=total, scalar=1.0 / w,
                                           in1=pool_pad[:, PAD:PAD + S], op0=ALU.mult,
                                           op1=ALU.subtract), pooled_ready)
                for i in range(2):
                    n = 2 * g + i
                    dve.wait_ge(mix_done, n + 1)
                    dve.wait_ge(szp_ready, n + 1)
                    if n >= 2:
                        dve.wait_ge(y_stored[n % 2], 16 * (Y0["y3"] // 2 + n // 2))
                    link(dve.scalar_tensor_tensor(out=y_d[:, n % 2, :], in0=aux[:, 0:S], scalar=col("pool_scale", n),
                                           in1=sz_p[:, :], op0=ALU.mult, op1=ALU.mult), y_made)

            dve.wait_ge(y_stored[0], 16 * (Y0["y3"] // 2 + KT // 2))
            dve.wait_ge(y_stored[1], 16 * (Y0["y3"] // 2 + KT // 2))
            dve.wait_ge(gate_stored, 16)
            dve.wait_ge(mz_stored[0], 16 * KT // 2)
            dve.wait_ge(mz_stored[1], 16 * KT // 2)
            dve.wait_ge(unit_done, BASE[5])
            link(dve.memset(i_row[:, :], 0.0), rows_clear)
            link(dve.memset(f_row[:, :], 0.0), rows_clear)
            link(dve.memset(mp_row[:, :], 0.0), rows_clear)
            link(dve.memset(v_tok[:, :, MD:VE], 1.0), rows_clear)
            dve.wait_ge(consts_e, 48)
            for i in range(3 * KT):
                block_diagonal(bd[:, i // KT, i % KT, :], blocks_e[:, i // KT, i % KT, :], bmask_e)
            ks = bd[:, 1, :, :].rearrange("p a b -> p (a b)")
            link(dve.tensor_scalar(ks, ks, float(MD) ** -0.5, None, ALU.mult), bd_ready)
            d0, d1 = slice(0, MH), slice(32, 32 + MH)
            dve.wait_ge(row_act, 1)
            dve.wait_ge(rows_in, 16 * 5)
            link(dve.scalar_tensor_tensor(out=f_row[:, :], in0=f_row[:, :], scalar=0.0, in1=t_row[:, :],
                                        op0=ALU.min, op1=ALU.subtract))
            link(dve.tensor_copy(b_row[d1, :], i_row[d1, ::-1]))
            link(dve.tensor_copy(a_row[d1, :], f_row[d1, ::-1]))
            link(dve.tensor_copy(i_row[d1, :], b_row[d1, :]))
            link(dve.tensor_copy(f_row[d1, :], a_row[d1, :]))
            link(dve.tensor_tensor_scan(b_row[:, :], reset_row[:, :], f_row[:, :], 0.0, ALU.mult, ALU.add))
            link(dve.tensor_tensor_scan(t_row[:, :], f_row[:, :], i_row[:, :], 0.0, ALU.add, ALU.max))
            link(dve.tensor_tensor(f_row[:, :], b_row[:, :], t_row[:, :], ALU.subtract))
            link(dve.tensor_tensor(i_row[:, :], i_row[:, :], b_row[:, :], ALU.subtract))
            link(dve.tensor_copy(mp_row[:, 1:CH], t_row[:, P - 1:S - P:P]))
            link(dve.tensor_copy(end_row[:, :], f_row[:, P - 1:S:P]))
            link(dve.tensor_tensor(dec_tmp[:, :], end_row[:, :], mp_row[:, :], ALU.add))
            link(dve.tensor_copy(reset_row[d0, :], f_row[d0, :]))
            link(dve.tensor_copy(reset_row[d1, :], f_row[d1, ::-1]))
            link(dve.tensor_copy(a_row[d0, :], i_row[d0, :]))
            link(dve.tensor_copy(a_row[d1, :], i_row[d1, ::-1]))
            signal(bm_made)
            signal(row_dve)

            def by_chunk(row):
                return row[:, :].rearrange("p (c s) -> p c s", c=CH)

            link(dve.tensor_tensor(by_chunk(f_row), by_chunk(f_row),
                                 mp_row[:, :].unsqueeze(2).broadcast_to([36, CH, P]), ALU.add))
            signal(row_dve)
            link(dve.tensor_tensor(by_chunk(i_row), by_chunk(i_row),
                                 end_row[:, :].unsqueeze(2).broadcast_to([36, CH, P]), ALU.add))
            signal(row_dve)
            dve.wait_ge(gt_done, 1)
            link(dve.tensor_copy(g_tok[:, :, :].rearrange("p a b -> p (a b)"), aux[:, 0:CH * 32]), gt_ready)
            dve.wait_ge(decay_in, 16)

            for h in range(MH):
                for m, dst in enumerate((q_t[:, 1, :], k_t[:, 1, :],
                                         k_tok[:, 4:8, :].rearrange("p c d -> p (c d)"), v_tok[:, 4:8, 0:MD])):
                    dve.wait_ge(prep_done, 8 * h + 2 * m + 2)
                    src = pair[1][:, :] if m < 3 else pair[1][:, :].rearrange("p (c d) -> p c d", c=4)
                    link(dve.tensor_copy(dst, src), prep_dve)
                dve.wait_ge(bm_loaded, 32 * (h + 1))
                for d in range(NDIR):
                    link(dve.tensor_tensor(by_chunk(bm_b[:, d, :]), by_chunk(bm_b[:, d, :]),
                                          mask_sb[:, d, :].unsqueeze(1).broadcast_to([P, CH, P]), ALU.add))
                signal(bm_ready)
                dve.wait_ge(prep_act, 4 * h + 4)
                dve.wait_ge(st_done, h + 1)

                def weights(n, d):
                    g = NDIR * (CH * h + n) + d
                    ks = NDIR * ((CH - 1) * h + n) + d
                    c = n if d == 0 else CH - 1 - n
                    dve.wait_ge(e_ready, g + 1)
                    if g >= 2:
                        dve.wait_ge(ab_done, g - 1)
                    link(dve.tensor_tensor(w_t[:, d, :], aux[:, c * P:(c + 1) * P], e_w[:, d, :],
                                    ALU.mult), wt_ready)
                    if n < CH - 1:
                        if ks >= 2:
                            dve.wait_ge(upd_done, ks - 1)
                        r = 16 + MH * d + h
                        link(dve.tensor_scalar(k_w[:, d, :], k_tok[:, c, :], g_tok[:, c, r:r + 1], None,
                                        ALU.mult), kw_ready)

                def finish(n, d):
                    g = NDIR * (CH * h + n) + d
                    ks = NDIR * ((CH - 1) * h + n) + d
                    c = n if d == 0 else CH - 1 - n
                    r = MH * d + h
                    if n < CH - 1:
                        dve.wait_ge(upd_done, ks + 1)
                        upd = aux[:, 2 * HALF:4 * HALF].rearrange("p (i e) -> p i e", i=2)[:, :, 0:VE]
                        if n == 0:
                            link(dve.tensor_copy(state[:, d, :, :], upd), state_ready)
                        else:
                            link(dve.scalar_tensor_tensor(out=state[:, d, :, :], in0=state[:, d, :, :],
                                                   scalar=decay_b[:, r, c:c + 1], in1=upd,
                                                   op0=ALU.mult, op1=ALU.add), state_ready)
                    dve.wait_ge(acp_ready, g + 1)
                    num = num_a[:, d, :]
                    if n >= 1:
                        dve.wait_ge(ab_done, g + 1)
                        link(dve.scalar_tensor_tensor(out=num_b[:, d, :], in0=pair[1][:, d * HALF:d * HALF + VE],
                                                    scalar=g_tok[:, c, 8 + r:9 + r], in1=num_a[:, d, :],
                                                    op0=ALU.mult, op1=ALU.add))
                        num = num_b[:, d, :]
                    link(dve.tensor_scalar(small[:, d, 2:3], num[:, MD:VE], -1.0, g_tok[:, c, 24 + r:25 + r],
                                         ALU.mult, ALU.max))
                    link(dve.tensor_tensor(small[:, d, 0:1], small[:, d, 2:3], num[:, MD:VE], ALU.max))
                    link(dve.reciprocal(small[:, d, 1:2], small[:, d, 0:1]))
                    if n < CH // 2:
                        link(dve.tensor_scalar(h_tok[:, c, :], num[:, 0:MD], small[:, d, 1:2], None,
                                        ALU.mult), h_done)
                    else:
                        link(dve.scalar_tensor_tensor(out=h_tok[:, c, :], in0=num[:, 0:MD], scalar=small[:, d, 1:2],
                                               in1=h_tok[:, c, :], op0=ALU.mult, op1=ALU.add), h_done)

                order = [(n, d) for n in range(CH) for d in range(NDIR)]
                weights(*order[0])
                for m in range(len(order)):
                    if m + 1 < len(order):
                        weights(*order[m + 1])
                    finish(*order[m])
                dve.wait_ge(h_done, NDIR * CH * (h + 1))
                for c in range(CH):
                    link(dve.bn_stats(bn6[:, c, :], h_tok[:, c, :]))
                for c in range(CH):
                    link(dve.bn_aggr(bn2[:, c, :], bn6[:, c, :]))
                signal(bn_ready)
                dve.wait_ge(rh_ready, h + 1)
                for c in range(CH):
                    link(dve.tensor_scalar(h_tok[:, c, :], h_tok[:, c, :], bn2[:, c, 0:1], rstd_h[:, c:c + 1],
                                          ALU.subtract, ALU.mult))
                signal(ln_done)
                for i in range(2):
                    n = 2 * h + i
                    if h >= 1:
                        dve.wait_ge(y_stored[i], 16 * ((Y0["y3"] + KT) // 2 + h))
                    link(dve.tensor_scalar(out_e[:, i, :], c_rows[:, n, :], col("skip", n), None, ALU.mult))
                    dve.wait_ge(ht_done, n + 1)
                    link(dve.scalar_tensor_tensor(out=out_e[:, i, :], in0=pair[i][:, :], scalar=col("mh_norm", n),
                                                in1=out_e[:, i, :], op0=ALU.mult, op1=ALU.add))
                    dve.wait_ge(mz_in[i], 16 * (h + 1))
                    link(dve.tensor_tensor(out_e[:, i, :], out_e[:, i, :], mz_sb[:, i, :], ALU.mult), y_made)

            for k in range(2 * KT):
                low(k, stage_f, OP0["y3"], o_hi, o_lo)
            for k in range(KT):
                dve.wait_ge(x_loaded[k], 48)
            add_residual(BASE[5], xf, 3 * KT)
            dve.wait_ge(rstd_ready, 5)
            for k in range(KT):
                if k >= 2:
                    dve.wait_ge(out_stored[k % 2], 16 * (k // 2))
                link(dve.scalar_tensor_tensor(out=stage_f[:, k % 2, :], in0=xf[:, k, :], scalar=col("norm_out", k),
                                       in1=rstd_f[:, :], op0=ALU.mult, op1=ALU.mult), out_made)


def _tables():
    f = np.float32
    n = np.arange(P)
    ang = 2 * np.pi * np.outer(n, n) / P
    scale = 1.0 / np.sqrt(S * P)
    c, s = np.cos(ang) * scale, np.sin(ang) * scale
    dft_d = np.stack([np.concatenate([c, s], 1), np.concatenate([-s, c], 1), np.concatenate([s, -c], 1)], 1)
    k = np.arange(S).reshape(P, RADIX).T
    phase = 2 * np.pi * (n[:, None, None] * k[None]) / S
    dft_s = np.stack([np.cos(phase), -np.sin(phase)], 1)
    pairs = P // 4
    inv = (f(10000.0) ** (-np.arange(pairs, dtype=f) / f(pairs))).astype(f)
    t = np.arange(S)
    row, colm = (t // 64).astype(f), (t % 64).astype(f)
    a = np.concatenate([row[None] * inv[:, None], colm[None] * inv[:, None]], 0).astype(f).astype(np.float64)
    cs, sn = np.cos(a), np.sin(a)
    rope = np.stack([np.concatenate([cs, cs]), np.concatenate([-sn, sn])], 1)
    edge = np.ones((4, 2, PAD))
    for g, w in enumerate(WINDOWS):
        left = (w - 1) // 2
        right = w - 1 - left
        for t_ in range(left):
            edge[g, 0, t_] = w / (t_ + right + 1)
        for j in range(right):
            edge[g, 1, PAD - right + j] = w / (left + 1 + right - 1 - j)
    i = np.arange(P)
    masks = np.stack([np.where(i[:, None] <= i[None], 0.0, NEG), np.where(i[:, None] >= i[None], 0.0, NEG)], 1)
    block_mask = (i[:, None] // 4 == np.arange(32)[None]).astype(f)
    reset = np.ones((36, S))
    reset[:, ::P] = 0.0
    return {"ident_in": np.eye(P), "dft_d": dft_d, "dft_s": dft_s, "rope": rope,
            "edge": np.broadcast_to(edge, (P, 4, 2, PAD)), "masks": masks, "block_mask": block_mask,
            "reset_mask": reset}


def _units(w, blocks):
    out = []
    for b in blocks:
        cols, k0 = b if isinstance(b, tuple) else (b, 0)
        part = w[k0 * P:(k0 + KT) * P][:, cols]
        out.append(part.reshape(KT, P, P).transpose(1, 0, 2).reshape(P, KT * P))
    return out


def kernel(**inputs):
    import concourse.bacc as _bacc
    from concourse.bass_utils import run_bass_kernel_spmd as _run

    a = {k: np.asarray(v) for k, v in inputs.items()}

    def cols(b):
        return np.arange(b * P, (b + 1) * P)

    pair_order = np.concatenate([np.arange(0, P, 2), np.arange(1, P, 2)])
    units = []
    for j in range(AB):
        units += _units(a["w_in_even"][0], [cols(b) for b in (16 + j, j, 8 + j, 20 + j, 4 + j, 12 + j)])
    units += _units(a["w_out_even"][0], [cols(e) for e in range(KT)])
    w = a["w_in_odd"][0]
    for g in range(KV_HEADS):
        units += _units(w, [cols(HEADS + g)[pair_order], cols(HEADS + KV_HEADS + g)])
    for h in range(HEADS):
        units += _units(w, [cols(h)[pair_order], cols(HEADS + 2 * KV_HEADS + h)])
    units += _units(a["w_out_odd"][0], [cols(e) for e in range(KT)])
    w = a["w_in_2"][0]
    units += _units(w, [cols(16 + t) for t in range(KT)])
    for g in range(4):
        units += _units(w, [cols(b) for b in (2 * g, 2 * g + 1, 8 + 2 * g, 9 + 2 * g)])
    units += _units(w, [cols(24 + t) for t in range(KT)])
    units += _units(a["w_out_2"][0], [(cols(e), KT * i) for e in range(KT) for i in range(2)])

    def by_block(v):
        return v.reshape(-1, P).T

    def taps(v):
        return v.reshape(v.shape[0], -1, P).transpose(2, 1, 0).reshape(P, -1)

    params = {"norm_even": by_block(a["norm_even"][0]), "conv_w": taps(a["conv_w"][0]),
              "norm_odd": by_block(a["norm_odd"][0]), "final_norm": by_block(a["final_norm"]),
              "norm_in": by_block(a["norm_in_g_2"][0]), "norm_out": by_block(a["norm_out_g_2"]),
              "q_gain": np.stack([a["q_gain"][0][pair_order], a["q_gain"][0][np.roll(pair_order, P // 2)]], 1),
              "k_gain": np.stack([a["k_gain"][0][pair_order], a["k_gain"][0][np.roll(pair_order, P // 2)]], 1),
              "pool_scale": by_block(a["pool_scale_2"][0]), "conv_w2": taps(a["conv_w_2"][0]),
              "conv_b2": by_block(a["conv_b_2"][0]), "mh_norm": by_block(a["mh_norm_w_2"][0]),
              "skip": by_block(a["skip_w_2"][0])}
    qkv = np.stack([a[k][0] for k in ("w_q_2", "w_k_2", "w_v_2")]).reshape(3, KT, 32, 4, 4)
    straight = qkv.reshape(3, KT, P, 4).transpose(2, 0, 1, 3)
    turned = qkv.transpose(0, 1, 2, 4, 3).reshape(3, KT, P, 4).transpose(2, 0, 1, 3)
    gw = a["w_gates_2"][0].reshape(NDIR, 3 * KT, P, 2, MH).transpose(2, 1, 3, 0, 4).reshape(P, 3 * KT, 16)
    gb = a["b_gates_2"][0].reshape(NDIR, 2, MH).transpose(1, 0, 2).reshape(16, 1)
    arrays = {"x_t": a["x"][0].T.reshape(KT, P, S), "weight_units": np.stack(units),
              "channel_params": np.concatenate([params[k] for k in PARAMS], 1),
              "qkv_blocks": np.stack([straight, turned]), "gate_w": gw, "gate_b": gb,
              "pool_w": a["pool_w_2"][0].reshape(4, 2, P, MD).transpose(0, 2, 1, 3)}
    arrays.update({k: v.astype(np.float32) for k, v in _tables().items()})
    arrays = {k: np.ascontiguousarray(v) for k, v in arrays.items()}

    nc = _bacc.Bacc("TRN2", target_bir_lowering=False, num_devices=1)
    args = {k: nc.dram_tensor(k, v.shape, mybir.dt.from_np(v.dtype), kind="ExternalInput").ap()
            for k, v in arrays.items()}
    out = nc.dram_tensor("out", [KT, P, S], F32, kind="ExternalOutput").ap()
    build(nc, out=out, **args)
    r = _run(nc, [arrays], core_ids=[0])
    return r.results[0]["out"].reshape(D, S).T.reshape(1, S, D)
```

```python
from contextlib import ExitStack

import numpy as np
import concourse.bass as bass
from concourse import mybir

P = 128
S = 1024
D = 1024
KT = D // P
HALF = 512
EPS = 1e-6
F32 = mybir.dt.float32
F32R = mybir.dt.float32r
ALU = mybir.AluOpType
ACT = mybir.ActivationFunctionType
AX = mybir.AxisListType

AB = 4
RADIX = 8
HEADS, KV_HEADS = 8, 2
GROUP = HEADS // KV_HEADS
QT = S // P
SCORE_SCALE = float(P) ** -0.5
WINDOWS = (2, 4, 8, 16)
PAD = 8
MH = 4
MD = 256
VE = MD + 1
CH = S // P
NDIR = 2
TAPS2 = 5
NEG = -1e30

EVEN_IN, EVEN_OUT, ODD_IN, ODD_OUT, SEC_IN, SEC_OUT = 24, 8, 20, 8, 32, 16
BASE = np.cumsum([0, EVEN_IN, EVEN_OUT, ODD_IN, ODD_OUT, SEC_IN, SEC_OUT]).tolist()
UNITS = BASE[-1]

PARAMS = {}
_at = 0
for _name, _n in (("norm_even", 8), ("conv_w", 12), ("norm_odd", 8), ("final_norm", 8), ("norm_in", 8),
                  ("norm_out", 8), ("q_gain", 2), ("k_gain", 2), ("pool_scale", 8), ("conv_w2", 40),
                  ("conv_b2", 8), ("mh_norm", 8), ("skip", 8)):
    PARAMS[_name] = _at
    _at += _n
N_PARAMS = _at


def linker(eng, step):
    count = {}

    def link(instruction, semaphore=None):
        semaphore = step if semaphore is None else semaphore
        instruction.then_inc(semaphore, 1)
        count[id(semaphore)] = count.get(id(semaphore), 0) + 1
        eng.wait_ge(semaphore, count[id(semaphore)])

    def signal(semaphore):
        eng.sem_inc(semaphore, 1)
        count[id(semaphore)] = count.get(id(semaphore), 0) + 1

    return link, signal


def build(nc, x_t, weight_units, channel_params, ident_in, dft_d, dft_s, rope, edge, masks, block_mask,
          qkv_blocks, gate_w, gate_b, pool_w, reset_mask, out):
    ctx = ExitStack()
    with ctx:
        def sem(name):
            return ctx.enter_context(nc.semaphore(name))

        def dram(name, shape):
            return nc.dram_tensor(name, shape, F32).ap()

        x1_dram = dram("x1_dram", [KT, P, S])
        x2_dram = dram("x2_dram", [KT, P, S])
        r_dram = dram("r_dram", [P, S])
        y1_dram = dram("y1_dram", [KT, P, S])
        y2_dram = dram("y2_dram", [KT, P, S])
        y3_dram = dram("y3_dram", [2 * KT, P, S])
        mz_dram = dram("mz_dram", [KT, P, S])
        gate_dram = dram("gate_dram", [16, S])
        bm_dram = dram("bm_dram", [2 * MH, S])
        decay_dram = dram("decay_dram", [2 * MH, CH])

        at = [-(-nc.sbuf_base // 32) * 32]

        def keep(name, shape, dt=F32):
            tensor = nc.alloc_sbuf_tensor_at(name, shape, dt, offset=at[0])
            size = 4
            for n in shape[1:]:
                size *= n
            at[0] += -(-size // 32) * 32
            assert at[0] <= nc.sbuf_usable_end, name
            return tensor

        par = keep("par", [P, N_PARAMS])
        ident = keep("ident", [P, P])
        ones = keep("ones", [P, P])
        eps_col = keep("eps_col", [P, 1])
        eps2_col = keep("eps2_col", [P, 1])
        ln_ahead = keep("ln_ahead", [P, 1])
        gain2 = keep("gain2", [P, KT])
        gain_both = keep("gain_both", [P, KT])
        w_raw = keep("w_raw", [P, 3, KT * P])
        w_hi = keep("w_hi", [P, 2, KT * P], F32R)
        w_lo = keep("w_lo", [P, 2, KT * P], F32R)

        def col(name, i=0):
            return par[:, PARAMS[name] + i:PARAMS[name] + i + 1]

        op_start = at[0]
        op_hi = keep("op_hi", [P, KT, S], F32R)
        op_lo = keep("op_lo", [P, KT, S], F32R)
        phase_start = at[0]
        xa = keep("xa", [P, KT, S])
        stage_n = nc.alloc_sbuf_tensor_at("stage_n", [P, 4, S], F32, offset=at[0])
        at[0] += 2 * 4 * S
        sq_a = keep("sq_a", [P, 2, S])
        rstd_a = keep("rstd_a", [P, S])
        acc_a = keep("acc_a", [P, S])
        y_a = keep("y_a", [P, 2, S])
        tab_d = keep("tab_d", [P, 3, 2 * P])
        tab_s = keep("tab_s", [P, 2, RADIX, P])
        spec = keep("spec", [P, RADIX, 2 * P])
        parts = keep("parts", [P, RADIX, P])
        fold = keep("fold", [P, RADIX, P])
        bu = keep("bu", [P, RADIX, P])
        ax_sb = keep("ax_sb", [P, S])
        u_pad = keep("u_pad", [P, S + 2])
        cv = keep("cv", [P, S])
        sz_b = keep("sz_b", [P, S])
        at[0] = phase_start + 4 * KT * S
        stage_y = keep("stage_y", [P, 6, S])
        at[0] = phase_start
        q_hi = keep("q_hi", [P, 2, S], F32R)
        q_lo = keep("q_lo", [P, 2, S], F32R)
        k_hi = keep("k_hi", [P, KV_HEADS, S], F32R)
        k_lo = keep("k_lo", [P, KV_HEADS, S], F32R)
        v_hi = keep("v_hi", [P, KV_HEADS, QT, P], F32R)
        v_lo = keep("v_lo", [P, KV_HEADS, QT, P], F32R)
        pt_hi = keep("pt_hi", [P, QT, 2 * P], F32R)
        pt_lo = keep("pt_lo", [P, QT, 2 * P], F32R)
        prob = keep("prob", [P, 2, S])
        rope_sb = keep("rope_sb", [P, 2, S])
        sz_q = keep("sz_q", [P, 2, S])
        q_raw = keep("q_raw", [P, 2, S])
        sq_b = keep("sq_b", [P, S])
        rstd_b = keep("rstd_b", [P, S])
        y_b = keep("y_b", [P, 2, S])
        stat_b = keep("stat_b", [P, 2, 4])
        at[0] = phase_start
        xc = keep("xc", [P, KT, S])
        at[0] += 2 * 4 * S
        sq_c = keep("sq_c", [P, 2, S])
        rstd_c = keep("rstd_c", [P, S])
        rstd_g = keep("rstd_g", [P, S])
        acc_c = keep("acc_c", [P, S])
        acc_g = keep("acc_g", [P, S])
        last_g = keep("last_g", [P, S])
        at[0] = phase_start
        u_rows = keep("u_rows", [P, KT, S + 4])
        c_rows = keep("c_rows", [P, KT, S])
        bdt = nc.alloc_sbuf_tensor_at("bdt", [P, 3 * KT, P], F32, offset=at[0])
        conv_acc = keep("conv_acc", [P, 2, S + 2 * PAD])
        pool_pad = keep("pool_pad", [P, S + 2 * PAD])
        pooled = keep("pooled", [P, 2, S])
        sz_p = keep("sz_p", [P, S])
        y_d_start = at[0]
        y_d = keep("y_d", [P, 2, S])
        pw_sb = keep("pw_sb", [P, 2, 2, MD])
        gw_sb = keep("gw_sb", [P, 3 * KT, 16])
        gw_eff = keep("gw_eff", [P, 2 * KT, 16])
        blocks_d = keep("blocks_d", [P, 3, KT, 4])
        bmask_d = keep("bmask_d", [P, 32])
        edge_sb = keep("edge_sb", [P, 4, 2, PAD])
        gate_rows = keep("gate_rows", [16, S])
        gb_sb = keep("gb_sb", [16, 1])
        at[0] = op_start
        q_t = keep("q_t", [P, 2, 2, S])
        kw_t = keep("kw_t", [P, 2, 2, S])
        k_tok = keep("k_tok", [P, 2, CH, MD])
        state = keep("state", [P, NDIR, 2, VE])
        num_a = keep("num_a", [P, NDIR, VE])
        assert at[0] <= op_start + 4 * S * (2 * KT - 2)
        at[0] = op_start + 4 * S * (2 * KT - 2)
        mz_sb = keep("mz_sb", [P, 2, S])
        assert at[0] <= phase_start
        h_tok = [nc.alloc_sbuf_tensor_at(f"h_tok{h}", [P, CH, MD], F32, offset=phase_start + 8 * h * S)
                 for h in range(MH)]
        at[0] = phase_start + 4 * KT * (2 * S + 4)
        bd = keep("bd", [P, 3, KT, P])
        blocks_e = keep("blocks_e", [P, 3, KT, 4])
        bmask_e = keep("bmask_e", [P, 32])
        mask_sb = keep("mask_sb", [P, NDIR, P])
        g_tok = keep("g_tok", [P, CH, 32])
        decay_b = keep("decay_b", [P, 2 * MH, CH])
        small = keep("small", [P, NDIR, 4])
        bn6 = keep("bn6", [P, CH, 6])
        bn2 = keep("bn2", [P, CH, 2])
        rstd_h = keep("rstd_h", [P, CH])
        rows_start = at[0]
        i_row = keep("i_row", [36, S])
        f_row = keep("f_row", [36, S])
        assert at[0] <= y_d_start
        at[0] = y_d_start + 4 * 2 * S
        t_row = keep("t_row", [36, S])
        b_row = keep("b_row", [36, S])
        reset_row = keep("reset_row", [36, S])
        a_row = keep("a_row", [36, S])
        mp_row = keep("mp_row", [36, CH])
        end_row = keep("end_row", [36, CH])
        dec_tmp = keep("dec_tmp", [36, CH])
        dec_row = keep("dec_row", [36, CH])
        at[0] = rows_start
        g_rows = keep("g_rows", [32, S])
        at[0] = rows_start
        v_tok = keep("v_tok", [P, 2, CH, VE])
        k_w = keep("k_w", [P, NDIR, MD])
        out_e = keep("out_e", [P, 2, S])
        bm_b = keep("bm_b", [P, NDIR, S])
        at[0] = op_start
        o_hi = keep("o_hi", [P, 2 * KT, S], F32R)
        assert at[0] == phase_start
        xf = keep("xf", [P, KT, S])
        o_lo = keep("o_lo", [P, 2 * KT, S], F32R)
        sq_f = keep("sq_f", [P, 2, S])
        acc_f = keep("acc_f", [P, S])
        rstd_f = keep("rstd_f", [P, S])

        pair = [ctx.enter_context(nc.psum_tensor(f"pair{i}", [P, S], F32)) for i in range(2)]
        aux = ctx.enter_context(nc.psum_tensor("aux", [P, 4 * HALF], F32))

        consts = sem("consts")
        tables_in, rope_in = sem("tables_in"), sem("rope_in")
        ready0 = sem("ready0")
        w_loaded = [sem(f"w_loaded{i}") for i in range(3)]
        w_hi_done = sem("w_hi_done")
        w_split = sem("w_split")
        unit_done = sem("unit_done")
        pair_free = [sem(f"pair_free{i}") for i in range(2)]
        x_loaded = [sem(f"x_loaded{i}") for i in range(KT)]
        x_done = sem("x_done")
        sq_ready, stat_done, rstd_ready = sem("sq_ready"), sem("stat_done"), sem("rstd_ready")
        acc_ready = sem("acc_ready")
        r_stored, r_loaded = sem("r_stored"), sem("r_loaded")
        low_made = sem("low_made")
        hn_ready, hi_ready, op_ready = sem("hn_ready"), sem("hi_ready"), sem("op_ready")
        x_stored = sem("x_stored")
        y_in = [sem(f"y_in{i}") for i in range(KT)]
        y_made = sem("y_made")
        y_stored = [sem(f"y_stored{i}") for i in range(2)]
        dve_step, act_step = sem("dve_step"), sem("act_step")
        bu_ready, parts_ready, fft1_done = sem("bu_ready"), sem("parts_ready"), sem("fft1_done")
        spec_ready, fft2_done = sem("spec_ready"), sem("fft2_done")
        ax_ready, prod_done, szb_ready, sza_ready = sem("ax_ready"), sem("prod_done"), sem("szb_ready"), sem("sza_ready")
        qsq, qstat, qrstd, qr_ready = sem("qsq"), sem("qstat"), sem("qrstd"), sem("qr_ready")
        raw_ready = sem("raw_ready")
        qhi_ready, q_ready = sem("qhi_ready"), sem("q_ready")
        bg_done, bg_free = sem("bg_done"), sem("bg_free")
        vt_ready, vtr_done, vhi_ready, v_ready = sem("vt_ready"), sem("vtr_done"), sem("vhi_ready"), sem("v_ready")
        szq_ready, s_done, neg_ready, exp_done = sem("szq_ready"), sem("s_done"), sem("neg_ready"), sem("exp_done")
        p_ready, t_done, pt_hi_ready, pt_ready = sem("p_ready"), sem("t_done"), sem("pt_hi_ready"), sem("pt_ready")
        pv_done, yq_done = sem("pv_done"), sem("yq_done")
        consts_d, pads_ready = sem("consts_d"), sem("pads_ready")
        last_g_made = sem("last_g_made")
        bdt_ready, weff_done, weff_ready = sem("bdt_ready"), sem("weff_done"), sem("weff_ready")
        u_ready, conv_done, c_ready, gate_done, gate_ready, gate_stored = (
            sem("u_ready"), sem("conv_done"), sem("c_ready"), sem("gate_done"), sem("gate_ready"), sem("gate_stored"))
        px_ready, pooled_ready, mix_done, szp_ready = sem("px_ready"), sem("pooled_ready"), sem("mix_done"), sem("szp_ready")
        pw_loaded = [sem(f"pw_loaded{i}") for i in range(2)]
        mz_ready = sem("mz_ready")
        mz_stored = [sem(f"mz_stored{i}") for i in range(2)]
        consts_e, rows_in = sem("consts_e"), sem("rows_in")
        rows_clear, bm_made, row_act, row_dve = sem("rows_clear"), sem("bm_made"), sem("row_act"), sem("row_dve")
        g_made, g_moved, decay_in = sem("g_made"), sem("g_moved"), sem("decay_in")
        gt_done, gt_ready, bd_ready = sem("gt_done"), sem("gt_ready"), sem("bd_ready")
        bm_loaded, bm_ready = sem("bm_loaded"), sem("bm_ready")
        prep_done, prep_act, ones_made = sem("prep_done"), sem("prep_act"), sem("ones_made")
        st_done, e_ready, wt_made, ab_done = sem("st_done"), sem("e_ready"), sem("wt_made"), sem("ab_done")
        kw_ready, upd_done, state_ready, acp_ready, h_done = (
            sem("kw_ready"), sem("upd_done"), sem("state_ready"), sem("acp_ready"), sem("h_done"))
        ht_read = sem("ht_read")
        bn_ready, rh_ready, ln_done, ht_done = sem("bn_ready"), sem("rh_ready"), sem("ln_done"), sem("ht_done")
        mz_in = [sem(f"mz_in{i}") for i in range(2)]
        out_made, out_stored = sem("out_made"), [sem(f"out_stored{i}") for i in range(2)]

        def job_of(unit):
            return unit if unit < BASE[5] else BASE[5] + (unit - BASE[5]) // 2

        def last_unit(job):
            return job if job < BASE[5] else BASE[5] + 2 * (job - BASE[5]) + 1

        def wait_job(eng, job):
            eng.wait_ge(unit_done, last_unit(job) + 1)

        OP0 = {"even": 0, "y1": KT, "odd": 2 * KT, "y2": 3 * KT, "in": 4 * KT, "y3": 5 * KT}
        UNIT0 = {"even": BASE[0], "y1": BASE[1], "odd": BASE[2], "y2": BASE[3], "in": BASE[4], "y3": BASE[5]}
        Y0 = {"y1": 0, "y2": KT, "y3": 2 * KT}

        Y_DRAM = {"y1": y1_dram, "y2": y2_dram, "y3": y3_dram}
        THROUGH = {"y1": KT - 2, "y2": KT - 1, "y3": 2 * KT - 2}
        STORED = {"y1": (0, 0), "y2": (3, 3), "y3": (7, 6)}

        def stored(layer, n):
            return 16 * (STORED[layer][n % 2] + n // 2 + 1)

        def back(layer, k):
            before = {"y1": 0, "y2": int(k < THROUGH["y1"]),
                      "y3": int(k % KT < THROUGH["y1"]) + int(k % KT < THROUGH["y2"])}[layer]
            return 16 * (before + k // KT + 1)

        def side_bank(h, n):
            if h >= 1:
                return pair[1][:, 0:HALF]
            return (pair[1][:, 0:HALF], pair[1][:, HALF:S], aux[:, 0:HALF], aux[:, HALF:S],
                    pair[0][:, 0:HALF], pair[0][:, HALF:S])[n]

        PREP_AT, SCORES_AT, WEIGHTS_AT, LN_AT, TURN_AT = 0, 8, 9, 2, (11, 13)
        ROWS_AT = 2

        block = ctx.enter_context(nc.Block())

        @block.sync
        def _(sp):
            loaded = [0]

            def weights_to(n):
                for u in range(loaded[0], min(n, UNITS)):
                    if u >= 3:
                        sp.wait_ge(w_split, u - 2)
                    sp.dma_start(w_raw[:, u % 3, :], weight_units[u]).then_inc(w_loaded[u % 3], 16)
                loaded[0] = max(loaded[0], n)

            def store_y(layer, n, buf):
                if n < THROUGH[layer]:
                    sp.wait_ge(y_made, Y0[layer] + n + 1)
                    sp.dma_start(Y_DRAM[layer][n], buf[:, n % 2, :]).then_inc(y_stored[n % 2], 16)

            def load_y(layer, k, buf, slots):
                sp.wait_ge(y_stored[k % 2], stored(layer, k))
                if k >= slots:
                    sp.wait_ge(op_ready, OP0[layer] + k - slots + 1)
                sp.dma_start(buf[:, k % slots, :], Y_DRAM[layer][k]).then_inc(y_in[k % KT], 16)

            for k in range(KT):
                sp.dma_start(xa[:, k, :], x_t[k]).then_inc(x_loaded[k], 16)
                if k == KT // 2:
                    weights_to(1)
            sp.dma_start(par[:, :], channel_params).then_inc(consts, 16)
            weights_to(2)
            sp.dma_start(ident[:, :], ident_in).then_inc(consts, 16)
            sp.dma_start(tab_d[:, :, :], dft_d).then_inc(tables_in, 16)
            sp.dma_start(tab_s[:, :, :, :], dft_s).then_inc(tables_in, 16)
            for j in range(AB):
                weights_to(6 * j + 9)
                store_y("y1", 2 * j, y_a)
                store_y("y1", 2 * j + 1, y_a)
                if j == 2:
                    sp.wait_ge(op_ready, KT)
                    for k in range(THROUGH["y1"]):
                        load_y("y1", k, stage_y, 6)
            weights_to(BASE[2] + 3)
            for k in range(KT):
                sp.wait_ge(x_done, k + 1)
                sp.dma_start(x1_dram[k], xa[:, k, :]).then_inc(x_stored, 16)
            sp.wait_ge(op_ready, OP0["odd"] + KT)
            sp.wait_ge(x_stored, 16 * KT)
            sp.dma_start(rope_sb[:, :, :], rope).then_inc(rope_in, 16)
            for h in range(HEADS):
                weights_to(min(BASE[2] + 11 + 2 * h, BASE[3] + 3))
                store_y("y2", h, y_b)
                if h == HEADS - 2:
                    sp.wait_ge(q_ready, KV_HEADS + HEADS)
                    for k in range(THROUGH["y2"]):
                        load_y("y2", k, q_raw, 2)
                    sp.wait_ge(s_done, QT * HEADS)
                    for k in range(KT):
                        sp.dma_start(xc[:, k, :], x1_dram[k]).then_inc(x_loaded[k], 16)
            weights_to(BASE[3] + 4)
            sp.wait_ge(op_ready, OP0["y2"] + KT)
            sp.dma_start(blocks_d[:, :, :, :], qkv_blocks[1]).then_inc(consts_d, 16)
            sp.dma_start(bmask_d[:, :], block_mask).then_inc(consts_d, 16)
            sp.dma_start(gw_sb[:, :, :], gate_w).then_inc(consts_d, 16)
            sp.dma_start(gb_sb[:, :], gate_b).then_inc(consts_d, 16)
            sp.dma_start(edge_sb[:, :, :, :], edge).then_inc(consts_d, 16)
            for k in range(KT):
                weights_to(BASE[3] + 5 + k)
                sp.wait_ge(x_done, KT + k + 1)
                sp.dma_start(x2_dram[k], xc[:, k, :]).then_inc(x_stored, 16)
            sp.wait_ge(rstd_ready, 4)
            sp.dma_start(r_dram, rstd_c[:, :]).then_inc(r_stored, 16)
            for g in range(2):
                sp.dma_start(pw_sb[:, g, :, :], pool_w[g]).then_inc(pw_loaded[g], 16)
            for g in range(4):
                weights_to(BASE[4] + 15 + 4 * g)
                store_y("y3", 2 * g, y_d)
                store_y("y3", 2 * g + 1, y_d)
                if g + 2 < 4:
                    sp.dma_start(pw_sb[:, g % 2, :, :], pool_w[g + 2]).then_inc(pw_loaded[g % 2], 16)
                if g == 2:
                    sp.wait_ge(gate_ready, 1)
                    sp.dma_start(gate_dram[:, :], gate_rows[:, :]).then_inc(gate_stored, 16)
            def load_bm(h):
                if h >= 1:
                    sp.wait_ge(wt_made, NDIR * h)
                for d in range(NDIR):
                    sp.dma_start(bm_b[:, d, :], bm_dram[MH * d + h:MH * d + h + 1, :]
                                 .broadcast_to([P, S])).then_inc(bm_loaded, 16)

            sp.wait_ge(y_made, Y0["y3"] + KT)
            sp.wait_ge(gate_stored, 16)
            sp.wait_ge(rows_clear, 2)
            for d in range(NDIR):
                sp.dma_start(i_row[32 * d:32 * d + MH, :],
                             gate_dram[MH * d:MH * d + MH, :]).then_inc(rows_in, 16)
                sp.dma_start(f_row[32 * d:32 * d + MH, :],
                             gate_dram[8 + MH * d:8 + MH * d + MH, :]).then_inc(rows_in, 16)
            sp.dma_start(reset_row[:, :], reset_mask).then_inc(rows_in, 16)
            sp.dma_start(blocks_e[:, :, :, :], qkv_blocks[0]).then_inc(consts_e, 16)
            sp.dma_start(bmask_e[:, :], block_mask).then_inc(consts_e, 16)
            sp.dma_start(mask_sb[:, :, :], masks).then_inc(consts_e, 16)
            for t in range(KT):
                weights_to(min(BASE[4] + 28 + t, BASE[5] + 3))
                sp.wait_ge(mz_ready, t + 1)
                sp.dma_start(mz_dram[t], y_d[:, t % 2, :]).then_inc(mz_stored[t % 2], 16)
                if t == ROWS_AT:
                    weights_to(BASE[4] + 28 + t + 1)
                    sp.wait_ge(bm_made, 1)
                    for d in range(NDIR):
                        sp.dma_start(bm_dram[MH * d:MH * d + MH, :],
                                     reset_row[32 * d:32 * d + MH, :]).then_inc(g_moved, 16)
                    sp.wait_ge(g_made, 1)
                    for d in range(NDIR):
                        for n, row in enumerate((a_row, t_row, f_row, b_row)):
                            sp.dma_start(g_rows[8 * n + MH * d:8 * n + MH * d + MH, :],
                                         row[32 * d:32 * d + MH, :]).then_inc(g_moved, 16)
                        sp.dma_start(decay_dram[MH * d:MH * d + MH, :],
                                     dec_row[32 * d:32 * d + MH, :]).then_inc(g_moved, 16)
                if t == KT - 3:
                    sp.wait_ge(g_moved, 16 * 12)
                    sp.dma_start(decay_b[:, :, :].rearrange("p r c -> p (r c)"),
                                 decay_dram.rearrange("r c -> (r c)").rearrange("(a n) -> a n", a=1)
                                 .broadcast_to([P, 2 * MH * CH])).then_inc(decay_in, 16)
                if t == KT - 2:
                    sp.wait_ge(gt_ready, 1)
                    load_bm(0)
            def load_mz(h):
                for t in range(2):
                    if h >= 1:
                        sp.wait_ge(y_made, Y0["y3"] + KT + 2 * h + t - 1)
                    sp.dma_start(mz_sb[:, t, :], mz_dram[2 * h + t]).then_inc(mz_in[t], 16)

            sp.wait_ge(unit_done, BASE[5])
            sp.wait_ge(mz_stored[0], 16 * KT // 2)
            sp.wait_ge(mz_stored[1], 16 * KT // 2)
            load_mz(0)
            for h in range(MH):
                if h + 1 < MH:
                    load_bm(h + 1)
                else:
                    sp.wait_ge(prep_done, 8 * MH)
                    sp.wait_ge(y_made, Y0["y3"] + KT + 2 * (MH - 2))
                    for k in range(4):
                        load_y("y3", k, xf, KT)
                if h >= 1:
                    for t in range(2):
                        store_y("y3", KT + 2 * (h - 1) + t, out_e)
                    load_mz(h)
            for k in range(4, 6):
                load_y("y3", k, xf, KT)
            sp.wait_ge(ht_done, 2 * MH)
            for k in range(6, KT):
                load_y("y3", k, xf, KT)
            for k in range(KT, THROUGH["y3"]):
                load_y("y3", k, xf, KT)
            for k in range(KT):
                sp.wait_ge(op_ready, OP0["y3"] + max(q for q in range(THROUGH["y3"]) if q % KT == k) + 1)
                sp.dma_start(xf[:, k, :], x2_dram[k]).then_inc(x_loaded[k], 16)
            sp.wait_ge(op_ready, OP0["y3"] + 2 * KT)
            sp.wait_ge(r_stored, 16)
            sp.dma_start(rstd_f[:, :], r_dram).then_inc(r_loaded, 16)
            weights_to(UNITS)
            for k in range(KT):
                sp.wait_ge(out_made, k + 1)
                sp.dma_start(out[k], xf[:, k, :]).then_inc(out_stored[k % 2], 16)
            sp.wait_ge(out_stored[0], 16 * KT // 2)
            sp.wait_ge(out_stored[1], 16 * KT // 2)

        @block.gpsimd
        def _(pool):
            def split(u):
                pool.wait_ge(w_loaded[u % 3], 16 * (u // 3 + 1))
                if u >= 2:
                    pool.wait_ge(unit_done, u - 1)
                    pool.wait_ge(w_split, u - 1)
                pool.tensor_copy(w_hi[:, u % 2, :], w_raw[:, u % 3, :]).then_inc(w_hi_done, 1)
                pool.wait_ge(w_hi_done, u + 1)
                pool.tensor_tensor(w_lo[:, u % 2, :], w_raw[:, u % 3, :], w_hi[:, u % 2, :],
                                   ALU.subtract).then_inc(w_split, 1)

            def mask(h):
                pool.wait_ge(bm_loaded, 32 * (h + 1))
                for d in range(NDIR):
                    rows = bm_b[:, d, :].rearrange("p (c s) -> p c s", c=CH)
                    pool.tensor_tensor(rows, rows, mask_sb[:, d, :].unsqueeze(1).broadcast_to([P, CH, P]),
                                       ALU.add).then_inc(bm_ready, 1)

            def norm_low(n, op0):
                for k in range(1, KT, 2):
                    pool.wait_ge(hi_ready, op0 + k + 1)
                    pool.tensor_tensor(op_lo[:, k, :], stage_n[:, k % 4, :], op_hi[:, k, :],
                                       ALU.subtract).then_inc(low_made, 1)

            NORM_BEFORE = {BASE[0]: (0, OP0["even"]), BASE[2]: (1, OP0["odd"]), BASE[4]: (2, OP0["in"])}
            for u in range(BASE[5]):
                split(u)
                if u - 1 in NORM_BEFORE:
                    norm_low(*NORM_BEFORE[u - 1])
            pool.wait_ge(consts_e, 48)
            mask(0)
            for u in range(BASE[5], BASE[5] + 2):
                split(u)
            for h in range(1, MH):
                mask(h)
            for u in range(BASE[5] + 2, UNITS):
                split(u)

        @block.tensor
        def _(pe):
            def unit(u, job, hi, lo, layer, kt0=0, wait_operand=False, first=True, last=True):
                pe.wait_ge(w_split, u + 1)
                if first and job >= 2:
                    pe.wait_ge(pair_free[job % 2], job // 2)
                acc = pair[job % 2]
                for k in range(KT):
                    if wait_operand:
                        pe.wait_ge(op_ready, OP0[layer] + kt0 + k + 1)
                    wh = w_hi[:, u % 2, k * P:(k + 1) * P]
                    wl = w_lo[:, u % 2, k * P:(k + 1) * P]
                    for n, (w, x) in enumerate(((wh, hi), (wh, lo), (wl, hi))):
                        for half in range(2):
                            cols = slice(half * HALF, (half + 1) * HALF)
                            mm = pe.matmul(acc[:, cols], w, x[:, kt0 + k, cols],
                                           start=(first and k == 0 and n == 0),
                                           stop=(last and k == KT - 1 and n == 2))
                mm.then_inc(unit_done, 1)

            def norm_stats(n, acc, last, o, last_ready=None):
                pe.wait_ge(acc_ready, (KT - 2) * (n + 1))
                for half in range(2):
                    cols = slice(half * HALF, (half + 1) * HALF)
                    pe.matmul(o[:, cols], ones[:, :], acc[:, cols], start=True, stop=False)
                if last_ready is None:
                    pe.wait_ge(sq_ready, KT * (n + 1))
                else:
                    pe.wait_ge(last_ready, 1)
                for half in range(2):
                    cols = slice(half * HALF, (half + 1) * HALF)
                    mm = pe.matmul(o[:, cols], ones[:, :], last[:, cols], start=False, stop=True)
                mm.then_inc(stat_done, 1)

            pe.wait_ge(ready0, 3)
            norm_stats(0, acc_a, sq_a[:, (KT - 1) % 2, :], aux[:, 0:S])

            def fft_channels(j):
                pe.wait_ge(parts_ready, j + 1)
                if j == 0:
                    pe.wait_ge(tables_in, 32)
                    pe.wait_ge(consts, 32)
                    pe.wait_ge(rstd_ready, 1)
                else:
                    pe.wait_ge(y_made, 2 * j - 1)
                for k1 in range(RADIX):
                    o = aux[:, k1 * 2 * P:(k1 + 1) * 2 * P]
                    if k1 % 4 == 0:
                        mm = pe.matmul(o, parts[:, k1 // 4, :], tab_d[:, 0, :], start=True, stop=True)
                    else:
                        r = min(k1, RADIX - k1)
                        pe.matmul(o, parts[:, 2 * r, :], tab_d[:, 0, :], start=True, stop=False)
                        mm = pe.matmul(o, parts[:, 2 * r + 1, :], tab_d[:, 1 if k1 < 4 else 2, :],
                                       start=False, stop=True)
                mm.then_inc(fft1_done, 1)

            def fft_time(j):
                pe.wait_ge(spec_ready, j + 1)
                for k1 in range(RADIX):
                    o = aux[:, k1 * P:(k1 + 1) * P]
                    pe.matmul(o, spec[:, k1, 0:P], tab_s[:, 0, k1, :], start=True, stop=False)
                    mm = pe.matmul(o, spec[:, k1, P:2 * P], tab_s[:, 1, k1, :], start=False, stop=True)
                mm.then_inc(fft2_done, 1)

            for j in range(AB):
                for i in range(6):
                    u = 6 * j + i
                    unit(u, u, op_hi, op_lo, "even", wait_operand=(u == 0))
                    if i == 1:
                        fft_channels(j)
                    if i == 2:
                        fft_time(j)
            for e in range(KT):
                unit(BASE[1] + e, BASE[1] + e, op_hi, op_lo, "y1", wait_operand=(e == 0))
            norm_stats(1, acc_a, sq_a[:, (KT - 1) % 2, :], aux[:, 0:S])

            def v_transpose(g):
                pe.wait_ge(vt_ready, g + 1)
                if g >= 1:
                    pe.wait_ge(v_ready, g)
                for t in range(QT):
                    mm = pe.transpose(aux[:, 2 * HALF + t * P:2 * HALF + (t + 1) * P],
                                      prob[:, g, t * P:(t + 1) * P], ident[:, :])
                mm.then_inc(vtr_done, 1)

            for g in range(KV_HEADS):
                unit(BASE[2] + 2 * g, BASE[2] + 2 * g, op_hi, op_lo, "odd", wait_operand=(g == 0))
                unit(BASE[2] + 2 * g + 1, BASE[2] + 2 * g + 1, op_hi, op_lo, "odd")
                pe.wait_ge(qsq, g + 1)
                if g == 0:
                    pe.wait_ge(rstd_ready, 2)
                else:
                    pe.wait_ge(qrstd, g)
                for half in range(2):
                    cols = slice(half * HALF, (half + 1) * HALF)
                    mm = pe.matmul(aux[:, cols], ones[:, :], sq_b[:, cols], start=True, stop=True)
                mm.then_inc(qstat, 1)
                v_transpose(g)

            def piece(h, which, c, part):
                u = BASE[2] + 4 + 2 * h + which
                cols = slice(c * HALF, (c + 1) * HALF)
                bank = side_bank(h, 4 * which + c)
                if part == 0:
                    pe.wait_ge(w_split, u + 1)
                    if h >= 1:
                        pe.wait_ge(bg_free, 6 * h + 4 * which + c)
                for k in range(4 * part, 4 * part + 4):
                    wh = w_hi[:, u % 2, k * P:(k + 1) * P]
                    wl = w_lo[:, u % 2, k * P:(k + 1) * P]
                    for n, (w, x) in enumerate(((wh, op_hi), (wh, op_lo), (wl, op_hi))):
                        mm = pe.matmul(bank, w, x[:, k, cols], start=(k == 0 and n == 0),
                                       stop=(k == KT - 1 and n == 2))
                if part == 1:
                    mm.then_inc(bg_done if c == 0 else unit_done, 1)

            def q_stats(h, c):
                pe.wait_ge(qsq, KV_HEADS + 2 * h + c + 1)
                if h >= 1:
                    pe.wait_ge(bg_free, 6 * h + 2 + c)
                else:
                    pe.wait_ge(qrstd, KV_HEADS)
                pe.matmul(side_bank(h, 2 + c), ones[:, :], sq_b[:, c * HALF:(c + 1) * HALF],
                          start=True, stop=True).then_inc(qstat, 1)

            def scores(t):
                h, i = t // QT, t % QT
                if i == 0:
                    pe.wait_ge(q_ready, KV_HEADS + h + 1)
                    pe.wait_ge(v_ready, KV_HEADS)
                if t >= 2:
                    pe.wait_ge(exp_done, t - 1)
                b = (t % 2) * S
                g = h // GROUP
                rows = slice(i * P, (i + 1) * P)
                for n, (a, k) in enumerate(((q_hi, k_hi), (q_hi, k_lo), (q_lo, k_hi))):
                    for half in range(2):
                        cols = slice(half * HALF, (half + 1) * HALF)
                        mm = pe.matmul(aux[:, b + half * HALF:b + (half + 1) * HALF],
                                       a[:, h % 2, rows], k[:, g, cols],
                                       start=(n == 0), stop=(n == 2))
                mm.then_inc(s_done, 1)

            def turn(t):
                pe.wait_ge(p_ready, t + 1)
                if t >= 1:
                    pe.wait_ge(pt_ready, t)
                else:
                    pe.wait_ge(bg_free, 6)
                for k in range(QT):
                    mm = pe.transpose(pair[0][:, k * P:(k + 1) * P],
                                      prob[:, t % 2, k * P:(k + 1) * P], ident[:, :])
                mm.then_inc(t_done, 1)

            def weigh_values(m):
                pe.wait_ge(pt_ready, 2 * m + 2)
                if m >= 1:
                    pe.wait_ge(yq_done, m)
                g = m // 4 // GROUP
                for k in range(QT):
                    for n, (v, p) in enumerate(((v_hi, pt_hi), (v_hi, pt_lo), (v_lo, pt_hi))):
                        mm = pe.matmul(pair[1][:, HALF:HALF + 2 * P], v[:, g, k, :], p[:, k, :],
                                       start=(k == 0 and n == 0), stop=(k == QT - 1 and n == 2))
                mm.then_inc(pv_done, 1)

            pe.wait_ge(pair_free[0], (BASE[2] + 4) // 2)
            pe.wait_ge(pair_free[1], (BASE[2] + 4) // 2)
            for c in range(2):
                piece(0, 0, c, 0)
                piece(0, 0, c, 1)
            piece(0, 1, 0, 0)
            q_stats(0, 0)
            q_stats(0, 1)
            piece(0, 1, 0, 1)
            piece(0, 1, 1, 0)
            piece(0, 1, 1, 1)
            scores(0)
            scores(1)
            BESIDE = {0: [(0, 0, 0)], 1: [(0, 0, 1)], 2: [(0, 1, 0)], 3: [(0, 1, 1)],
                      5: [(1, 0, 0), (1, 0, 1)], 6: [(1, 1, 0)], 7: [(1, 1, 1)]}
            for t in range(QT * HEADS):
                h, i = t // QT, t % QT
                turn(t)
                if h + 1 < HEADS and i == 4:
                    q_stats(h + 1, 0)
                if t + 2 < QT * HEADS:
                    scores(t + 2)
                if h + 1 < HEADS:
                    if i == 4:
                        q_stats(h + 1, 1)
                    for which, c, part in BESIDE.get(i, []):
                        piece(h + 1, which, c, part)
                if i % 2:
                    weigh_values(t // 2)
            pe.wait_ge(pt_ready, QT * HEADS)
            pe.wait_ge(yq_done, 4 * HEADS)
            for e in range(KT):
                unit(BASE[3] + e, BASE[3] + e, op_hi, op_lo, "y2", wait_operand=(e == 0))
                if e == 1:
                    pe.wait_ge(bdt_ready, 3 * KT)
                    for i in range(3 * KT):
                        t, which = i // 3, i % 3
                        pos = (t if which < 2 else KT + t) * 16
                        mm = pe.matmul(aux[:, pos:pos + 16], bdt[:, i, :], gw_sb[:, which * KT + t, :],
                                       start=(which != 1), stop=(which != 0))
                    mm.then_inc(weff_done, 1)
            pe.wait_ge(weff_ready, 1)
            norm_stats(2, acc_g, last_g, aux[:, S:2 * S], last_g_made)
            norm_stats(2, acc_c, sq_c[:, (KT - 1) % 2, :], aux[:, 0:S])

            def gates(t):
                for half in range(2):
                    cols = slice(half * HALF, (half + 1) * HALF)
                    o = aux[0:16, 2 * HALF + half * HALF:2 * HALF + (half + 1) * HALF]
                    if t == 0:
                        pe.wait_ge(rstd_ready, 4)
                    pe.wait_ge(u_ready, t + 1)
                    pe.matmul(o, gw_eff[:, KT + t, :], u_rows[:, t, 2 + half * HALF:2 + (half + 1) * HALF],
                              start=(t == 0), stop=False)
                    pe.wait_ge(c_ready, t + 1)
                    mm = pe.matmul(o, gw_eff[:, t, :], c_rows[:, t, cols], start=False, stop=(t == KT - 1))
                if t == KT - 1:
                    mm.then_inc(gate_done, 1)

            for t in range(KT):
                unit(BASE[4] + t, BASE[4] + t, op_hi, op_lo, "in", wait_operand=(t == 0))
                if t >= 2:
                    gates(t - 2)
            for g in range(4):
                for i in range(4):
                    unit(BASE[4] + 8 + 4 * g + i, BASE[4] + 8 + 4 * g + i, op_hi, op_lo, "in")
                    if g == 0 and i < 2:
                        gates(KT - 2 + i)
                    if i >= 2:
                        m = i - 2
                        pe.wait_ge(pooled_ready, 2 * g + 2)
                        pe.wait_ge(pw_loaded[g % 2], 16 * (g // 2 + 1))
                        if 2 * g + m >= 1:
                            pe.wait_ge(y_made, Y0["y3"] + 2 * g + m)
                        for half in range(2):
                            cols = slice(half * HALF, (half + 1) * HALF)
                            for k in range(2):
                                mm = pe.matmul(aux[:, cols], pw_sb[:, g % 2, k, m * P:(m + 1) * P],
                                               pooled[:, k, cols], start=(k == 0), stop=(k == 1))
                        mm.then_inc(mix_done, 1)
            for t in range(KT):
                unit(BASE[4] + 24 + t, BASE[4] + 24 + t, op_hi, op_lo, "in")
                if t == KT - 2:
                    pe.wait_ge(g_moved, 16 * 12)
                    for c in range(CH):
                        mm = pe.transpose(aux[:, c * 32:(c + 1) * 32], g_rows[:, c * P:(c + 1) * P],
                                          ident[0:32, 0:32])
                    mm.then_inc(gt_done, 1)

            pe.wait_ge(bd_ready, 1)
            pe.wait_ge(gt_ready, 1)
            pe.wait_ge(pair_free[(BASE[5] - 1) % 2], (BASE[5] - 1) // 2 + 1)
            pe.wait_ge(pair_free[(BASE[5] - 2) % 2], (BASE[5] - 2) // 2 + 1)

            def prepare(h, n):
                if h == 0 and n >= 2:
                    pe.wait_ge(prep_act, n - 1)
                if h >= 1 and n >= 1:
                    pe.wait_ge(prep_act, 8 * h + n)
                if h >= 1 and n == 0:
                    pe.wait_ge(wt_made, NDIR * h)
                    if h >= 3:
                        pe.wait_ge(ht_read, 2 * (h - 2))
                o = aux[:, S:2 * S] if h == 0 and n % 2 else aux[:, 0:S]
                if n < 4:
                    for half in range(2):
                        cols = slice(half * HALF, (half + 1) * HALF)
                        mm = pe.matmul(o[:, cols], bd[:, n // 2, 2 * h + n % 2, :],
                                       c_rows[:, 2 * h + n % 2, cols], start=True, stop=True)
                else:
                    for c in range(4):
                        chunk = 4 * (n % 2) + c
                        for i in range(2):
                            if n < 6:
                                x = c_rows[:, 2 * h + i, chunk * P:(chunk + 1) * P]
                            else:
                                x = u_rows[:, 2 * h + i, 2 + chunk * P:2 + (chunk + 1) * P]
                            mm = pe.matmul(o[:, c * MD + i * P:c * MD + (i + 1) * P], x,
                                           bd[:, 1 if n < 6 else 2, 2 * h + i, :], start=True, stop=True)
                mm.then_inc(prep_done, 1)

            def head_scores(h):
                pe.wait_ge(prep_act, 8 * h + 8)
                for c in range(CH):
                    for i in range(2):
                        mm = pe.matmul(aux[:, c * P:(c + 1) * P], kw_t[:, h % 2, i, c * P:(c + 1) * P],
                                       q_t[:, h % 2, i, c * P:(c + 1) * P], start=(i == 0), stop=(i == 1))
                mm.then_inc(st_done, 1)

            def turn_head(h, i, o):
                pe.wait_ge(ln_done, h + 1)
                for c in range(CH):
                    mm = pe.transpose(o[:, c * P:(c + 1) * P], h_tok[h][:, c, i * P:(i + 1) * P],
                                      ident[:, :])
                mm.then_inc(ht_done, 1)

            for n in range(8):
                prepare(0, n)
            head_scores(0)
            for h in range(MH):
                for m in range(NDIR * CH):
                    n, d = m // 2, m % 2
                    c = n if d == 0 else CH - 1 - n
                    g = NDIR * CH * h + m
                    ks = NDIR * (CH - 1) * h + m
                    if m < NDIR:
                        pe.wait_ge(wt_made, NDIR * h + m + 1)
                    if g >= 2:
                        pe.wait_ge(h_done, g - 1)
                    mm = pe.matmul(pair[0][:, d * HALF:d * HALF + VE], kw_t[:, h % 2, d, c * P:(c + 1) * P],
                                   v_tok[:, h % 2, c, :], start=True, stop=True)
                    if n >= 1:
                        pe.wait_ge(state_ready, NDIR * ((CH - 1) * h + n - 1) + d + 1)
                        for i in range(2):
                            mm = pe.matmul(pair[1][:, d * HALF:d * HALF + VE],
                                           q_t[:, h % 2, i, c * P:(c + 1) * P], state[:, d, i, :],
                                           start=(i == 0), stop=(i == 1))
                    mm.then_inc(ab_done, 1)
                    if n < CH - 1:
                        pe.wait_ge(kw_ready, ks + 1)
                        if ks >= 1:
                            pe.wait_ge(state_ready, ks)
                        for i in range(2):
                            o = aux[:, 2 * HALF + i * HALF:2 * HALF + i * HALF + VE]
                            mm = pe.matmul(o, k_w[:, d, i * P:(i + 1) * P], v_tok[:, h % 2, c, :],
                                           start=True, stop=True)
                        mm.then_inc(upd_done, 1)
                    if h + 1 < MH and PREP_AT <= m < PREP_AT + 8:
                        prepare(h + 1, m - PREP_AT)
                    if h + 1 < MH and m == SCORES_AT:
                        head_scores(h + 1)
                    if h >= 1 and m in TURN_AT:
                        if m == TURN_AT[0]:
                            pe.wait_ge(wt_made, NDIR * min(h + 2, MH))
                        else:
                            pe.wait_ge(ht_read, 2 * h - 1)
                        turn_head(h - 1, TURN_AT.index(m), aux[:, 0:S])
            pe.wait_ge(ht_read, 2 * (MH - 1))
            pe.wait_ge(state_ready, NDIR * (CH - 1) * MH)
            for c in range(CH):
                pe.wait_ge(ln_done, MH + c)
                for i in range(2):
                    mm = pe.transpose(aux[:, i * S + c * P:i * S + (c + 1) * P],
                                      h_tok[MH - 1][:, c, i * P:(i + 1) * P], ident[:, :])
            mm.then_inc(ht_done, 2)

            pe.wait_ge(acp_ready, NDIR * CH * MH)
            pe.wait_ge(h_done, NDIR * CH * MH)
            for e in range(KT):
                for i in range(2):
                    unit(BASE[5] + 2 * e + i, BASE[5] + e, o_hi, o_lo, "y3", kt0=KT * i,
                         wait_operand=(e == 0), first=(i == 0), last=(i == 1))
            norm_stats(3, acc_f, sq_f[:, (KT - 1) % 2, :], aux[:, 0:S])

        @block.scalar
        def _(act):
            link, signal = linker(act, act_step)

            def norm_squares(n, x, sq, acc, x0=None):
                for k in range(KT):
                    if x0 is None:
                        act.wait_ge(x_loaded[k], 16)
                    else:
                        act.wait_ge(x_done, x0 + k + 1)
                    if k >= 3:
                        act.wait_ge(acc_ready, (KT - 2) * n + k - 2)
                    link(act.activation(acc[:, :] if k == 0 else sq[:, k % 2, :], x[:, k, :], ACT.Square),
                         sq_ready)

            def norm_rstd(count, sums, rstd, bias=eps_col):
                link(act.activation(ln_ahead[:, :], bias[:, :], ACT.Ln, bias=bias[:, :]))
                act.wait_ge(stat_done, count)
                link(act.activation(rstd[:, :], sums, ACT.Ln, bias=bias[:, :], scale=1.0 / D))
                link(act.activation(rstd[:, :], rstd[:, :], ACT.Exp, scale=-0.5), rstd_ready)

            def split_norm(hn0, hi):
                for k in range(KT):
                    act.wait_ge(hn_ready, hn0 + k + 1)
                    link(act.activation(hi[:, k, :], stage_n[:, k % 4, :], ACT.Copy), hi_ready)

            def y_hi(layer, k, src, hi):
                act.wait_ge(unit_done, UNIT0[layer])
                if k < THROUGH[layer]:
                    act.wait_ge(y_in[k % KT], back(layer, k))
                else:
                    act.wait_ge(y_made, Y0[layer] + k + 1)
                link(act.activation(hi[:, k, :], src, ACT.Copy), hi_ready)

            act.wait_ge(ready0, 3)
            norm_squares(0, xa, sq_a, acc_a)
            norm_rstd(1, aux[:, 0:S], rstd_a)
            split_norm(0, op_hi)
            for j in range(AB):
                u = 6 * j
                wait_job(act, u)
                if j >= 1:
                    act.wait_ge(parts_ready, j)
                link(act.activation(bu[:, :, :].rearrange("p a b -> p (a b)"), pair[u % 2][:, :],
                                     ACT.Copy), bu_ready)
                signal(pair_free[u % 2])
                wait_job(act, u + 1)
                if j >= 1:
                    act.wait_ge(prod_done, j)
                link(act.activation(ax_sb[:, :], pair[(u + 1) % 2][:, :], ACT.Copy), ax_ready)
                signal(pair_free[(u + 1) % 2])
                act.wait_ge(fft1_done, j + 1)
                if j >= 1:
                    act.wait_ge(fft2_done, j)
                link(act.activation(spec[:, :, :].rearrange("p a b -> p (a b)"), aux[:, :],
                                     ACT.Copy), spec_ready)
                wait_job(act, u + 3)
                if j >= 1:
                    act.wait_ge(y_made, 2 * j - 1)
                link(act.activation(sz_b[:, :], pair[(u + 3) % 2][:, :], ACT.Silu), szb_ready)
                signal(pair_free[(u + 3) % 2])
                wait_job(act, u + 5)
                if j >= 1:
                    act.wait_ge(y_stored[1], stored("y1", 2 * j - 1))
                link(act.activation(y_a[:, 1, :], pair[(u + 5) % 2][:, :], ACT.Silu), sza_ready)
                signal(pair_free[(u + 5) % 2])
            for k in range(KT):
                y_hi("y1", k, stage_y[:, k, :] if k < THROUGH["y1"] else y_a[:, k % 2, :], op_hi)
            act.wait_ge(op_ready, OP0["y1"] + KT)
            norm_squares(1, xa, sq_a, acc_a, 0)
            norm_rstd(2, aux[:, 0:S], rstd_a)
            act.wait_ge(unit_done, BASE[2])
            split_norm(KT, op_hi)

            act.wait_ge(op_ready, OP0["odd"] + KT)
            act.wait_ge(x_stored, 16 * KT)

            def raw(n, src, cols, freed):
                if n >= 1:
                    act.wait_ge(q_ready, n)
                half = P // 2
                link(act.activation(q_raw[:, 0, cols], src, ACT.Copy))
                signal(freed)
                link(act.activation(sq_b[:, cols], q_raw[:, 0, cols], ACT.Square), qsq)
                link(act.activation(q_raw[0:half, 1, cols], q_raw[half:P, 0, cols], ACT.Copy))
                link(act.activation(q_raw[half:P, 1, cols], q_raw[0:half, 0, cols], ACT.Copy))
                signal(raw_ready)

            def head_rstd():
                link(act.activation(rstd_b[:, :], rstd_b[:, :], ACT.Exp, scale=-0.5), qrstd)

            def head_ln(src, cols):
                link(act.activation(rstd_b[:, cols], src, ACT.Ln, bias=eps_col[:, :], scale=1.0 / P))

            def split_hi(r, dst, cols):
                act.wait_ge(qr_ready, r + 1)
                link(act.activation(dst, q_raw[:, 0, cols], ACT.Copy), qhi_ready)

            whole = slice(0, S)
            for g in range(KV_HEADS):
                u = BASE[2] + 2 * g
                wait_job(act, u)
                raw(g, pair[u % 2][:, :], whole, pair_free[u % 2])
                u = BASE[2] + 2 * g + 1
                wait_job(act, u)
                link(act.activation(prob[:, g, :], pair[u % 2][:, :], ACT.Copy), vt_ready)
                signal(pair_free[u % 2])
                act.wait_ge(qstat, g + 1)
                head_ln(aux[:, 0:S], whole)
                head_rstd()
                split_hi(g, k_hi[:, g, :], whole)
                act.wait_ge(vtr_done, g + 1)
                link(act.activation(v_hi[:, g, :, :].rearrange("p a b -> p (a b)"),
                                     aux[:, 2 * HALF:4 * HALF], ACT.Copy), vhi_ready)

            def columns(c):
                return slice(c * HALF, (c + 1) * HALF)

            def q_raw_half(h, c):
                u = BASE[2] + 4 + 2 * h
                if c == 0:
                    act.wait_ge(bg_done, 2 * h + 1)
                else:
                    act.wait_ge(unit_done, u + 1)
                raw(KV_HEADS + h, side_bank(h, c), columns(c), bg_free)
                if c == 1:
                    signal(pair_free[u % 2])

            def q_sums(h, c):
                act.wait_ge(qstat, KV_HEADS + 2 * h + c + 1)
                link(act.activation(rstd_b[:, columns(c)], side_bank(h, 2 + c), ACT.Copy))
                signal(bg_free)
                if c == 1:
                    head_ln(rstd_b[:, :], whole)
                    head_rstd()

            def q_hi_head(h):
                if h >= 2:
                    act.wait_ge(s_done, QT * (h - 1))
                split_hi(KV_HEADS + h, q_hi[:, h % 2, :], whole)

            def z_half(h, c):
                u = BASE[2] + 5 + 2 * h
                if c == 0:
                    act.wait_ge(bg_done, 2 * h + 2)
                    if h >= 2:
                        act.wait_ge(yq_done, 4 * (h - 1))
                else:
                    act.wait_ge(unit_done, u + 1)
                link(act.activation(sz_q[:, h % 2, columns(c)], side_bank(h, 4 + c), ACT.Copy))
                signal(bg_free)
                if c == 1:
                    signal(pair_free[u % 2])

            def gate_silu(h):
                link(act.activation(sz_q[:, h % 2, :], sz_q[:, h % 2, :], ACT.Silu), szq_ready)

            def exponentials(t):
                act.wait_ge(neg_ready, t + 1)
                if t >= 2:
                    act.wait_ge(t_done, t - 1)
                link(act.activation(prob[:, t % 2, :], aux[:, (t % 2) * S:(t % 2 + 1) * S], ACT.Exp,
                                     bias=stat_b[:, t % 2, 0:1], scale=SCORE_SCALE,
                                     accum_out=stat_b[:, t % 2, 1:2]), exp_done)

            def turned(t):
                act.wait_ge(t_done, t + 1)
                if t >= 2:
                    act.wait_ge(pv_done, t // 2)
                link(act.activation(pt_hi[:, :, (t % 2) * P:(t % 2 + 1) * P],
                                     pair[0][:, :].rearrange("p (k q) -> p k q", k=QT),
                                     ACT.Copy), pt_hi_ready)

            for c in range(2):
                q_raw_half(0, c)
            for c in range(2):
                q_sums(0, c)
            q_hi_head(0)
            for c in range(2):
                z_half(0, c)
            exponentials(0)
            for t in range(QT * HEADS):
                h, i = t // QT, t % QT
                beside = h + 1 < HEADS
                turned(t)
                if beside and i == 4:
                    q_sums(h + 1, 0)
                if t + 1 < QT * HEADS:
                    exponentials(t + 1)
                if i == 1:
                    gate_silu(h)
                if beside and i == 4:
                    q_sums(h + 1, 1)
                if beside and i == 5:
                    q_hi_head(h + 1)
                if beside and i in (1, 3):
                    q_raw_half(h + 1, i // 2)
                if beside and i in (5, 7):
                    z_half(h + 1, i // 2 - 2)
                if not beside and i >= 1:
                    y_hi("y2", i - 1, q_raw[:, (i - 1) % 2, :], op_hi)
            y_hi("y2", KT - 1, y_b[:, (KT - 1) % 2, :], op_hi)
            norm_squares(2, xc, sq_c, acc_c, KT)
            norm_rstd(3, aux[:, S:2 * S], rstd_g, eps2_col)
            act.wait_ge(unit_done, BASE[4])
            split_norm(2 * KT, op_hi)
            norm_rstd(4, aux[:, 0:S], rstd_c)
            act.wait_ge(r_stored, 16)

            act.wait_ge(op_ready, OP0["in"] + KT)
            act.wait_ge(x_stored, 32 * KT)
            act.wait_ge(pads_ready, 1)

            def conv_silu(t):
                act.wait_ge(conv_done, t + 1)
                link(act.activation(c_rows[:, t, :], conv_acc[:, t % 2, 0:S], ACT.Silu), c_ready)

            for t in range(KT):
                u = BASE[4] + t
                wait_job(act, u)
                link(act.activation(u_rows[:, t, 2:2 + S], pair[u % 2][:, :], ACT.Copy), u_ready)
                signal(pair_free[u % 2])
                if t >= 1:
                    conv_silu(t - 1)
            conv_silu(KT - 1)
            for g in range(4):
                for i in range(2):
                    n = 2 * g + i
                    u = BASE[4] + 8 + 4 * g + i
                    wait_job(act, u)
                    if n >= 1:
                        act.wait_ge(pooled_ready, n)
                    link(act.activation(pool_pad[:, PAD:PAD + S], pair[u % 2][:, :], ACT.Copy), px_ready)
                    signal(pair_free[u % 2])
                    if n == 2:
                        act.wait_ge(gate_done, 1)
                        act.wait_ge(consts_d, 80)
                        link(act.activation(gate_rows[:, :], aux[0:16, 2 * HALF:4 * HALF], ACT.Identity,
                                             bias=gb_sb[:, :]), gate_ready)
                for i in range(2):
                    n = 2 * g + i
                    u = BASE[4] + 10 + 4 * g + i
                    wait_job(act, u)
                    if n >= 1:
                        act.wait_ge(y_made, Y0["y3"] + n)
                    link(act.activation(sz_p[:, :], pair[u % 2][:, :], ACT.Silu), szp_ready)
                    signal(pair_free[u % 2])
            def reversed_row(row):
                return row[:, ::-1]

            def log_sigmoid():
                act.wait_ge(rows_in, 16 * 5)
                act.wait_ge(rows_clear, 3)
                link(act.activation(t_row[:, :], f_row[:, :], ACT.Abs))
                link(act.activation(t_row[:, :], t_row[:, :], ACT.Exp, scale=-1.0))
                link(act.activation(t_row[:, :], t_row[:, :], ACT.Ln, bias=ones[0:36, 0:1]), row_act)

            def gate_factors():
                d0, d1 = slice(0, MH), slice(32, 32 + MH)
                act.wait_ge(row_dve, 1)
                link(act.activation(b_row[d0, :], t_row[d0, :], ACT.Exp, scale=-1.0))
                link(act.activation(b_row[d1, :], reversed_row(t_row[d1, :]), ACT.Exp, scale=-1.0))
                link(act.activation(dec_row[d0, :], dec_tmp[d0, :], ACT.Exp))
                link(act.activation(dec_row[d1, :], reversed_row(dec_tmp[d1, :]), ACT.Exp))
                act.wait_ge(row_dve, 2)
                link(act.activation(t_row[d0, :], f_row[d0, :], ACT.Exp))
                link(act.activation(t_row[d1, :], reversed_row(f_row[d1, :]), ACT.Exp))
                act.wait_ge(row_dve, 3)
                link(act.activation(f_row[d0, :], i_row[d0, :], ACT.Exp))
                link(act.activation(f_row[d1, :], reversed_row(i_row[d1, :]), ACT.Exp), g_made)

            for t in range(KT):
                u = BASE[4] + 24 + t
                wait_job(act, u)
                if t < 2:
                    act.wait_ge(y_stored[t], stored("y3", KT - 2 + t))
                else:
                    act.wait_ge(mz_stored[t % 2], 16 * (t // 2))
                link(act.activation(y_d[:, t % 2, :], pair[u % 2][:, :], ACT.Silu), mz_ready)
                signal(pair_free[u % 2])
                if t == 0:
                    log_sigmoid()
                if t == ROWS_AT:
                    gate_factors()

            def take(h, n):
                act.wait_ge(prep_done, 8 * h + n + 1)
                if h >= 2 and n == 0:
                    act.wait_ge(ab_done, NDIR * CH * (h - 1))
                    act.wait_ge(upd_done, NDIR * (CH - 1) * (h - 1))
                    act.wait_ge(kw_ready, NDIR * (CH - 1) * (h - 1))
                src = aux[:, S:2 * S] if h == 0 and n % 2 else aux[:, 0:S]
                b = h % 2
                chunks = slice(4 * (n % 2), 4 * (n % 2) + 4)
                if n < 4:
                    dst = (q_t if n < 2 else kw_t)[:, b, n % 2, :]
                elif n < 6:
                    dst = k_tok[:, b, chunks, :].rearrange("p c d -> p (c d)")
                else:
                    act.wait_ge(ones_made, 1)
                    dst = v_tok[:, b, chunks, 0:MD]
                    src = src.rearrange("p (c d) -> p c d", c=4)
                link(act.activation(dst, src, ACT.Copy), prep_act)

            def decayed(h, q):
                d, c = q // CH, q % CH
                if q == 0:
                    act.wait_ge(gt_ready, 1)
                if c == 0:
                    act.wait_ge(bm_ready, NDIR * h + d + 1)
                r = MH * d + h
                cols = slice(c * P, (c + 1) * P)
                link(act.activation(bm_b[:, d, cols], bm_b[:, d, cols], ACT.Exp,
                                     bias=g_tok[:, c, r:r + 1]), e_ready)

            def head_factor(h):
                act.wait_ge(bn_ready, h + 1)
                if h >= 1:
                    act.wait_ge(ln_done, h)
                link(act.activation(rstd_h[:, :], bn2[:, :, 1], ACT.Ln, bias=eps_col[:, :]))
                link(act.activation(rstd_h[:, :], rstd_h[:, :], ACT.Exp, scale=-0.5), rh_ready)

            for n in range(8):
                take(0, n)
                for q in (2 * n, 2 * n + 1):
                    decayed(0, q)
            for h in range(MH):
                for m in range(NDIR * CH):
                    d = m % 2
                    g = NDIR * CH * h + m
                    act.wait_ge(ab_done, g + 1)
                    if g >= 2:
                        act.wait_ge(h_done, g - 1)
                    link(act.activation(num_a[:, d, :], pair[0][:, d * HALF:d * HALF + VE],
                                         ACT.Copy), acp_ready)
                    if h + 1 < MH and PREP_AT <= m < PREP_AT + 8:
                        take(h + 1, m - PREP_AT)
                    if h >= 1 and m == 1:
                        head_factor(h - 1)
                    if h + 1 < MH and 2 <= m < 10:
                        decayed(h + 1, 2 * (m - 2))
                        decayed(h + 1, 2 * (m - 2) + 1)
            link(act.activation(ln_ahead[:, :], eps_col[:, :], ACT.Ln, bias=eps_col[:, :]))
            head_factor(MH - 1)

            act.wait_ge(h_done, NDIR * CH * MH)
            act.wait_ge(upd_done, NDIR * (CH - 1) * MH)
            for k in range(2 * KT):
                y_hi("y3", k, xf[:, k % KT, :] if k < THROUGH["y3"] else out_e[:, k % 2, :], o_hi)
            norm_squares(3, xf, sq_f, acc_f, 2 * KT)
            norm_rstd(5, aux[:, 0:S], rstd_f)

        @block.vector
        def _(dve):
            link, signal = linker(dve, dve_step)

            def low_part(lo, full, hi, done):
                link(dve.tensor_tensor(lo, full, hi, ALU.subtract), done)

            def norm_apply(n, x, rstd, gain, hn0, op0):
                dve.wait_ge(rstd_ready, n + 1)
                for k in range(KT + 2):
                    if k < KT:
                        if k == 2:
                            dve.wait_ge(stat_done, (1, 2, 4)[n])
                        link(dve.scalar_tensor_tensor(out=stage_n[:, k % 4, :], in0=x[:, k, :],
                                               scalar=gain(k), in1=rstd[:, :], op0=ALU.mult,
                                               op1=ALU.mult), hn_ready)
                    if k % 2 and k >= 3:
                        dve.wait_ge(low_made, KT // 2 * n + (k - 1) // 2)
                        signal(op_ready)
                    if k % 2 and k < KT:
                        low(k - 1, stage_n[:, (k - 1) % 4, :], op0)

            def low(k, full, op0, hi=None, lo=None):
                dve.wait_ge(hi_ready, op0 + k + 1)
                low_part((op_lo if lo is None else lo)[:, k, :], full,
                         (op_hi if hi is None else hi)[:, k, :], op_ready)

            def accumulate(n, k, sq, acc, weighted=None):
                dve.wait_ge(sq_ready, KT * n + k + 1)
                if weighted is not None:
                    if k == 0:
                        link(dve.tensor_scalar(weighted[:, :], acc[:, :], gain2[:, 0:1], None, ALU.mult))
                    else:
                        link(dve.scalar_tensor_tensor(out=weighted[:, :], in0=sq[:, k % 2, :],
                                                      scalar=gain2[:, k:k + 1], in1=weighted[:, :],
                                                      op0=ALU.mult, op1=ALU.add))
                if k >= 1:
                    link(dve.tensor_tensor(acc[:, :], acc[:, :], sq[:, k % 2, :], ALU.add), acc_ready)

            def free(unit_no):
                signal(pair_free[job_of(unit_no) % 2])

            link(dve.memset(ones[:, :], 1.0), ready0)
            link(dve.memset(eps_col[:, :], EPS), ready0)
            link(dve.memset(eps2_col[:, :], EPS * EPS), ready0)
            link(dve.memset(u_pad[:, 0:1], 0.0))
            link(dve.memset(u_pad[:, S + 1:S + 2], 0.0))

            for k in range(KT - 1):
                accumulate(0, k, sq_a, acc_a)
            dve.wait_ge(consts, 32)
            final = par[:, PARAMS["final_norm"]:PARAMS["final_norm"] + KT]
            link(dve.tensor_tensor(gain2[:, :], final, final, ALU.mult))
            link(dve.tensor_scalar(gain2[:, :], gain2[:, :], EPS, None, ALU.add))
            link(dve.tensor_tensor(gain_both[:, :], final,
                                   par[:, PARAMS["norm_in"]:PARAMS["norm_in"] + KT], ALU.mult))
            norm_apply(0, xa, rstd_a, lambda k: col("norm_even", k), 0, 0)
            R2 = float(np.sqrt(0.5))
            for j in range(AB):
                dve.wait_ge(bu_ready, j + 1)
                link(dve.tensor_tensor(fold[:, 0:4, :], bu[:, 0:4, :], bu[:, 4:8, :], ALU.add))
                link(dve.tensor_tensor(fold[:, 4:8, :], bu[:, 0:4, :], bu[:, 4:8, :], ALU.subtract))
                if j >= 1:
                    dve.wait_ge(fft1_done, j)
                link(dve.tensor_tensor(bu[:, 0:2, :], fold[:, 0:2, :], fold[:, 2:4, :], ALU.add))
                link(dve.tensor_tensor(parts[:, 4:6, :], fold[:, 0:2, :], fold[:, 2:4, :], ALU.subtract))
                link(dve.tensor_tensor(bu[:, 2, :], fold[:, 5, :], fold[:, 7, :], ALU.subtract))
                link(dve.tensor_tensor(bu[:, 3, :], fold[:, 5, :], fold[:, 7, :], ALU.add))
                link(dve.tensor_tensor(parts[:, 0, :], bu[:, 0, :], bu[:, 1, :], ALU.add))
                link(dve.tensor_tensor(parts[:, 1, :], bu[:, 0, :], bu[:, 1, :], ALU.subtract))

                def combine(dst, a, scale, b, op, done=None):
                    link(dve.scalar_tensor_tensor(out=dst, in0=a, scalar=scale, in1=b, op0=ALU.mult, op1=op), done)

                combine(parts[:, 2, :], bu[:, 2, :], R2, fold[:, 4, :], ALU.add)
                combine(parts[:, 3, :], bu[:, 3, :], R2, fold[:, 6, :], ALU.add)
                combine(parts[:, 6, :], bu[:, 2, :], -R2, fold[:, 4, :], ALU.add)
                combine(parts[:, 7, :], bu[:, 3, :], R2, fold[:, 6, :], ALU.subtract, parts_ready)
                u = 6 * j + 2
                wait_job(dve, u)
                dve.wait_ge(ax_ready, j + 1)
                link(dve.tensor_tensor(u_pad[:, 1:S + 1], pair[u % 2][:, :], ax_sb[:, :], ALU.mult), prod_done)
                dve.wait_ge(prod_done, j + 1)
                free(u)
                link(dve.tensor_scalar(cv[:, :], u_pad[:, 0:S], col("conv_w", 3 * j), None, ALU.mult))
                for tap in (1, 2):
                    link(dve.scalar_tensor_tensor(out=cv[:, :], in0=u_pad[:, tap:tap + S],
                                                scalar=col("conv_w", 3 * j + tap), in1=cv[:, :],
                                                op0=ALU.mult, op1=ALU.add))
                dve.wait_ge(fft2_done, j + 1)
                dve.wait_ge(szb_ready, j + 1)
                if j >= 1:
                    dve.wait_ge(y_stored[0], stored("y1", 2 * j - 2))
                link(dve.tensor_tensor(y_a[:, 0, :].rearrange("p (k2 k1) -> p k1 k2", k1=RADIX),
                                aux[:, 0:S].rearrange("p (k1 k2) -> p k1 k2", k1=RADIX),
                                sz_b[:, :].rearrange("p (k2 k1) -> p k1 k2", k1=RADIX),
                                ALU.mult), y_made)
                u = 6 * j + 4
                wait_job(dve, u)
                link(dve.tensor_tensor(cv[:, :], pair[u % 2][:, :], cv[:, :], ALU.mult))
                free(u)
                dve.wait_ge(sza_ready, j + 1)
                link(dve.tensor_tensor(y_a[:, 1, :], cv[:, :], y_a[:, 1, :], ALU.mult), y_made)
            for k in range(KT):
                low(k, stage_y[:, k, :] if k < THROUGH["y1"] else y_a[:, k % 2, :], OP0["y1"])

            def add_residual(unit0, k, x):
                job = unit0 + k
                wait_job(dve, job)
                link(dve.tensor_tensor(x[:, k, :], pair[job % 2][:, :], x[:, k, :], ALU.add), x_done)
                signal(pair_free[job % 2])

            for k in range(KT):
                if k >= 1:
                    accumulate(1, k - 1, sq_a, acc_a)
                add_residual(BASE[1], k, xa)
            norm_apply(1, xa, rstd_a, lambda k: col("norm_odd", k), KT, OP0["odd"])

            dve.wait_ge(x_stored, 16 * KT)
            dve.wait_ge(op_ready, OP0["odd"] + KT)
            dve.wait_ge(rope_in, 16)

            def rotate(r, gain, cols):
                dve.wait_ge(raw_ready, r + 1)
                for n in range(2):
                    link(dve.scalar_tensor_tensor(out=q_raw[:, n, cols], in0=q_raw[:, n, cols],
                                                  scalar=col(gain, n), in1=rope_sb[:, n, cols],
                                                  op0=ALU.mult, op1=ALU.mult))
                link(dve.tensor_tensor(q_raw[:, 0, cols], q_raw[:, 0, cols], q_raw[:, 1, cols], ALU.add))

            def scale_head(n):
                dve.wait_ge(qrstd, n + 1)
                link(dve.tensor_tensor(q_raw[:, 0, :], q_raw[:, 0, :], rstd_b[:, :], ALU.mult), qr_ready)

            def split_lo(r, lo, hi, cols):
                dve.wait_ge(qhi_ready, r + 1)
                low_part(lo, q_raw[:, 0, cols], hi, q_ready)

            whole = slice(0, S)
            for g in range(KV_HEADS):
                rotate(g, "k_gain", whole)
                scale_head(g)
                split_lo(g, k_lo[:, g, :], k_hi[:, g, :], whole)
                dve.wait_ge(vhi_ready, g + 1)
                low_part(v_lo[:, g, :, :].rearrange("p a b -> p (a b)"), aux[:, 2 * HALF:4 * HALF],
                         v_hi[:, g, :, :].rearrange("p a b -> p (a b)"), v_ready)

            def q_rotate_half(h, c):
                rotate(KV_HEADS + 2 * h + c, "q_gain", slice(c * HALF, (c + 1) * HALF))

            def q_lo_head(h):
                split_lo(KV_HEADS + h, q_lo[:, h % 2, :], q_hi[:, h % 2, :], whole)

            def maxima(t):
                dve.wait_ge(s_done, t + 1)
                if t >= 2:
                    dve.wait_ge(exp_done, t - 1)
                link(dve.reduce_max(stat_b[:, t % 2, 2:3], aux[:, (t % 2) * S:(t % 2 + 1) * S], AX.X))
                link(dve.tensor_scalar(stat_b[:, t % 2, 0:1], stat_b[:, t % 2, 2:3], -SCORE_SCALE, None,
                                ALU.mult), neg_ready)

            def normalise(t):
                dve.wait_ge(exp_done, t + 1)
                link(dve.reciprocal(stat_b[:, t % 2, 3:4], stat_b[:, t % 2, 1:2]))
                link(dve.tensor_scalar(prob[:, t % 2, :], prob[:, t % 2, :], stat_b[:, t % 2, 3:4], None,
                                ALU.mult), p_ready)

            def turned_low(t):
                dve.wait_ge(pt_hi_ready, t + 1)
                cols = slice((t % 2) * P, (t % 2 + 1) * P)
                low_part(pt_lo[:, :, cols], pair[0][:, :].rearrange("p (k q) -> p k q", k=QT),
                         pt_hi[:, :, cols], pt_ready)

            def gate_values(n):
                h, m = n // 4, n % 4
                dve.wait_ge(pv_done, n + 1)
                if m == 0:
                    dve.wait_ge(szq_ready, h + 1)
                    if h >= 2:
                        dve.wait_ge(y_stored[h % 2], stored("y2", h - 2))
                cols = slice(m * 2 * P, (m + 1) * 2 * P)
                link(dve.tensor_tensor(y_b[:, h % 2, cols], pair[1][:, HALF:HALF + 2 * P],
                                sz_q[:, h % 2, cols], ALU.mult), yq_done)
                if m == 3:
                    signal(y_made)

            for c in range(2):
                q_rotate_half(0, c)
            scale_head(KV_HEADS)
            q_lo_head(0)
            maxima(0)
            maxima(1)
            normalise(0)
            for t in range(QT * HEADS):
                h, i = t // QT, t % QT
                beside = h + 1 < HEADS
                if beside and i == 5:
                    scale_head(KV_HEADS + h + 1)
                turned_low(t)
                if t + 1 < QT * HEADS:
                    normalise(t + 1)
                if t + 2 < QT * HEADS:
                    maxima(t + 2)
                if t >= 2 and t % 2 == 0:
                    gate_values(t // 2 - 1)
                if beside and i in (2, 4):
                    q_rotate_half(h + 1, i // 2 - 1)
                if beside and i == 5:
                    q_lo_head(h + 1)
                if not beside and i >= 1:
                    low(i - 1, q_raw[:, (i - 1) % 2, :], OP0["y2"])
            gate_values(4 * HEADS - 1)
            low(KT - 1, y_b[:, (KT - 1) % 2, :], OP0["y2"])
            dve.wait_ge(consts_d, 80)

            def block_diagonal(dst, blocks, mask, done=None):
                link(dve.tensor_tensor(dst.rearrange("p (m o) -> p m o", o=4),
                                       blocks.unsqueeze(1).broadcast_to([P, 32, 4]),
                                       mask[:, :].unsqueeze(2).broadcast_to([P, 32, 4]), ALU.mult), done)

            for i in range(3 * KT):
                block_diagonal(bdt[:, i, :], blocks_d[:, i % 3, i // 3, :], bmask_d, bdt_ready)
            for k in range(KT):
                dve.wait_ge(x_loaded[k], 32)
                if k >= 1:
                    accumulate(2, k - 1, sq_c, acc_c, acc_g)
                add_residual(BASE[3], k, xc)
                if k == 2:
                    dve.wait_ge(weff_done, 1)
                    link(dve.tensor_copy(gw_eff[:, :, :].rearrange("p a b -> p (a b)"),
                                         aux[:, 0:2 * KT * 16]), weff_ready)
            dve.wait_ge(sq_ready, 3 * KT)
            link(dve.tensor_scalar(last_g[:, :], sq_c[:, (KT - 1) % 2, :], gain2[:, KT - 1:KT], None,
                                   ALU.mult), last_g_made)
            norm_apply(2, xc, rstd_g, lambda k: gain_both[:, k:k + 1], 2 * KT, OP0["in"])

            dve.wait_ge(op_ready, OP0["in"] + KT)
            dve.wait_ge(x_stored, 32 * KT)
            for t in range(KT):
                link(dve.memset(u_rows[:, t, 0:2], 0.0))
                link(dve.memset(u_rows[:, t, 2 + S:4 + S], 0.0))
            link(dve.memset(pool_pad[:, 0:PAD], 0.0))
            link(dve.memset(pool_pad[:, PAD + S:2 * PAD + S], 0.0), pads_ready)
            for t in range(KT):
                dve.wait_ge(u_ready, t + 1)
                if t >= 2:
                    dve.wait_ge(c_ready, t - 1)
                acc = conv_acc[:, t % 2, 0:S]
                link(dve.tensor_scalar(acc, u_rows[:, t, 0:S], col("conv_w2", TAPS2 * t), col("conv_b2", t),
                                     ALU.mult, ALU.add))
                for tap in range(1, TAPS2):
                    link(dve.scalar_tensor_tensor(out=acc, in0=u_rows[:, t, tap:tap + S],
                                                 scalar=col("conv_w2", TAPS2 * t + tap), in1=acc,
                                                 op0=ALU.mult, op1=ALU.add))
                signal(conv_done)
            dve.wait_ge(c_ready, KT)
            for g, w in enumerate(WINDOWS):
                left = (w - 1) // 2
                right = w - 1 - left
                for i in range(2):
                    n = 2 * g + i
                    dve.wait_ge(px_ready, n + 1)
                    src, length, span, b = pool_pad[:, :], S + 2 * PAD, 1, 0
                    while span < w:
                        length -= span
                        dst = conv_acc[:, b, 0:length]
                        link(dve.tensor_tensor(dst, src[:, 0:length], src[:, span:span + length], ALU.add))
                        src, b, span = conv_acc[:, b, :], 1 - b, 2 * span
                    total = src[:, PAD - left:PAD - left + S]
                    if left:
                        link(dve.tensor_tensor(total[:, 0:left], total[:, 0:left], edge_sb[:, g, 0, 0:left], ALU.mult))
                    link(dve.tensor_tensor(total[:, S - right:S], total[:, S - right:S],
                                         edge_sb[:, g, 1, PAD - right:PAD], ALU.mult))
                    if g >= 1:
                        dve.wait_ge(mix_done, 2 * g)
                    link(dve.scalar_tensor_tensor(out=pooled[:, i, :], in0=total, scalar=1.0 / w,
                                           in1=pool_pad[:, PAD:PAD + S], op0=ALU.mult,
                                           op1=ALU.subtract), pooled_ready)
                for i in range(2):
                    n = 2 * g + i
                    dve.wait_ge(mix_done, n + 1)
                    dve.wait_ge(szp_ready, n + 1)
                    if n >= 2:
                        dve.wait_ge(y_stored[n % 2], stored("y3", n - 2))
                    link(dve.scalar_tensor_tensor(out=y_d[:, n % 2, :], in0=aux[:, 0:S], scalar=col("pool_scale", n),
                                           in1=sz_p[:, :], op0=ALU.mult, op1=ALU.mult), y_made)

            dve.wait_ge(gate_stored, 16)
            dve.wait_ge(mix_done, KT)
            link(dve.memset(i_row[:, :], 0.0), rows_clear)
            link(dve.memset(f_row[:, :], 0.0), rows_clear)
            link(dve.memset(mp_row[:, :], 0.0), rows_clear)
            d0, d1 = slice(0, MH), slice(32, 32 + MH)
            dve.wait_ge(row_act, 1)
            dve.wait_ge(rows_in, 16 * 5)
            link(dve.scalar_tensor_tensor(out=f_row[:, :], in0=f_row[:, :], scalar=0.0, in1=t_row[:, :],
                                        op0=ALU.min, op1=ALU.subtract))
            link(dve.tensor_copy(b_row[d1, :], i_row[d1, ::-1]))
            link(dve.tensor_copy(a_row[d1, :], f_row[d1, ::-1]))
            link(dve.tensor_copy(i_row[d1, :], b_row[d1, :]))
            link(dve.tensor_copy(f_row[d1, :], a_row[d1, :]))
            link(dve.tensor_tensor_scan(b_row[:, :], reset_row[:, :], f_row[:, :], 0.0, ALU.mult, ALU.add))
            link(dve.tensor_tensor_scan(t_row[:, :], f_row[:, :], i_row[:, :], 0.0, ALU.add, ALU.max))
            link(dve.tensor_tensor(f_row[:, :], b_row[:, :], t_row[:, :], ALU.subtract))
            link(dve.tensor_tensor(i_row[:, :], i_row[:, :], b_row[:, :], ALU.subtract))
            link(dve.tensor_copy(mp_row[:, 1:CH], t_row[:, P - 1:S - P:P]))
            link(dve.tensor_copy(end_row[:, :], f_row[:, P - 1:S:P]))
            link(dve.tensor_tensor(dec_tmp[:, :], end_row[:, :], mp_row[:, :], ALU.add))
            link(dve.tensor_copy(reset_row[d0, :], f_row[d0, :]))
            link(dve.tensor_copy(reset_row[d1, :], f_row[d1, ::-1]))
            link(dve.tensor_copy(a_row[d0, :], i_row[d0, :]))
            link(dve.tensor_copy(a_row[d1, :], i_row[d1, ::-1]))
            signal(bm_made)
            signal(row_dve)

            def by_chunk(row):
                return row[:, :].rearrange("p (c s) -> p c s", c=CH)

            link(dve.tensor_tensor(by_chunk(f_row), by_chunk(f_row),
                                 mp_row[:, :].unsqueeze(2).broadcast_to([36, CH, P]), ALU.add))
            signal(row_dve)
            link(dve.tensor_tensor(by_chunk(i_row), by_chunk(i_row),
                                 end_row[:, :].unsqueeze(2).broadcast_to([36, CH, P]), ALU.add))
            signal(row_dve)
            dve.wait_ge(consts_e, 48)
            for i in range(3 * KT):
                block_diagonal(bd[:, i // KT, i % KT, :], blocks_e[:, i // KT, i % KT, :], bmask_e)
            ks = bd[:, 1, :, :].rearrange("p a b -> p (a b)")
            link(dve.tensor_scalar(ks, ks, float(MD) ** -0.5, None, ALU.mult), bd_ready)
            dve.wait_ge(gt_done, 1)
            link(dve.tensor_copy(g_tok[:, :, :].rearrange("p a b -> p (a b)"), aux[:, 0:CH * 32]), gt_ready)
            dve.wait_ge(mz_stored[0], 16 * KT // 2)
            dve.wait_ge(mz_stored[1], 16 * KT // 2)
            for b in range(2):
                link(dve.memset(v_tok[:, b, :, MD:VE], 1.0))
            signal(ones_made)
            dve.wait_ge(decay_in, 16)

            def weigh_scores(h, d):
                dve.wait_ge(st_done, h + 1)
                dve.wait_ge(e_ready, NDIR * CH * h + CH * (d + 1))
                link(dve.tensor_tensor(kw_t[:, h % 2, d, :], aux[:, 0:S], bm_b[:, d, :], ALU.mult), wt_made)

            def weigh_keys(h, m):
                n, d = m // 2, m % 2
                ks = NDIR * (CH - 1) * h + m
                c = n if d == 0 else CH - 1 - n
                if m == 0:
                    dve.wait_ge(prep_act, 8 * h + 8)
                if ks >= 2:
                    dve.wait_ge(upd_done, ks - 1)
                r = 16 + MH * d + h
                link(dve.tensor_scalar(k_w[:, d, :], k_tok[:, h % 2, c, :], g_tok[:, c, r:r + 1], None,
                                ALU.mult), kw_ready)

            def finish(h, m):
                n, d = m // 2, m % 2
                g = NDIR * CH * h + m
                ks = NDIR * (CH - 1) * h + m
                c = n if d == 0 else CH - 1 - n
                r = MH * d + h
                if n < CH - 1:
                    dve.wait_ge(upd_done, ks + 1)
                    upd = aux[:, 2 * HALF:4 * HALF].rearrange("p (i e) -> p i e", i=2)[:, :, 0:VE]
                    if n == 0:
                        link(dve.tensor_copy(state[:, d, :, :], upd), state_ready)
                    else:
                        link(dve.scalar_tensor_tensor(out=state[:, d, :, :], in0=state[:, d, :, :],
                                               scalar=decay_b[:, r, c:c + 1], in1=upd,
                                               op0=ALU.mult, op1=ALU.add), state_ready)
                dve.wait_ge(acp_ready, g + 1)
                num = num_a[:, d, :]
                if n >= 1:
                    dve.wait_ge(ab_done, g + 1)
                    link(dve.scalar_tensor_tensor(out=num, in0=pair[1][:, d * HALF:d * HALF + VE],
                                                scalar=g_tok[:, c, 8 + r:9 + r], in1=num,
                                                op0=ALU.mult, op1=ALU.add))
                link(dve.tensor_scalar(small[:, d, 2:3], num[:, MD:VE], -1.0, g_tok[:, c, 24 + r:25 + r],
                                     ALU.mult, ALU.max))
                link(dve.tensor_tensor(small[:, d, 0:1], small[:, d, 2:3], num[:, MD:VE], ALU.max))
                link(dve.reciprocal(small[:, d, 1:2], small[:, d, 0:1]))
                if n < CH // 2:
                    link(dve.tensor_scalar(h_tok[h][:, c, :], num[:, 0:MD], small[:, d, 1:2], None,
                                    ALU.mult), h_done)
                else:
                    link(dve.scalar_tensor_tensor(out=h_tok[h][:, c, :], in0=num[:, 0:MD],
                                           scalar=small[:, d, 1:2], in1=h_tok[h][:, c, :],
                                           op0=ALU.mult, op1=ALU.add), h_done)
                    link(dve.bn_stats(bn6[:, c, :], h_tok[h][:, c, :]))

            def norm_sums():
                for c in range(CH):
                    link(dve.bn_aggr(bn2[:, c, :], bn6[:, c, :]))
                signal(bn_ready)

            def norm_step(h, c):
                if c == 0:
                    dve.wait_ge(rh_ready, h + 1)
                link(dve.tensor_scalar(h_tok[h][:, c, :], h_tok[h][:, c, :], bn2[:, c, 0:1],
                                      rstd_h[:, c:c + 1], ALU.subtract, ALU.mult))
                if c == CH - 1 or h == MH - 1:
                    signal(ln_done)

            def out_skip(h, i):
                n = 2 * h + i
                if h >= 1:
                    dve.wait_ge(y_stored[i], stored("y3", KT + 2 * h - 2 + i))
                link(dve.tensor_scalar(out_e[:, i, :], c_rows[:, n, :], col("skip", n), None, ALU.mult))

            def out_gain(h, i, src):
                n = 2 * h + i
                dve.wait_ge(ht_done, n + 1)
                link(dve.scalar_tensor_tensor(out=out_e[:, i, :], in0=src, scalar=col("mh_norm", n),
                                            in1=out_e[:, i, :], op0=ALU.mult, op1=ALU.add), ht_read)

            def out_gate(h, i):
                dve.wait_ge(mz_in[i], 16 * (h + 1))
                link(dve.tensor_tensor(out_e[:, i, :], out_e[:, i, :], mz_sb[:, i, :], ALU.mult), y_made)

            for d in range(NDIR):
                weigh_scores(0, d)
            for m in range(2):
                weigh_keys(0, m)
            for h in range(MH):
                for m in range(NDIR * CH):
                    if 1 <= m < NDIR * (CH - 1) - 1:
                        weigh_keys(h, m + 1)
                    elif m >= NDIR * (CH - 1) and h + 1 < MH:
                        weigh_keys(h + 1, m - NDIR * (CH - 1))
                    finish(h, m)
                    if h >= 1 and m == 0:
                        norm_sums()
                    if h + 1 < MH and 0 <= m - WEIGHTS_AT < NDIR:
                        weigh_scores(h + 1, m - WEIGHTS_AT)
                    if h >= 1 and LN_AT <= m < LN_AT + CH:
                        norm_step(h - 1, m - LN_AT)
                    if h >= 1:
                        for i in range(2):
                            if m == TURN_AT[i] - 2:
                                out_skip(h - 1, i)
                            if m == TURN_AT[i]:
                                out_gain(h - 1, i, aux[:, 0:S])
                            if m == TURN_AT[i] + 1:
                                out_gate(h - 1, i)
            norm_sums()
            def y_low(k):
                low(k, xf[:, k % KT, :] if k < THROUGH["y3"] else out_e[:, k % 2, :], OP0["y3"], o_hi, o_lo)

            for c in range(CH):
                norm_step(MH - 1, c)
            for i in range(2):
                out_skip(MH - 1, i)
            y_low(0)
            for k in (1, 2):
                y_low(k)
            for i in range(2):
                out_gain(MH - 1, i, aux[:, i * S:(i + 1) * S])
            for k in range(3, 6):
                y_low(k)
            for i in range(2):
                out_gate(MH - 1, i)
            for k in range(6, 2 * KT):
                y_low(k)
            dve.wait_ge(r_loaded, 16)
            for k in range(KT):
                dve.wait_ge(x_loaded[k], 48)
                link(dve.scalar_tensor_tensor(out=xf[:, k, :], in0=xf[:, k, :], scalar=col("final_norm", k),
                                       in1=rstd_f[:, :], op0=ALU.mult, op1=ALU.mult))
            for k in range(KT):
                if k >= 1:
                    accumulate(3, k - 1, sq_f, acc_f)
                add_residual(BASE[5], k, xf)
            dve.wait_ge(rstd_ready, 5)
            for k in range(KT):
                link(dve.scalar_tensor_tensor(out=xf[:, k, :], in0=xf[:, k, :], scalar=col("norm_out", k),
                                       in1=rstd_f[:, :], op0=ALU.mult, op1=ALU.mult), out_made)


def _tables():
    f = np.float32
    n = np.arange(P)
    ang = 2 * np.pi * np.outer(n, n) / P
    scale = 1.0 / np.sqrt(S * P)
    c, s = np.cos(ang) * scale, np.sin(ang) * scale
    dft_d = np.stack([np.concatenate([c, s], 1), np.concatenate([-s, c], 1), np.concatenate([s, -c], 1)], 1)
    k = np.arange(S).reshape(P, RADIX).T
    phase = 2 * np.pi * (n[:, None, None] * k[None]) / S
    dft_s = np.stack([np.cos(phase), -np.sin(phase)], 1)
    pairs = P // 4
    inv = (f(10000.0) ** (-np.arange(pairs, dtype=f) / f(pairs))).astype(f)
    t = np.arange(S)
    row, colm = (t // 64).astype(f), (t % 64).astype(f)
    a = np.concatenate([row[None] * inv[:, None], colm[None] * inv[:, None]], 0).astype(f).astype(np.float64)
    cs, sn = np.cos(a), np.sin(a)
    rope = np.stack([np.concatenate([cs, cs]), np.concatenate([-sn, sn])], 1)
    edge = np.ones((4, 2, PAD))
    for g, w in enumerate(WINDOWS):
        left = (w - 1) // 2
        right = w - 1 - left
        for t_ in range(left):
            edge[g, 0, t_] = w / (t_ + right + 1)
        for j in range(right):
            edge[g, 1, PAD - right + j] = w / (left + 1 + right - 1 - j)
    i = np.arange(P)
    masks = np.stack([np.where(i[:, None] <= i[None], 0.0, NEG), np.where(i[:, None] >= i[None], 0.0, NEG)], 1)
    block_mask = (i[:, None] // 4 == np.arange(32)[None]).astype(f)
    reset = np.ones((36, S))
    reset[:, ::P] = 0.0
    return {"ident_in": np.eye(P), "dft_d": dft_d, "dft_s": dft_s, "rope": rope,
            "edge": np.broadcast_to(edge, (P, 4, 2, PAD)), "masks": masks, "block_mask": block_mask,
            "reset_mask": reset}


def _units(w, blocks):
    out = []
    for b in blocks:
        cols, k0 = b if isinstance(b, tuple) else (b, 0)
        part = w[k0 * P:(k0 + KT) * P][:, cols]
        out.append(part.reshape(KT, P, P).transpose(1, 0, 2).reshape(P, KT * P))
    return out


def kernel(**inputs):
    import concourse.bacc as _bacc
    from concourse.bass_utils import run_bass_kernel_spmd as _run

    a = {k: np.asarray(v) for k, v in inputs.items()}

    def cols(b):
        return np.arange(b * P, (b + 1) * P)

    pair_order = np.concatenate([np.arange(0, P, 2), np.arange(1, P, 2)])
    units = []
    for j in range(AB):
        units += _units(a["w_in_even"][0], [cols(b) for b in (16 + j, j, 8 + j, 20 + j, 4 + j, 12 + j)])
    made = np.concatenate([cols(b) for j in range(AB) for b in (AB + j, j)])
    units += _units(a["w_out_even"][0][made], [cols(e) for e in range(KT)])
    w = a["w_in_odd"][0]
    for g in range(KV_HEADS):
        units += _units(w, [cols(HEADS + g)[pair_order], cols(HEADS + KV_HEADS + g)])
    for h in range(HEADS):
        units += _units(w, [cols(h)[pair_order], cols(HEADS + 2 * KV_HEADS + h)])
    units += _units(a["w_out_odd"][0], [cols(e) for e in range(KT)])
    w = a["w_in_2"][0]
    units += _units(w, [cols(16 + t) for t in range(KT)])
    for g in range(4):
        units += _units(w, [cols(b) for b in (2 * g, 2 * g + 1, 8 + 2 * g, 9 + 2 * g)])
    units += _units(w, [cols(24 + t) for t in range(KT)])
    units += _units(a["w_out_2"][0], [(cols(e), KT * i) for e in range(KT) for i in range(2)])

    def by_block(v):
        return v.reshape(-1, P).T

    def taps(v):
        return v.reshape(v.shape[0], -1, P).transpose(2, 1, 0).reshape(P, -1)

    params = {"norm_even": by_block(a["norm_even"][0]), "conv_w": taps(a["conv_w"][0]),
              "norm_odd": by_block(a["norm_odd"][0]), "final_norm": by_block(a["final_norm"]),
              "norm_in": by_block(a["norm_in_g_2"][0]), "norm_out": by_block(a["norm_out_g_2"]),
              "q_gain": np.stack([a["q_gain"][0][pair_order], a["q_gain"][0][np.roll(pair_order, P // 2)]], 1),
              "k_gain": np.stack([a["k_gain"][0][pair_order], a["k_gain"][0][np.roll(pair_order, P // 2)]], 1),
              "pool_scale": by_block(a["pool_scale_2"][0]), "conv_w2": taps(a["conv_w_2"][0]),
              "conv_b2": by_block(a["conv_b_2"][0]), "mh_norm": by_block(a["mh_norm_w_2"][0]),
              "skip": by_block(a["skip_w_2"][0])}
    qkv = np.stack([a[k][0] for k in ("w_q_2", "w_k_2", "w_v_2")]).reshape(3, KT, 32, 4, 4)
    straight = qkv.reshape(3, KT, P, 4).transpose(2, 0, 1, 3)
    turned = qkv.transpose(0, 1, 2, 4, 3).reshape(3, KT, P, 4).transpose(2, 0, 1, 3)
    gw = a["w_gates_2"][0].reshape(NDIR, 3 * KT, P, 2, MH).transpose(2, 1, 3, 0, 4).reshape(P, 3 * KT, 16)
    gb = a["b_gates_2"][0].reshape(NDIR, 2, MH).transpose(1, 0, 2).reshape(16, 1)
    arrays = {"x_t": a["x"][0].T.reshape(KT, P, S), "weight_units": np.stack(units),
              "channel_params": np.concatenate([params[k] for k in PARAMS], 1),
              "qkv_blocks": np.stack([straight, turned]), "gate_w": gw, "gate_b": gb,
              "pool_w": a["pool_w_2"][0].reshape(4, 2, P, MD).transpose(0, 2, 1, 3)}
    arrays.update({k: v.astype(np.float32) for k, v in _tables().items()})
    arrays = {k: np.ascontiguousarray(v) for k, v in arrays.items()}

    nc = _bacc.Bacc("TRN2", target_bir_lowering=False, num_devices=1)
    args = {k: nc.dram_tensor(k, v.shape, mybir.dt.from_np(v.dtype), kind="ExternalInput").ap()
            for k, v in arrays.items()}
    out = nc.dram_tensor("out", [KT, P, S], F32, kind="ExternalOutput").ap()
    build(nc, out=out, **args)
    r = _run(nc, [arrays], core_ids=[0])
    return r.results[0]["out"].reshape(D, S).T.reshape(1, S, D)
```
